# Optimizing a Trainium2 kernel written in Bass

```python
import jax, jax.numpy as jnp
from jax import lax
import numpy as np

D_MODEL = 1024
BATCH = 1
SEQ = 1024
DEPTH = 1
DEC_BATCH = 8
DEC_SEQ = 4
PAST_LEN = 4096
PAGE_SIZE = 128

N_HEADS = 16
HEAD_DIM = D_MODEL // N_HEADS
N_KV_HEADS = 4
GQA_GROUP = N_HEADS // N_KV_HEADS
WINDOW = 128
ATTN_BLOCK = WINDOW
ROPE_THETA = 10000.0
NEG_INF = -1e30
LRU_WIDTH = D_MODEL
LRU_BLOCKS = 16
LRU_BLOCK_W = LRU_WIDTH // LRU_BLOCKS
CONV_WIDTH = 4
LRU_C = 8.0
N_GROUPS = 4
EXPERTS_PER_GROUP = 8
N_EXPERTS = N_GROUPS * EXPERTS_PER_GROUP
TOP_K = 2
D_EXPERT = D_MODEL // 2
MOE_BLOCK = 128
NORM_EPS = 1e-6
Q_DIM = N_HEADS * HEAD_DIM
KV_DIM = N_KV_HEADS * HEAD_DIM
IN_DIM = Q_DIM + 2 * KV_DIM + 2 * LRU_WIDTH + 2 * D_MODEL

PARAM_NAMES = ('w_ada', 'b_ada', 'g_pre_mix', 'g_post_mix', 'g_pre_ffn', 'g_post_ffn', 'w_in', 'sinks',
               'w_conv', 'b_conv', 'w_lru_a', 'b_lru_a', 'w_lru_x', 'b_lru_x', 'lru_lambda',
               'w_attn_branch', 'w_lru_branch', 'w_out', 'w_router_group', 'b_router_group',
               'w_router_expert', 'b_router_expert', 'w_exp_gate', 'w_exp_up', 'w_exp_down')

kernel_name = 'hybrid_swa_rglru_hmoe_decode_step'

def _rms_norm(x, g):
    xf = x.astype(jnp.float32)
    y = xf * lax.rsqrt(jnp.mean(xf * xf, axis=-1, keepdims=True) + NORM_EPS)
    return (y * g.astype(jnp.float32)).astype(x.dtype)

def _rope(x, pos):
    half = HEAD_DIM // 2
    inv = jnp.power(jnp.float32(ROPE_THETA), -jnp.arange(half, dtype=jnp.float32) / half)
    ang = pos.astype(jnp.float32)[:, None] * inv[None, :]
    cos = jnp.cos(ang)[:, None, :]
    sin = jnp.sin(ang)[:, None, :]
    xf = x.astype(jnp.float32)
    x1, x2 = xf[..., :half], xf[..., half:]
    return jnp.concatenate([x1 * cos - x2 * sin, x2 * cos + x1 * sin], axis=-1).astype(x.dtype)

def _window_attention(q, k, v, q_pos, k_pos, sinks):
    s = jnp.einsum('...qhgd,...khd->...hgqk', q, k, preferred_element_type=jnp.float32) * (HEAD_DIM ** -0.5)
    d = q_pos[..., :, None] - k_pos[..., None, :]
    valid = (d >= 0) & (d <= WINDOW) & (k_pos[..., None, :] >= 0)
    s = jnp.where(valid[..., None, None, :, :], s, NEG_INF)
    sink = sinks.astype(jnp.float32).reshape(N_KV_HEADS, GQA_GROUP, 1, 1)
    m = jnp.maximum(jnp.max(s, axis=-1, keepdims=True), sink)
    p = jnp.exp(s - m)
    denom = jnp.sum(p, axis=-1, keepdims=True) + jnp.exp(sink - m)
    o = jnp.einsum('...hgqk,...khd->...qhgd', p / denom, v.astype(jnp.float32))
    return o.astype(q.dtype)

def _prompt_attention(q, k, v, sinks):
    B, S = q.shape[0], q.shape[1]
    nb = S // ATTN_BLOCK
    qb = q.reshape(B, nb, ATTN_BLOCK, N_KV_HEADS, GQA_GROUP, HEAD_DIM)
    kb = k.reshape(B, nb, ATTN_BLOCK, N_KV_HEADS, HEAD_DIM)
    vb = v.reshape(B, nb, ATTN_BLOCK, N_KV_HEADS, HEAD_DIM)

    def with_prev(t):
        prev = jnp.concatenate([jnp.zeros_like(t[:, :1]), t[:, :-1]], axis=1)
        return jnp.concatenate([prev, t], axis=2)

    pos = jnp.arange(S, dtype=jnp.int32).reshape(nb, ATTN_BLOCK)
    k_pos = jnp.concatenate([pos - ATTN_BLOCK, pos], axis=-1)
    o = _window_attention(qb, with_prev(kb), with_prev(vb), pos, k_pos, sinks)
    return o.reshape(B, S, Q_DIM)

def _sample_attention(q, k, v, k_cache, v_cache, sinks, q_pos):
    B, T = q.shape[0], q.shape[1]
    k_all = jnp.concatenate([k_cache.astype(k.dtype), k], axis=1)
    v_all = jnp.concatenate([v_cache.astype(v.dtype), v], axis=1)
    k_pos = (PAST_LEN - k_cache.shape[1]) + jnp.arange(k_all.shape[1], dtype=jnp.int32)
    qg = q.reshape(B, T, N_KV_HEADS, GQA_GROUP, HEAD_DIM)
    o = _window_attention(qg, k_all, v_all, q_pos, k_pos, sinks)
    return o.reshape(B, T, Q_DIM), k_all[:, -WINDOW:], v_all[:, -WINDOW:]

def _causal_conv(x, prev, w, b):
    T = x.shape[1]
    xp = jnp.concatenate([prev.astype(x.dtype), x], axis=1)
    y = sum(xp[:, j:j + T] * w[j] for j in range(CONV_WIDTH)) + b
    return y, xp[:, -(CONV_WIDTH - 1):]

def _rg_lru(x, h0, w_a, b_a, w_x, b_x, lam):
    B, T, _ = x.shape
    xf = x.astype(jnp.float32)
    xb = xf.reshape(B, T, LRU_BLOCKS, LRU_BLOCK_W)
    r = jax.nn.sigmoid(jnp.einsum('btni,nij->btnj', xb, w_a.astype(jnp.float32)).reshape(B, T, LRU_WIDTH)
                       + b_a.astype(jnp.float32))
    i = jax.nn.sigmoid(jnp.einsum('btni,nij->btnj', xb, w_x.astype(jnp.float32)).reshape(B, T, LRU_WIDTH)
                       + b_x.astype(jnp.float32))
    log_a = -LRU_C * r * jax.nn.softplus(-lam.astype(jnp.float32))
    a = jnp.exp(log_a)
    u = jnp.sqrt(-jnp.expm1(2.0 * log_a)) * (i * xf)
    u = u.at[:, 0].add(a[:, 0] * h0.astype(jnp.float32))

    def combine(left, right):
        return (left[0] * right[0], right[0] * left[1] + right[1])

    _, h = lax.associative_scan(combine, (a, u), axis=1)
    return h, h[:, -1]

def _hier_moe(h, w_rg, b_rg, w_re, b_re, w_gate, w_up, w_down):
    B, T, D = h.shape
    N = B * T
    hf = h.reshape(N, D)
    g_logits = (hf @ w_rg).astype(jnp.float32) + b_rg.astype(jnp.float32)
    p_group = jax.nn.softmax(g_logits, axis=-1)
    g_star = jnp.argmax(g_logits, axis=-1).astype(jnp.int32)
    e_logits = ((hf @ w_re).astype(jnp.float32) + b_re.astype(jnp.float32)).reshape(N, N_GROUPS, EXPERTS_PER_GROUP)
    in_group = jnp.take_along_axis(e_logits, g_star[:, None, None], axis=1)[:, 0]
    top_v, top_i = lax.top_k(in_group, TOP_K)
    gate_w = jax.nn.softmax(top_v, axis=-1) * jnp.take_along_axis(p_group, g_star[:, None], axis=1)
    e_idx = g_star[:, None] * EXPERTS_PER_GROUP + top_i.astype(jnp.int32)

    A = N * TOP_K
    flat_e = e_idx.reshape(-1)
    flat_w = gate_w.reshape(-1)
    order = jnp.argsort(flat_e)
    sorted_e = flat_e[order]
    tok = (order // TOP_K).astype(jnp.int32)
    counts = jnp.bincount(flat_e, length=N_EXPERTS).astype(jnp.int32)
    padded = (counts + MOE_BLOCK - 1) // MOE_BLOCK * MOE_BLOCK
    starts = jnp.cumsum(counts) - counts
    pends = jnp.cumsum(padded)
    pstarts = pends - padded
    dest = pstarts[sorted_e] + jnp.arange(A, dtype=jnp.int32) - starts[sorted_e]
    n_blocks = -(-A // MOE_BLOCK) + N_EXPERTS
    P = n_blocks * MOE_BLOCK
    slot_tok = jnp.full((P,), N, jnp.int32).at[dest].set(tok)
    slot_w = jnp.zeros((P,), jnp.float32).at[dest].set(flat_w[order])
    block_e = jnp.minimum(jnp.searchsorted(pends, jnp.arange(n_blocks, dtype=jnp.int32) * MOE_BLOCK, side='right'),
                          N_EXPERTS - 1).astype(jnp.int32)
    h_pad = jnp.concatenate([hf, jnp.zeros((1, D), hf.dtype)], axis=0)
    xb = h_pad[slot_tok].reshape(n_blocks, MOE_BLOCK, D)

    def expert_block(args):
        xblk, e = args
        g = xblk @ w_gate[e]
        u = xblk @ w_up[e]
        return (jax.nn.silu(g) * u) @ w_down[e]

    yb = lax.map(expert_block, (xb, block_e)).reshape(P, D)
    y = jnp.zeros((N + 1, D), jnp.float32).at[slot_tok].add(yb.astype(jnp.float32) * slot_w[:, None])[:N]
    return y.astype(h.dtype).reshape(B, T, D)

def _layer(x, c, k_prev, v_prev, conv_prev, h_prev, p, sample):
    B, T, _ = x.shape
    mod = jax.nn.silu(c) @ p['w_ada'] + p['b_ada']
    sh_a, sc_a, gt_a, sh_f, sc_f, gt_f = [m[:, None, :] for m in jnp.split(mod, 6, axis=-1)]

    h = _rms_norm(x, p['g_pre_mix']) * (1.0 + sc_a) + sh_a
    proj = h @ p['w_in']
    o1 = Q_DIM
    o2 = o1 + KV_DIM
    o3 = o2 + KV_DIM
    o4 = o3 + LRU_WIDTH
    o5 = o4 + LRU_WIDTH
    o6 = o5 + D_MODEL
    q, k, v, xl, yl, ga, gr = jnp.split(proj, [o1, o2, o3, o4, o5, o6], axis=-1)

    start = PAST_LEN if sample else 0
    pos = start + jnp.arange(T, dtype=jnp.int32)
    q = _rope(q.reshape(B, T, N_HEADS, HEAD_DIM), pos)
    k = _rope(k.reshape(B, T, N_KV_HEADS, HEAD_DIM), pos)
    v = v.reshape(B, T, N_KV_HEADS, HEAD_DIM)
    if sample:
        o_attn, k_new, v_new = _sample_attention(q, k, v, k_prev, v_prev, p['sinks'], pos)
    else:
        o_attn = _prompt_attention(q, k, v, p['sinks'])
        k_new, v_new = k[:, -WINDOW:], v[:, -WINDOW:]

    xc, conv_new = _causal_conv(xl, conv_prev, p['w_conv'], p['b_conv'])
    hl, h_new = _rg_lru(xc, h_prev, p['w_lru_a'], p['b_lru_a'], p['w_lru_x'], p['b_lru_x'], p['lru_lambda'])
    o_lru = (hl * jax.nn.gelu(yl.astype(jnp.float32))).astype(x.dtype)

    b_attn = o_attn @ p['w_attn_branch']
    b_lru = o_lru @ p['w_lru_branch']
    merged = jax.nn.sigmoid(ga) * b_attn + jax.nn.sigmoid(gr) * b_lru
    mix = merged @ p['w_out']
    x = x + gt_a * _rms_norm(mix, p['g_post_mix'])

    h2 = _rms_norm(x, p['g_pre_ffn']) * (1.0 + sc_f) + sh_f
    f = _hier_moe(h2, p['w_router_group'], p['b_router_group'], p['w_router_expert'], p['b_router_expert'],
                  p['w_exp_gate'], p['w_exp_up'], p['w_exp_down'])
    x = x + gt_f * _rms_norm(f, p['g_post_ffn'])
    return x, k_new, v_new, conv_new, h_new.astype(x.dtype)

def setup_inputs(seed: int = 0) -> dict:
    key = jax.random.key(seed)
    ks = jax.random.split(key, 40)
    f32 = jnp.float32

    def nrm(k, shape, scale):
        return jax.random.normal(k, shape, f32) * scale

    L = DEPTH
    D = D_MODEL
    a8 = jax.random.uniform(ks[20], (L, LRU_WIDTH), f32, minval=0.9, maxval=0.999)
    a = a8 ** (1.0 / LRU_C)
    lam = jnp.log(a) - jnp.log1p(-a)
    return {
        'x_prompt': nrm(ks[0], (BATCH, SEQ, D), 1.0),
        'x_sample': nrm(ks[1], (DEC_BATCH, DEC_SEQ, D), 1.0),
        'cache_k_win': nrm(ks[2], (L, DEC_BATCH, WINDOW, N_KV_HEADS, HEAD_DIM), 1.0),
        'cache_v_win': nrm(ks[3], (L, DEC_BATCH, WINDOW, N_KV_HEADS, HEAD_DIM), 1.0),
        'state_conv': nrm(ks[4], (L, DEC_BATCH, CONV_WIDTH - 1, LRU_WIDTH), 1.0),
        'state_h': nrm(ks[5], (L, DEC_BATCH, LRU_WIDTH), 0.5),
        'c_prompt': nrm(ks[6], (BATCH, D), 1.0),
        'c_sample': nrm(ks[7], (DEC_BATCH, D), 1.0),
        'w_ada': nrm(ks[8], (L, D, 6 * D), 0.5 * D ** -0.5),
        'b_ada': nrm(ks[9], (L, 6 * D), 0.01),
        'g_pre_mix': 1.0 + nrm(ks[10], (L, D), 0.1),
        'g_post_mix': 1.0 + nrm(ks[11], (L, D), 0.1),
        'g_pre_ffn': 1.0 + nrm(ks[12], (L, D), 0.1),
        'g_post_ffn': 1.0 + nrm(ks[13], (L, D), 0.1),
        'w_in': nrm(ks[14], (L, D, IN_DIM), D ** -0.5),
        'sinks': nrm(ks[15], (L, N_HEADS), 1.0),
        'w_conv': nrm(ks[16], (L, CONV_WIDTH, LRU_WIDTH), CONV_WIDTH ** -0.5),
        'b_conv': nrm(ks[17], (L, LRU_WIDTH), 0.01),
        'w_lru_a': nrm(ks[18], (L, LRU_BLOCKS, LRU_BLOCK_W, LRU_BLOCK_W), LRU_BLOCK_W ** -0.5),
        'b_lru_a': nrm(ks[19], (L, LRU_WIDTH), 0.01),
        'w_lru_x': nrm(ks[21], (L, LRU_BLOCKS, LRU_BLOCK_W, LRU_BLOCK_W), LRU_BLOCK_W ** -0.5),
        'b_lru_x': nrm(ks[22], (L, LRU_WIDTH), 0.01),
        'lru_lambda': lam,
        'w_attn_branch': nrm(ks[23], (L, Q_DIM, D), Q_DIM ** -0.5),
        'w_lru_branch': nrm(ks[24], (L, LRU_WIDTH, D), LRU_WIDTH ** -0.5),
        'w_out': nrm(ks[25], (L, D, D), D ** -0.5),
        'w_router_group': nrm(ks[26], (L, D, N_GROUPS), D ** -0.5),
        'b_router_group': nrm(ks[27], (L, N_GROUPS), 0.01),
        'w_router_expert': nrm(ks[28], (L, D, N_EXPERTS), D ** -0.5),
        'b_router_expert': nrm(ks[29], (L, N_EXPERTS), 0.01),
        'w_exp_gate': nrm(ks[30], (L, N_EXPERTS, D, D_EXPERT), D ** -0.5),
        'w_exp_up': nrm(ks[31], (L, N_EXPERTS, D, D_EXPERT), D ** -0.5),
        'w_exp_down': nrm(ks[32], (L, N_EXPERTS, D_EXPERT, D), D_EXPERT ** -0.5),
    }

def reference(x_prompt, x_sample, cache_k_win, cache_v_win, state_conv, state_h, c_prompt, c_sample,
              w_ada, b_ada, g_pre_mix, g_post_mix, g_pre_ffn, g_post_ffn, w_in, sinks,
              w_conv, b_conv, w_lru_a, b_lru_a, w_lru_x, b_lru_x, lru_lambda,
              w_attn_branch, w_lru_branch, w_out, w_router_group, b_router_group,
              w_router_expert, b_router_expert, w_exp_gate, w_exp_up, w_exp_down):
    weights = (w_ada, b_ada, g_pre_mix, g_post_mix, g_pre_ffn, g_post_ffn, w_in, sinks,
               w_conv, b_conv, w_lru_a, b_lru_a, w_lru_x, b_lru_x, lru_lambda,
               w_attn_branch, w_lru_branch, w_out, w_router_group, b_router_group,
               w_router_expert, b_router_expert, w_exp_gate, w_exp_up, w_exp_down)
    y_p, y_s = x_prompt, x_sample
    kp, vp, cp, hp, ks_, vs_, cs_, hs_ = [], [], [], [], [], [], [], []
    for layer in range(DEPTH):
        p = {name: w[layer] for name, w in zip(PARAM_NAMES, weights)}
        zero_conv = jnp.zeros((x_prompt.shape[0], CONV_WIDTH - 1, LRU_WIDTH), x_prompt.dtype)
        zero_h = jnp.zeros((x_prompt.shape[0], LRU_WIDTH), jnp.float32)
        y_p, k1, v1, c1, h1 = _layer(y_p, c_prompt, None, None, zero_conv, zero_h, p, False)
        y_s, k2, v2, c2, h2 = _layer(y_s, c_sample, cache_k_win[layer], cache_v_win[layer],
                                     state_conv[layer], state_h[layer], p, True)
        kp.append(k1); vp.append(v1); cp.append(c1); hp.append(h1)
        ks_.append(k2); vs_.append(v2); cs_.append(c2); hs_.append(h2)
    return (y_p, y_s, jnp.stack(kp), jnp.stack(vp), jnp.stack(cp), jnp.stack(hp),
            jnp.stack(ks_), jnp.stack(vs_), jnp.stack(cs_), jnp.stack(hs_))


_drawn_inputs = setup_inputs


def setup_inputs(seed=0):
    import zlib

    import numpy as np

    out = dict(_drawn_inputs(seed))
    spreads = {}
    factors = {'sinks': 5.737,
     'b_lru_a': 22.855,
     'b_lru_x': 5.585,
     'b_router_expert': 2.701,
     'b_router_group': 2.946}
    for name, (base, spread) in spreads.items():
        noise = np.random.default_rng([zlib.crc32(name.encode()), seed]).standard_normal(out[name].shape)
        drawn = base * np.exp(spread * noise) if base else spread * noise
        out[name] = __import__('jax').numpy.asarray(drawn.astype(out[name].dtype))
    for name, factor in factors.items():
        out[name] = (out[name] * factor).astype(out[name].dtype)
    return out
```

```python
from contextlib import ExitStack

import numpy as np

import concourse.bass as bass
from concourse import mybir
from concourse.alu_op_type import AluOpType as ALU

F32 = mybir.dt.float32
BF16 = mybir.dt.bfloat16
I32 = mybir.dt.int32
U32 = mybir.dt.uint32
ACT = mybir.ActivationFunctionType
AX_X = mybir.AxisListType.X

P = 128
D = 1024
SEQ = 1024
NB, NT = 8, 4
NS = NB * NT
PAST = 4096
TOK = SEQ + NS
KC = D // P
HD = 64
KV = 256
GRP = 3
GW = TOK // GRP
BLKS = SEQ // P
TILES = BLKS + 1
SCALE = 0.125
EPS = 1e-6
NE, NG, EPG = 32, 4, 8
FE = 512
FC = FE // P
A_MAX = 2 * TOK
MAXB = (A_MAX + NE * (P - 1)) // P
MAXB += MAXB % 2
MINB = A_MAX // P
NADA = 6 * D // 512
N_QK = 30
N_PROJ = N_QK + 12 * KC
GELU_C = 0.7978845608028654
GELU_A = 0.044715
XPAD = 3


class Chain:

    def __init__(self, eng, sem):
        self.eng, self.sem, self.base, self.n = eng, sem, 0, 0

    def __call__(self, ins):
        self.n += 1
        ins.then_inc(self.sem, 1)
        self.eng.wait_ge(self.sem, self.base + self.n)

    def enter(self, i, per):
        self.kept, self.per, self.start = self.n, per, self.base
        self.base, self.n = self.base + self.kept + i * per, 0

    def leave(self, trips):
        assert self.n == self.per, (self.n, self.per)
        self.base, self.n = self.start, self.kept + trips * self.per


def build(nc, I, O):
    ctx = ExitStack()
    with ctx:
        base0 = (nc.sbuf_base + 63) // 64 * 64
        room = (nc.sbuf_usable_end - base0) // 4

        def at(name, shape, word, dt=F32):
            words = int(np.prod(shape[1:])) * (2 if dt == BF16 else 4) // 4
            assert word + words <= room, (name, word, words, room)
            return nc.alloc_sbuf_tensor_at(name, list(shape), dt, offset=base0 + 4 * word)

        big = KC * TOK
        hT = at("hT", [P, KC, TOK], 0)
        oT = at("oT", [P, KC, TOK], big)
        olT = at("olT", [P, KC, TOK], 2 * big)

        cur = 3 * big

        def small(name, shape, dt=F32):
            nonlocal cur
            t = at(name, shape, cur, dt)
            cur += (int(np.prod(shape[1:])) * (2 if dt == BF16 else 4) + 31) // 32 * 8
            return t

        ident = small("ident", [P, P])
        identb = small("identb", [P, P], BF16)
        rot = small("rot", [P, P])
        mask_s = small("mask_s", [P, P + NT], BF16)
        sel = small("sel", [1 + NB, P + NS])
        halves = small("halves", [P, 2])
        nsink = small("nsink", [P, 2 * KC])
        nsink_s = small("nsink_s", [P, 1])
        lvec = small("lvec", [P, KC, 8])
        lcur = small("lcur", [P, 8])
        h0 = small("h0", [P, KC, NB])
        stc = small("stc", [P, KC, NB, XPAD])
        tail = small("tail", [P, KC, 36])
        eps = small("eps", [P, 1])
        mx = small("mx", [P, 2, 2])
        ngm = small("ngm", [P, 2, 2])
        skd = small("skd", [P, 2, 2])
        sme = small("sme", [P, 2, 2])
        ske = small("ske", [P, 2, 2])
        rcp = small("rcp", [P, 2, 2])
        spt = small("spt", [P, 5, KC])
        sst = small("sst", [P, 2, 4])
        mod = at("mod", [1 + NB, 4 * D], cur)
        cur += 4 * D
        zone_k = cur
        kT = at("kT", [P, 2, P + TOK], zone_k)
        vtok = at("vtok", [P, TILES + 1, KV], zone_k + 2 * (P + TOK))
        wA = at("wA", [P, KC, P], zone_k + 2 * (P + TOK) + (TILES + 1) * KV)
        w0 = zone_k + 2 * (P + TOK) + (TILES + 1) * KV + KC * P
        wB = at("wB", [P, KC, P], w0)
        wlg = at("wlg", [P, 2, P], w0 + KC * P)
        tmp0 = w0 + KC * P + 2 * P
        merged = at("merged", [P, KC, TOK], zone_k)
        after_merged = zone_k + big
        assert after_merged <= room

        wada = [at(f"wada{i}", [P, KC, 512], w) for i, w in
                enumerate((big, big + 4096, 2 * big, 2 * big + 4096))]
        cT = at("cT", [P, KC, 1 + NB], tmp0)
        cE = at("cE", [P, KC, 1 + NB], tmp0 + 80)
        gpre = at("gpre", [P, KC], tmp0 + 160)
        shT = at("shT", [P, KC, 1 + NB], tmp0 + 176)
        scT = at("scT", [P, KC, 1 + NB], tmp0 + 256)
        modh = at("modh", [1 + NB, 2 * D], tmp0 + 336)
        bada = at("bada", [1 + NB, 6 * D], tmp0 + 336 + 2 * D)
        sq = at("sq", [P, 2, TOK], zone_k)
        rms_bc = at("rms_bc", [P, TOK], zone_k + 2 * TOK)
        hs_tmp = at("hs_tmp", [P, KC, NS], zone_k + 3 * TOK)
        ones = at("ones", [P, P], zone_k + 3 * TOK + KC * NS)

        cosT = at("cosT", [P, TOK], tmp0)
        sinT = at("sinT", [P, TOK], tmp0 + TOK)
        rtmp = at("rtmp", [P, TOK], tmp0 + 2 * TOK)
        wV = at("wV", [P, KC, KV], tmp0 + 3 * TOK)
        sa = tmp0 + 3 * TOK + KC * KV
        kcx = at("kcx", [P, 2, NB, P + NT], sa)
        vc = at("vc", [P, NB, KV], sa + 2 * NB * (P + NT))
        qs = at("qs", [P, 2, NB, 32], tmp0)
        pS = at("pS", [P, NB, P + NT], tmp0 + 512)
        pZ = at("pZ", [P, NB * 36], tmp0 + 512 + 1056)
        pTs = at("pTs", [P, NB, P], tmp0 + 512 + 1056 + 288)
        pTn = at("pTn", [NS, NB, P], tmp0 + 512 + 1056 + 288 + 1024)
        ss0 = tmp0 + 512 + 1056 + 288 + 2048
        mxs, ngs, sks, sms, skes, rcs = [at(n, [P, NB], ss0 + 8 * i) for i, n in
                                         enumerate(("mxs", "ngs", "sks", "sms", "skes", "rcs"))]
        xlp = at("xlp", [P, XPAD + SEQ], tmp0)
        xls = at("xls", [P, NB, XPAD + NT], tmp0 + 1032)
        l1 = tmp0 + 1032 + 56
        yl, xc, gA, gB, gC = [at(n, [P, TOK], l1 + i * TOK) for i, n in
                              enumerate(("yl", "xc", "gA", "gB", "gC"))]
        t8 = at("t8", [P, NB], l1 + 5 * TOK)
        a0 = l1 + 5 * TOK + 8
        qst = at("qst", [P, 4, 2, P], a0)
        vst = at("vst", [P, 4, 2, P], a0 + 1024)
        pp = at("pp", [P, 2, 2, 2 * P], a0 + 2048)
        pT = at("pT", [P, 2, 4, P], a0 + 2048 + 1024)
        masks = at("masks", [P, BLKS, 2 * P], a0 + 2048 + 2048, BF16)
        zeros = at("zeros", [P, D], a0 + 2048 + 2048 + 1024)
        wmg = [at(f"wmg{i}", [P, KC, P], a0 + i * KC * P) for i in range(4)]
        KLO = 5
        wout_lo = at("wout_lo", [P, KLO, D], after_merged)
        assert after_merged + KLO * D <= a0
        wout_hi = at("wout_hi", [P, KC - KLO, D], a0 + 4 * KC * P)
        sg0 = a0 + 4 * KC * P + (KC - KLO) * D
        sga, sgr, mtmp = [at(n, [P, GW], sg0 + i * GW) for i, n in enumerate(("sga", "sgr", "mtmp"))]
        x1 = at("x1", [P, TILES, D], 0)
        bc0 = TILES * D
        G2p, G2s = at("G2p", [P, D], bc0), at("G2s", [NS, D], bc0 + D)
        G1p, G1s = at("G1p", [P, D], bc0 + 2 * D), at("G1s", [NS, D], bc0 + 3 * D)
        A2p, A2s = at("A2p", [P, D], bc0 + 4 * D), at("A2s", [NS, D], bc0 + 5 * D)
        B2p, B2s = at("B2p", [P, D], bc0 + 6 * D), at("B2s", [NS, D], bc0 + 7 * D)
        t4 = bc0 + 8 * D
        xin = at("xin", [P, 2, D], t4)
        h2 = at("h2", [P, 2, D], t4 + 2 * D)
        h2T = at("h2T", [P, KC, P], t4 + 4 * D)
        mst = at("mst", [P, 2, KC, P], t4 + 5 * D)
        junk = at("junk", [P, D], t4 + 7 * D, BF16)
        rcur = cur - 4 * D

        def keep(name, shape, dt=F32):
            nonlocal rcur
            t = at(name, shape, rcur, dt)
            rcur += (int(np.prod(shape[1:])) * (2 if dt == BF16 else 4) + 31) // 32 * 8
            return t

        EW = KC * FE * 2 + FC * D
        ew0 = room // 8 * 8 - 2 * EW
        wr = keep("wr", [P, KC, NG + NE])
        lg = keep("lg", [P, TILES, NG + NE])
        brt = keep("brt", [P, NG + NE])
        slot_tok = keep("slot_tok", [P, MAXB + 2], I32)
        pos_i = keep("pos_i", [P, TILES * 2], I32)
        wts = keep("wts", [P, TILES, 2])
        blk_i = keep("blk_i", [P, MAXB + 2], I32)
        cnt_i = keep("cnt_i", [P, 2], I32)
        idx = keep("idx", [P, 4], I32)
        wcur = keep("wcur", [P, 2])
        tpid = keep("tpid", [P, 2, TILES * 2], BF16)
        assert rcur <= ew0, (rcur, ew0)
        wg = [at(f"wg{s}", [P, KC, FE], ew0 + s * EW) for s in range(2)]
        wu = [at(f"wu{s}", [P, KC, FE], ew0 + s * EW + KC * FE) for s in range(2)]
        wd = [at(f"wd{s}", [P, FC, D], ew0 + s * EW + 2 * KC * FE) for s in range(2)]
        xg = at("xg", [P, 2, D], t4)
        xT = at("xT", [P, KC, P], t4 + 2 * D)
        sgm = at("sgm", [P, FC, P], t4 + 3 * D)
        aT = at("aT", [P, FC, P], t4 + 3 * D + FC * P)
        ysb = at("ysb", [P, 2, D], t4 + 4 * D)
        f0 = at("f0", [P, 2, D], t4)
        f1 = at("f1", [P, 2, D], t4 + 2 * D)
        yo = at("yo", [P, 2, D], t4 + 4 * D)
        fjunk = at("fjunk", [P, D], t4 + 6 * D, BF16)
        rt = bc0 + 2 * D

        def rtm(name, shape, dt=F32):
            nonlocal rt
            t = at(name, shape, rt, dt)
            rt += (int(np.prod(shape[1:])) * (2 if dt == BF16 else 4) + 31) // 32 * 8
            assert rt <= t4
            return t

        TK = TILES * 2
        lg8 = rtm("lg8", [P, TILES, 8])
        gm8 = rtm("gm8", [P, TILES, 8])
        gi8 = rtm("gi8", [P, TILES, 8], U32)
        gix = rtm("gix", [P, TILES])
        ohg = rtm("ohg", [P, TILES, NG])
        prd = rtm("prd", [P, TILES, EPG, NG])
        ing = rtm("ing", [P, TILES, EPG])
        em8 = rtm("em8", [P, TILES, 8])
        ei8 = rtm("ei8", [P, TILES, 8], U32)
        eix = rtm("eix", [P, TILES, 2])
        oh = rtm("oh", [P, TILES, 2, NE], BF16)
        ohs = rtm("ohs", [P, TILES, NE], BF16)
        gex = rtm("gex", [P, TILES, NG])
        gsm = rtm("gsm", [P, TILES])
        e1 = rtm("e1", [P, TILES])
        cmp9 = rtm("cmp9", [P, NE, TILES])
        nbk = rtm("nbk", [P, NE])
        incl = rtm("incl", [P, NE])
        bas = rtm("bas", [P, NE])
        cntf = rtm("cntf", [P, NE])
        qrk = rtm("qrk", [P, TILES, NE])
        mq = rtm("mq", [P, TILES, 2, NE])
        pos_f = rtm("pos_f", [P, TK])
        sl_i = rtm("sl_i", [P, 2, TK], I32)
        sl_f = rtm("sl_f", [P, 2, TK])
        ohslot = rtm("ohslot", [P, TK, P], BF16)
        ohblk = rtm("ohblk", [P, TK, MAXB], BF16)
        rhs2 = rtm("rhs2", [P, TK, 2, MAXB], BF16)
        slf = rtm("slf", [P, MAXB])
        cmpb = at("cmpb", [P, MAXB, NE], t4 + 2 * D)
        iot = at("iot", [P, P], t4 + 7 * D + 512)
        ubf = at("ubf", [P, 2, P], t4 + 7 * D + 512 + P, BF16)
        assert t4 + 7 * D + 512 + 2 * P <= 3 * big
        ps = ctx.enter_context(nc.psum_tensor("ps", [P, 8, 512], F32))
        h2_dram = nc.dram_tensor("h2_dram", [TOK, D], F32)
        y_dram = nc.dram_tensor("y_dram", [(MAXB + 2) * P, D], F32)

        def sem(name):
            return ctx.enter_context(nc.semaphore(name))

        ld_c, ld_bada, ld_small = sem("ld_c"), sem("ld_bada"), sem("ld_small")
        ld_wada = [sem(f"ld_wada{i}") for i in range(4)]
        ld_x = [sem(f"ld_x{i}") for i in range(4)]
        ld_rope, ld_kc, ld_wV = sem("ld_rope"), sem("ld_kc"), sem("ld_wV")
        ld_wA, ld_wB, ld_wlg = sem("ld_wA"), sem("ld_wB"), sem("ld_wlg")
        ld_wmg = [sem(f"ld_wmg{i}") for i in range(4)]
        ld_wout, ld_spread, ld_route = sem("ld_wout"), sem("ld_spread"), sem("ld_route")
        ld_xin = [sem(f"ld_xin{i}") for i in range(2)]
        ch_dve, ch_act, ch_pool = sem("ch_dve"), sem("ch_act"), sem("ch_pool")
        ch_unit, ch_lru, ch_tok, ch_fin = sem("ch_unit"), sem("ch_lru"), sem("ch_tok"), sem("ch_fin")
        ones_set, c_exp, c_silu = sem("ones_set"), sem("c_exp"), sem("c_silu")
        lam_abs, lam_exp, small_ready = sem("lam_abs"), sem("lam_exp"), sem("small_ready")
        ada_done, ada_kept = sem("ada_done"), sem("ada_kept")
        sq_ready, sq_used, ssq_done = sem("sq_ready"), sem("sq_used"), sem("ssq_done")
        rms_root, modT_done = sem("rms_root"), sem("modT_done")
        h_scaled, h_ready, hs_ready = sem("h_scaled"), sem("h_ready"), sem("hs_ready")
        pads_set = sem("pads_set")
        proj_done, proj_kept = sem("proj_done"), sem("proj_kept")
        v_done, v_kept = sem("v_done"), sem("v_kept")
        rot_done, rope_done = sem("rot_done"), sem("rope_done")
        s_staged, s_scores, s_negmax, s_exp = sem("s_staged"), sem("s_scores"), sem("s_negmax"), sem("s_exp")
        s_norm, s_turned, s_kept, s_pv, s_out = sem("s_norm"), sem("s_turned"), sem("s_kept"), sem("s_pv"), sem("s_out")
        u_staged, u_scores, u_negmax, u_exp = sem("u_staged"), sem("u_scores"), sem("u_negmax"), sem("u_exp")
        u_norm, u_turned, u_kept, u_pv, u_out = sem("u_norm"), sem("u_turned"), sem("u_kept"), sem("u_pv"), sem("u_out")
        xc_ready, gates_sum, decay, gap, gap_root = sem("xc_ready"), sem("gates_sum"), sem("decay"), sem("gap"), sem("gap_root")
        y_sq, y_arg, y_tanh, lru_done = sem("y_sq"), sem("y_arg"), sem("y_tanh"), sem("lru_done")
        lru_in = sem("lru_in")
        mg_done, mg_sig, mg_out = sem("mg_done"), sem("mg_sig"), sem("mg_out")
        mst_ready, mix_done, mix_sq, x1_half, x1_ready = sem("mst_ready"), sem("mix_done"), sem("mix_sq"), sem("x1_half"), sem("x1_ready")
        x1_sq, h2_ready, st_h2, h2_turned, h2T_ready = sem("x1_sq"), sem("h2_ready"), [sem("st_h2a"), sem("st_h2b")], sem("h2_turned"), sem("h2T_ready")
        lg_done, lg_kept, spread_done, spread_kept = sem("lg_done"), sem("lg_kept"), sem("spread_done"), sem("spread_kept")
        oh_ready, rank_done, rt_sub, rt_exp, pairs_ready = sem("oh_ready"), sem("rank_done"), sem("rt_sub"), sem("rt_exp"), sem("pairs_ready")
        hot_ready, slot_done, slots_ready = sem("hot_ready"), sem("slot_done"), sem("slots_ready")
        ld_g, ld_u, ld_d = [[sem(f"ld_{n}{s}") for s in range(2)] for n in "gud"]
        idx_ready, xg_ready, xg_used = sem("idx_ready"), [sem("xg_ready0"), sem("xg_ready1")], sem("xg_used")
        xT_a, xT_b = sem("xT_a"), sem("xT_b")
        gate_done, up_done, sg_ready, a_ready = sem("gate_done"), sem("up_done"), sem("sg_ready"), sem("a_ready")
        y_half, y_done, yk_a, yk_b = sem("y_half"), sem("y_done"), sem("yk_a"), sem("yk_b")
        st_y = [sem("st_y0"), sem("st_y1")]
        ch_moe, ch_fin2 = sem("ch_moe"), sem("ch_fin2")
        idx_seen = sem("idx_seen")
        fi_ready, ld_f = sem("fi_ready"), [sem("ld_f0"), sem("ld_f1")]
        f_sum, f_sq, f_used, yo_ready = sem("f_sum"), sem("f_sq"), sem("f_used"), sem("yo_ready")
        st_out = [sem("st_out0"), sem("st_out1")]
        st_side, st_kws, st_tail = sem("st_side"), sem("st_kws"), sem("st_tail")
        zeros_set, st_zeros = sem("zeros_set"), sem("st_zeros")

        block = ctx.enter_context(nc.Block())

        def bc(ap, shape):
            return ap.broadcast_to(list(shape))

        def grp(t):
            return t.rearrange("p (g t) -> p g t", g=GRP)

        def ge(eng, s, v):
            if not (isinstance(v, int) and v <= 0):
                eng.wait_ge(s, v)

        def outs_at(s):
            return (s,) if s < 6 else (6, 7, 8) if s == 8 else (9, 10, 11) if s == 9 else ()

        GC = [slice(g * GW, (g + 1) * GW) for g in range(GRP)]

        def number(i, o):
            return N_QK + 12 * i - 3 + o + (3 if isinstance(i, int) and i == 0 and o < 3 else 0)

        @block.sync
        def _(sp):
            for n in range(NADA):
                if n >= 4:
                    sp.wait_ge(ada_done, n - 3)
                sp.dma_start(wada[n % 4][:, :, :],
                             I["w_ada"][:, n * 512:(n + 1) * 512].rearrange("(k p) n -> p k n", p=P)
                             ).then_inc(ld_wada[n % 4], 16)
                if n < 4:
                    sp.dma_start(hT[:, 2 * n:2 * n + 2, :],
                                 I["xT"][2 * n * P:(2 * n + 2) * P, :].rearrange("(k p) t -> p k t", p=P)
                                 ).then_inc(ld_x[n], 16)
            sp.dma_start(wA[:, :, :], I["w_qk"][0]).then_inc(ld_wA, 16)
            sp.dma_start(wB[:, :, :], I["w_qk"][1]).then_inc(ld_wB, 16)
            sp.wait_ge(ada_kept, NADA)
            sp.wait_ge(h_ready, KC)
            sp.wait_ge(hs_ready, 1)
            sp.dma_start(wV[:, :, :], I["w_v"]).then_inc(ld_wV, 16)
            sp.dma_start(cosT[:, :], I["cos"]).then_inc(ld_rope, 16)
            sp.dma_start(sinT[:, :], I["sin"]).then_inc(ld_rope, 16)
            for p in range(2):
                sp.dma_start(kcx[:, p, :, 0:P], I["kcT"][:, p]).then_inc(ld_kc, 16)
            sp.dma_start(vc[:, :, :], I["v_cache"].rearrange("b k n -> k b n")).then_inc(ld_kc, 16)
            with sp.Fori(0, 4) as i:
                sp.wait_ge(proj_done, 6 * i + 3)
                sp.dma_start(wA[:, :, :], I["w_qk"][bass.ds(2 * i + 2, 1)].rearrange("a p k m -> p (a k) m")).then_inc(ld_wA, 16)
                sp.wait_ge(proj_done, 6 * i + 6)
                sp.dma_start(wB[:, :, :], I["w_qk"][bass.ds(2 * i + 3, 1)].rearrange("a p k m -> p (a k) m")).then_inc(ld_wB, 16)
            sp.wait_ge(proj_done, N_QK - 3)
            sp.dma_start(wA[:, :, :], I["w_xl"][0]).then_inc(ld_wA, 16)
            sp.wait_ge(zeros_set, 1)
            left = MAXB + 2 - MINB
            sp.dma_start(y_dram[MINB * P:, :].rearrange("(b p) n -> p b n", p=P),
                         bc(zeros[:, :].unsqueeze(1), (P, left, D))).then_inc(st_zeros, 16)
            sp.wait_ge(proj_done, N_QK)
            sp.dma_start(wB[:, :, :], I["w_yl"][0]).then_inc(ld_wB, 16)
            sp.dma_start(wlg[:, :, :], I["w_lg"][0]).then_inc(ld_wlg, 16)

            def round_weights(i):
                nxt = lambda name: I[name][bass.ds(i, 1)].rearrange("a p k m -> p (a k) m")
                sp.wait_ge(proj_done, number(i - 1, 2) + 1)
                sp.dma_start(wA[:, :, :], nxt("w_xl")).then_inc(ld_wA, 16)
                sp.wait_ge(proj_done, number(i - 1, 11) + 1)
                sp.dma_start(wlg[:, :, :], nxt("w_lg")).then_inc(ld_wlg, 16)
                sp.wait_ge(proj_done, number(i, 5) + 1)
                sp.dma_start(wB[:, :, :], nxt("w_yl")).then_inc(ld_wB, 16)

            round_weights(1)
            with sp.Fori(2, KC) as i:
                round_weights(i)
            sp.wait_ge(u_out, 4 + KC * BLKS)
            names = ("w_ga", "w_at", "w_gr", "w_lr")
            for q in range(4):
                sp.dma_start(wmg[q][:, :, :], I[names[q]][0]).then_inc(ld_wmg[q], 16)
            w_out = I["w_out"].rearrange("(k p) n -> p k n", p=P)
            sp.wait_ge(st_zeros, 16)
            sp.dma_start(wout_hi[:, :, :], w_out[:, KLO:, :]).then_inc(ld_wout, 16)
            sp.wait_ge(lru_done, KC + 1)
            sp.dma_start(wout_lo[:, :, :], w_out[:, 0:KLO, :]).then_inc(ld_wout, 16)
            with sp.Fori(1, KC) as i:
                for q in range(4):
                    sp.wait_ge(mg_done, 12 * i - 3 + q)
                    sp.dma_start(wmg[q][:, :, :], I[names[q]][bass.ds(i, 1)].rearrange("a p k m -> p (a k) m")).then_inc(ld_wmg[q], 16)
            sp.wait_ge(mg_done, 4 * GRP * KC)
            for row, (tp, ts) in enumerate(((G1p, G1s), (A2p, A2s), (G2p, G2s))):
                sp.dma_start(tp[:, :], I["g_rows"][row].partition_broadcast(P)).then_inc(ld_spread, 16)
                sp.dma_start(ts[:, :], I["g_rows"][row].partition_broadcast(NS)).then_inc(ld_spread, 16)
            for t in range(2):
                sp.dma_start(xin[:, t, :], I["x"][t * P:(t + 1) * P, :]).then_inc(ld_xin[t], 16)
            sp.dma_start(iot[:, :], I["iota"]).then_inc(ld_route, 16)
            sp.dma_start(ubf[:, :, :], I["upper"]).then_inc(ld_route, 16)
            sp.wait_ge(spread_done, 16)
            sp.dma_start(wr[:, :, :], I["w_r"]).then_inc(ld_route, 16)
            sp.dma_start(brt[:, :], I["b_r"].partition_broadcast(P)).then_inc(ld_route, 16)
            sp.dma_start(tpid[:, :, :], I["tpid"]).then_inc(ld_route, 16)

            def h2_store(t, s, n=P):
                sp.wait_ge(h2_ready, t + 1)
                sp.dma_start(h2_dram[bass.ds(t * P, n), :], h2[0:n, s, :]).then_inc(st_h2[s], 16)

            with sp.Fori(0, 3) as i:
                for s in range(2):
                    t = 2 * i + s
                    h2_store(t, s)
                    sp.wait_ge(x1_ready, t + 1)
                    sp.dma_start(xin[:, s, :], I["x"][bass.ds(t * P + 2 * P, P), :]).then_inc(ld_xin[s], 16)
            h2_store(6, 0)
            sp.wait_ge(x1_ready, 7)
            sp.dma_start(xin[0:NS, 0, :], I["x"][SEQ:TOK, :]).then_inc(ld_xin[0], 16)
            h2_store(7, 1)
            h2_store(8, 0, NS)

            sp.wait_ge(pairs_ready, 1)
            pairs = sp.value_load(cnt_i[0:1, 0:1], min_val=1, max_val=MAXB // 2)
            with sp.Fori(0, pairs) as i:
                for s in range(2):
                    e = sp.value_load(blk_i[0:1, bass.ds(2 * i + s, 1)], min_val=0, max_val=NE - 1)
                    sp.wait_ge(gate_done, 2 * i + s + 1)
                    sp.dma_start(wg[s][:, :, :], I["w_gate"][bass.ds(e, 1)].rearrange("a (p k) n -> p (a k) n", k=KC)).then_inc(ld_g[s], 16)
                    sp.wait_ge(up_done, 2 * i + s + 1)
                    sp.dma_start(wu[s][:, :, :], I["w_up"][bass.ds(e, 1)].rearrange("a (p k) n -> p (a k) n", k=KC)).then_inc(ld_u[s], 16)
                    sp.wait_ge(y_done, 2 * i + s + 1)
                    sp.dma_start(wd[s][:, :, :], I["w_down"][bass.ds(e, 1)].rearrange("a (m p) n -> p (a m) n", p=P)).then_inc(ld_d[s], 16)

            def out_store(t, s, n=P):
                sp.wait_ge(yo_ready, t + 1)
                sp.dma_start(O["y"][bass.ds(t * P, n), :], yo[0:n, s, :]).then_inc(st_out[s], 16)

            with sp.Fori(0, 4) as i:
                for s in range(2):
                    out_store(2 * i + s, s)
            out_store(8, 0, NS)
            sp.wait_ge(st_out[0], 16 * 5)
            sp.wait_ge(st_out[1], 16 * 4)
            sp.wait_ge(st_side, 16 * 4)
            sp.wait_ge(st_tail, 16)
            sp.wait_ge(st_kws, 32)

        @block.gpsimd
        def _(pool):
            pool.memset(ones[:, :], 1.0).then_inc(ones_set, 1)
            pool.memset(eps[:, :], EPS).then_inc(ones_set, 1)
            pool.memset(zeros[:, :], 0.0).then_inc(zeros_set, 1)
            pool.wait_ge(h_ready, KC)
            pool.wait_ge(hs_ready, 1)
            pool.memset(kT[:, :, 0:P], 0.0).then_inc(pads_set, 1)
            pool.memset(vtok[:, 0, :], 0.0).then_inc(pads_set, 1)
            pool.wait_ge(rope_done, 10)
            pool.wait_ge(v_kept, TILES)
            pool.wait_ge(s_out, 1)
            pool.wait_ge(st_kws, 32)
            pool.wait_ge(ld_small, 13 * 16)
            pool.sem_inc(u_out, 4)
            with pool.Fori(0, BLKS) as i:
                for u in range(KC):
                    pool.wait_ge(u_out, 8 * i + u + 1)
                    pool.tensor_tensor(qst[:, u % 4, :, :], bc(oT[:, u, bass.ds(i * P, P)].unsqueeze(1), (P, 2, P)),
                                       bc(halves[:, :].unsqueeze(2), (P, 2, P)), ALU.mult).then_inc(u_staged, 1)
                    lo = (u // 4) * P
                    pool.tensor_copy(vst[:, u % 4, :, :], vtok[:, bass.ds(i, 2), lo:lo + P]).then_inc(u_staged, 1)

            pool.wait_ge(slots_ready, 1)
            pool.wait_ge(st_h2[0], 16 * 5)
            pool.wait_ge(st_h2[1], 16 * 4)
            pairs = pool.value_load(cnt_i[0:1, 0:1], min_val=1, max_val=MAXB // 2)
            pool.sem_inc(xg_used, 1)

            def gather(j, n, s):
                if not isinstance(n, int):
                    pool.wait_ge(xg_used, n - 1)
                pool.tensor_copy(idx[:, s:s + 1], slot_tok[:, bass.ds(j, 1)]).then_inc(idx_ready, 1)
                pool.wait_ge(idx_ready, n)
                pool.sem_inc(idx_seen, 1)
                pool.indirect_dma_start(xg[:, s, :], None, h2_dram[:, :],
                                        bass.IndirectOffsetOnAxis(idx[:, s:s + 1], 0)).then_inc(xg_ready[s], 16)

            gather(0, 1, 0)
            with pool.Fori(0, pairs) as i:
                gather(2 * i + 1, 2 * i + 2, 1)
                gather(2 * i + 2, 2 * i + 3, 0)
            pool.wait_ge(st_y[0], pairs * 16 + 16)
            pool.wait_ge(st_y[1], pairs * 16 + 16)
            pool.wait_ge(xg_ready[0], pairs * 16 + 16)
            pool.sem_inc(f_used, 2)

            def pick(t, s, n=P):
                pool.wait_ge(f_used, t + 1)
                for k, f in ((0, f0), (1, f1)):
                    pool.tensor_copy(idx[:, 2 * s + k:2 * s + k + 1], pos_i[:, bass.ds(2 * t + k, 1)]).then_inc(fi_ready, 1)
                pool.wait_ge(fi_ready, 2 * t + 2)
                pool.sem_inc(idx_seen, 1)
                for k, f in ((0, f0), (1, f1)):
                    pool.indirect_dma_start(f[0:n, s, :], None, y_dram[:, :],
                                            bass.IndirectOffsetOnAxis(idx[0:n, 2 * s + k:2 * s + k + 1], 0)).then_inc(ld_f[s], 16)

            with pool.Fori(0, 4) as i:
                pick(2 * i, 0)
                pick(2 * i + 1, 1)
            pick(8, 0, NS)

        @block.scalar
        def _(act):
            act.dma_start(cT[:, :, :], I["cT"]).then_inc(ld_c, 16)
            act.dma_start(bada[:, :], I["b_ada"].partition_broadcast(1 + NB)).then_inc(ld_bada, 16)
            for t, name in ((ident, "ident"), (identb, "identb"), (rot, "rot"), (masks, "masks"), (halves, "halves"), (mask_s, "mask_s"), (sel, "sel"), (nsink_s, "sink_s"),
                            (lvec, "lvec"), (h0, "h0"), (stc, "stc"), (gpre, "gpre")):
                act.dma_start(t.ap(), I[name]).then_inc(ld_small, 16)
            act.dma_start(nsink[:, :], I["sinks"].partition_broadcast(P)).then_inc(ld_small, 16)
            act.wait_ge(ld_c, 16)
            act.activation(cE[:, :, :], cT[:, :, :], ACT.Exp, scale=-1.0).then_inc(c_exp, 1)
            act.wait_ge(lam_abs, 1)
            act.activation(spt[:, 1, :], spt[:, 0, :], ACT.Exp, scale=-1.0).then_inc(lam_exp, 1)
            for k in range(KC):
                act.wait_ge(ld_x[k // 2], 16)
                ge(act, sq_used, k - 1)
                act.activation(sq[:, k % 2, :], hT[:, k, :], ACT.Square).then_inc(sq_ready, 1)
            act.wait_ge(ssq_done, 1)
            act.wait_ge(ones_set, 2)
            act.activation(grp(rms_bc[:, :]), ps[:, 0:GRP, 0:GW], ACT.Sqrt, bias=eps[:, :], scale=1.0 / D).then_inc(rms_root, 1)
            for k in range(KC):
                act.wait_ge(h_scaled, k + 1)
                act.activation(hT[:, k, 0:SEQ], hT[:, k, 0:SEQ], ACT.Identity, bias=shT[:, k, 0:1]).then_inc(h_ready, 1)

            act.wait_ge(pads_set, 2)

            def keep(n, dst, bank):
                act.wait_ge(proj_done, n + 1)
                act.activation(dst, ps[:, bank, 0:GW], ACT.Copy).then_inc(proj_kept, 1)

            for p in range(2):
                for g in range(GRP):
                    keep(3 * p + g, kT[:, p, P + g * GW:P + (g + 1) * GW], g)
            for t in range(TILES):
                n = P if t < BLKS else NS
                act.wait_ge(v_done, t + 1)
                act.activation(vtok[0:n, t + 1, :], ps[0:n, 6 + t % 2, 0:KV], ACT.Copy).then_inc(v_kept, 1)
            act.wait_ge(v_kept, TILES)
            act.dma_start(O["vwp"], vtok[:, BLKS, :]).then_inc(st_side, 16)
            act.dma_start(O["vnew"], vtok[0:NS, TILES, :]).then_inc(st_side, 16)
            act.dma_start(O["vold"], I["v_cache"][:, NT:P, :]).then_inc(st_side, 16)
            act.wait_ge(rope_done, 2)
            act.dma_start(O["kwp"], kT[:, :, SEQ:SEQ + P]).then_inc(st_side, 16)
            with act.Fori(0, 4) as i:
                for q in range(2):
                    for g in range(GRP):
                        keep(6 * i + 6 + 3 * q + g, oT[:, 2 * i + q, GC[g]], g)

            act.wait_ge(s_negmax, 1)
            for b in range(NB):
                act.activation(pS[:, b, :], ps[:, 3 + b // 3, (b % 3) * (P + NT):(b % 3 + 1) * (P + NT)], ACT.Exp,
                               bias=ngs[:, b:b + 1], scale=SCALE, accum_out=sms[:, b:b + 1])
            act.activation(skes[:, :], sks[:, :], ACT.Exp).then_inc(s_exp, 1)
            for hf in range(2):
                act.wait_ge(s_turned, 2 * hf + 1)
                act.activation(pTs[:, 4 * hf:4 * hf + 4, :], ps[:, 6 + hf, :].rearrange("p (b r) -> p b r", b=4), ACT.Copy).then_inc(s_kept, 1)
                act.wait_ge(s_turned, 2 * hf + 2)
                act.activation(pTn[:, 4 * hf:4 * hf + 4, :], ps[0:NS, 3 + hf, :].rearrange("p (b r) -> p b r", b=4), ACT.Copy).then_inc(s_kept, 1)
            act.wait_ge(s_staged, 2)
            for p in range(2):
                act.dma_start(O["kws"][:, p], kcx[:, p, :, NT:P + NT]).then_inc(st_kws, 16)

            act.wait_ge(s_out, 1)
            act.wait_ge(st_kws, 32)
            act.sem_inc(u_exp, 2)

            def keep_outs(i, s):
                if s == 0:
                    act.wait_ge(xc_ready, i + 1)
                if s == 3:
                    act.wait_ge(lru_done, i)
                if s == KC:
                    act.wait_ge(lru_done, i + 1)
                for o in outs_at(s):
                    act.wait_ge(proj_done, number(i, o) + 1)
                    src = ps[:, o % 3, 0:GW]
                    g = o % 3
                    if o < 3 and g < 2:
                        act.activation(xlp[:, XPAD + g * GW:XPAD + (g + 1) * GW], src, ACT.Copy).then_inc(proj_kept, 1)
                    elif o < 3:
                        act.activation(xlp[:, XPAD + g * GW:], ps[:, o % 3, 0:GW - NS], ACT.Copy)
                        act.activation(xls[:, :, XPAD:], ps[:, o % 3, GW - NS:GW].rearrange("p (b t) -> p b t", b=NB), ACT.Copy).then_inc(proj_kept, 1)
                    elif o < 6:
                        act.activation(yl[:, GC[g]], src, ACT.Copy).then_inc(proj_kept, 1)
                    else:
                        dst, bias = ((gA, 0), (gB, 1))[o % 2]
                        act.activation(dst[:, GC[(o - 6) // 2]], src, ACT.Exp, bias=lcur[:, bias:bias + 1], scale=-1.0).then_inc(proj_kept, 1)

            def lru_step(i, s):
                if s == 1:
                    act.wait_ge(gates_sum, i)
                    act.activation(gC[:, :], gA[:, :], ACT.Exp, scale=lcur[:, 2:3])
                    act.activation(gA[:, :], gA[:, :], ACT.Tanh, scale=lcur[:, 2:3]).then_inc(decay, 1)
                if s == 2:
                    act.wait_ge(gap, i)
                    act.activation(xc[:, :], xc[:, :], ACT.Sqrt, scale=-1.0).then_inc(gap_root, 1)
                if s == 5:
                    act.wait_ge(lru_in, i)
                    act.activation(gB[:, :], yl[:, :], ACT.Square).then_inc(y_sq, 1)
                if s == 6:
                    act.wait_ge(y_arg, i)
                    act.activation(gB[:, :], gB[:, :], ACT.Tanh, scale=GELU_C).then_inc(y_tanh, 1)

            def act_round(i, first=False):
                for s in range(KC + 2):
                    if s < KC:
                        act.wait_ge(u_negmax, 8 * i + s + 1)
                        act.wait_ge(u_turned, 8 * i + s + 1)
                        for a in range(2):
                            act.activation(pp[:, s % 2, a, :], ps[:, 3 + s % 2, a * 2 * P:(a + 1) * 2 * P], ACT.Exp,
                                           bias=ngm[:, s % 2, a:a + 1], scale=SCALE, accum_out=sme[:, s % 2, a:a + 1])
                        act.activation(ske[:, s % 2, :], skd[:, s % 2, :], ACT.Exp).then_inc(u_exp, 1)
                    if s < KC and not (first and 3 <= s < 6):
                        keep_outs(i, s)
                    if not first:
                        if s == 5:
                            act.wait_ge(proj_kept, number(i, 5) + 1)
                        lru_step(i, s)
                    if s >= 2:
                        act.wait_ge(u_pv, 8 * i + s - 2 + 3)
                        act.activation(oT[:, s - 2, bass.ds(i * P, P)], ps[:, 7, 0:P], ACT.Copy).then_inc(u_out, 1)
                    if s >= KC:
                        keep_outs(i, s)

            act_round(0, True)
            with act.Fori(1, BLKS) as i:
                act_round(i)
            act.sem_inc(mg_sig, 3)
            act.wait_ge(lru_done, KC)
            for g in range(GRP):
                act.wait_ge(proj_done, N_PROJ - 2 + g)
                act.activation(yl[:, GC[g]], ps[:, g, 0:GW], ACT.Copy).then_inc(proj_kept, 1)
            act.wait_ge(proj_kept, N_PROJ)
            for s in range(KC):
                lru_step(KC, s)
            act.wait_ge(lru_done, KC + 1)
            act.dma_start(O["tail"], tail[:, :, :]).then_inc(st_tail, 16)

            with act.Fori(0, KC) as n:
                for g in range(GRP):
                    for q, dst in ((0, sga), (2, sgr)):
                        m = 4 * g + q
                        act.wait_ge(mg_done, 12 * n + m + 1)
                        act.wait_ge(mg_out, 6 * n + 2 * g + (2 if q == 0 else 3))
                        act.activation(dst[:, :], ps[:, m % 6, 0:GW], ACT.Sigmoid).then_inc(mg_sig, 1)

            def stage(t, s, n=P):
                act.activation(mst[:, s, :, 0:n], merged[:, :, bass.ds(t * P, n)], ACT.Copy).then_inc(mst_ready, 1)

            def tile_norms(t, s, n=P, ahead=True, ahead_n=P):
                act.wait_ge(mix_done, t + 1)
                act.activation(junk[0:n, :].rearrange("p (h c) -> p h c", h=2), ps[0:n, 2 * s:2 * s + 2, :], ACT.Square,
                               accum_out=sst[0:n, s, 0:1]).then_inc(ch_act, 1)
                act.wait_ge(ch_act, 2 * t + 1)
                act.activation(sst[0:n, s, 1:2], sst[0:n, s, 0:1], ACT.Sqrt, bias=eps[0:n, :], scale=1.0 / D).then_inc(mix_sq, 1)
                if ahead:
                    stage(t + 2, s, ahead_n)
                act.wait_ge(x1_ready, t + 1)
                act.activation(junk[0:n, :], x1[0:n, bass.ds(t, 1), :].rearrange("p a c -> p (a c)"), ACT.Square,
                               accum_out=sst[0:n, s, 2:3]).then_inc(ch_act, 1)
                act.wait_ge(ch_act, 2 * t + 2)
                act.activation(sst[0:n, s, 3:4], sst[0:n, s, 2:3], ACT.Sqrt, bias=eps[0:n, :], scale=1.0 / D).then_inc(x1_sq, 1)
                act.wait_ge(h2_turned, t + 1)
                ge(act, lg_done, t)
                act.activation(h2T[:, :, 0:n], ps[:, 4:6, :].rearrange("p h (k c) -> p (h k) c", c=P)[:, :, 0:n], ACT.Copy).then_inc(h2T_ready, 1)

            act.wait_ge(mg_out, 6 * KC + 3)
            stage(0, 0)
            stage(1, 1)
            tile_norms(0, 0)
            tile_norms(1, 1)
            with act.Fori(1, 3) as i:
                for s in range(2):
                    tile_norms(2 * i + s, s)
            tile_norms(6, 0, ahead_n=NS)
            tile_norms(7, 1, ahead=False)
            tile_norms(8, 0, n=NS, ahead=False)

            act.wait_ge(rt_sub, 1)
            act.activation(gex[:, :, :], gex[:, :, :], ACT.Exp)
            act.activation(e1[:, :], e1[:, :], ACT.Exp).then_inc(rt_exp, 1)

            act.wait_ge(pairs_ready, 1)
            pairs = act.value_load(cnt_i[0:1, 0:1], min_val=1, max_val=MAXB // 2)
            act.sem_inc(st_y[0], 16)
            act.sem_inc(st_y[1], 16)
            act.sem_inc(yk_a, 1)

            def keep_x(n):
                act.wait_ge(xg_used, n + 2)
                act.activation(xT[:, 0:4, :], ps[:, 0, :].rearrange("p (k c) -> p k c", c=P), ACT.Copy).then_inc(xT_a, 1)

            keep_x(0)
            with act.Fori(0, pairs) as i:
                for s in range(2):
                    n = 2 * i + s
                    act.wait_ge(gate_done, n + 3)
                    act.activation(sgm[:, :, :], ps[:, 2, :].rearrange("p (m c) -> p m c", c=P), ACT.Sigmoid).then_inc(sg_ready, 1)
                    keep_x(n + 1)
                    act.wait_ge(y_half, n + 1)
                    act.wait_ge(st_y[s], 16 * i + 16)
                    act.activation(ysb[:, s, 0:512], ps[:, 4, :], ACT.Copy).then_inc(yk_a, 1)
                    act.wait_ge(yk_a, n + 2)
                    act.wait_ge(yk_b, n + 2)
                    act.dma_start(y_dram[bass.ds(n * P, P), :], ysb[:, s, :]).then_inc(st_y[s], 16)

            def fin(t, s, n=P):
                act.wait_ge(f_sum, t + 1)
                act.activation(fjunk[0:n, :], f0[0:n, s, :], ACT.Square, accum_out=sst[0:n, s, 0:1]).then_inc(ch_fin, 1)
                act.wait_ge(ch_fin, t + 1)
                act.activation(sst[0:n, s, 1:2], sst[0:n, s, 0:1], ACT.Sqrt, bias=eps[0:n, :], scale=1.0 / D).then_inc(f_sq, 1)

            with act.Fori(0, 4) as i:
                for s in range(2):
                    fin(2 * i + s, s)
            fin(8, 0, NS)

        @block.vector
        def _(dve):
            c = Chain(dve, ch_dve)
            V = nc.vector
            dve.wait_ge(c_exp, 1)
            c(V.tensor_scalar(cE[:, :, :], cE[:, :, :], 1.0, None, ALU.add))
            c(V.reciprocal(cE[:, :, :], cE[:, :, :]))
            V.tensor_tensor(cE[:, :, :], cE[:, :, :], cT[:, :, :], ALU.mult).then_inc(c_silu, 1)
            dve.wait_ge(ld_small, 13 * 16)
            lam = lvec[:, :, 2]
            c(V.tensor_scalar(spt[:, 2, :], lam, -1.0, None, ALU.mult))
            V.tensor_tensor(spt[:, 0, :], lam, spt[:, 2, :], ALU.max).then_inc(lam_abs, 1)
            dve.wait_ge(lam_abs, 1)
            dve.wait_ge(lam_exp, 1)
            c(V.tensor_scalar(spt[:, 2, :], spt[:, 2, :], 0.0, None, ALU.max))
            c(V.tensor_scalar(spt[:, 3, :], spt[:, 1, :], 2.0, None, ALU.add))
            c(V.reciprocal(spt[:, 3, :], spt[:, 3, :]))
            c(V.tensor_tensor(spt[:, 3, :], spt[:, 1, :], spt[:, 3, :], ALU.mult))
            c(V.tensor_tensor(spt[:, 4, :], spt[:, 3, :], spt[:, 3, :], ALU.mult))
            c(V.tensor_scalar(spt[:, 0, :], spt[:, 4, :], 1.0 / 17, None, ALU.mult))
            for d in (15, 13, 11, 9, 7, 5, 3):
                c(V.scalar_tensor_tensor(spt[:, 0, :], spt[:, 0, :], 1.0 / d, spt[:, 4, :], ALU.add, ALU.mult))
            c(V.scalar_tensor_tensor(spt[:, 0, :], spt[:, 0, :], 1.0, spt[:, 3, :], ALU.add, ALU.mult))
            c(V.scalar_tensor_tensor(spt[:, 0, :], spt[:, 0, :], 2.0, spt[:, 2, :], ALU.mult, ALU.add))
            c(V.tensor_scalar(lvec[:, :, 2], spt[:, 0, :], -8.0, None, ALU.mult))
            c(V.tensor_scalar(lvec[:, :, 0:2], lvec[:, :, 0:2], -1.0, None, ALU.mult))
            c(V.tensor_scalar(nsink[:, :], nsink[:, :], -1.0, None, ALU.mult))
            c(V.tensor_scalar(nsink_s[:, :], nsink_s[:, :], -1.0, None, ALU.mult))
            dve.wait_ge(ld_bada, 16)

            def keep_mod(n):
                dve.wait_ge(ada_done, n + 1)
                dst = modh[:, n * 512:(n + 1) * 512] if n < 4 else mod[:, (n - 4) * 512:(n - 3) * 512]
                V.tensor_tensor(dst, ps[0:1 + NB, 3 + n % 4, :], bada[:, n * 512:(n + 1) * 512], ALU.add).then_inc(ada_kept, 1)

            for n in range(4):
                keep_mod(n)
            dve.wait_ge(modT_done, 1)
            c(V.tensor_copy(shT[:, :, :], ps[:, 7, 0:KC * (1 + NB)].rearrange("p (k j) -> p k j", k=KC)))
            c(V.scalar_tensor_tensor(scT[:, :, :], ps[:, 7, KC * (1 + NB):2 * KC * (1 + NB)].rearrange("p (k j) -> p k j", k=KC),
                                     1.0, bc(gpre[:, :].unsqueeze(2), (P, KC, 1 + NB)), ALU.add, ALU.mult))
            dve.wait_ge(rms_root, 1)
            c(V.reciprocal(rms_bc[:, :], rms_bc[:, :]))
            for k in range(KC):
                V.scalar_tensor_tensor(hT[:, k, 0:SEQ], hT[:, k, 0:SEQ], scT[:, k, 0:1], rms_bc[:, 0:SEQ],
                                       ALU.mult, ALU.mult).then_inc(h_scaled, 1)
                keep_mod(4 + k)
            hs4 = hs_tmp[:, :, :].rearrange("p k (b t) -> p k b t", b=NB)
            c(V.tensor_tensor(hs_tmp[:, :, :], hT[:, :, SEQ:TOK], bc(rms_bc[:, SEQ:TOK].unsqueeze(1), (P, KC, NS)), ALU.mult))
            c(V.tensor_tensor(hs4, hs4, bc(scT[:, :, 1:1 + NB].unsqueeze(3), (P, KC, NB, NT)), ALU.mult))
            V.tensor_tensor(hT[:, :, SEQ:TOK].rearrange("p k (b t) -> p k b t", b=NB), hs4,
                            bc(shT[:, :, 1:1 + NB].unsqueeze(3), (P, KC, NB, NT)), ALU.add).then_inc(hs_ready, 1)

            dve.wait_ge(ld_rope, 32)

            def rope(n, dst):
                dve.wait_ge(proj_kept, 3 * n + 3)
                ge(dve, rope_done, n)
                c(V.tensor_tensor(rtmp[:, :], dst, cosT[:, :], ALU.mult))
                dve.wait_ge(rot_done, n + 1)
                c(V.tensor_tensor(grp(dst), ps[:, 3:3 + GRP, 0:GW], grp(sinT[:, :]), ALU.mult))
                V.tensor_tensor(dst, dst, rtmp[:, :], ALU.add).then_inc(rope_done, 1)

            for p in range(2):
                rope(p, kT[:, p, P:])
            with dve.Fori(0, 4) as i:
                c.enter(i, 4)
                for q in range(2):
                    rope(2 * i + 2 + q, oT[:, bass.ds(2 * i + q, 1), :].rearrange("p a t -> p (a t)"))
            c.leave(4)

            dve.wait_ge(rope_done, 10)
            dve.wait_ge(ld_kc, 48)
            for p in range(2):
                V.tensor_copy(kcx[:, p, :, P:], kT[:, p, P + SEQ:].rearrange("p (b t) -> p b t", b=NB)).then_inc(s_staged, 1)
            for p in range(2):
                src = oT[:, 4 * p:4 * p + 4, SEQ:TOK].rearrange("p j (b t) -> p b j t", b=NB)
                for two in range(2):
                    V.tensor_copy(qs[:, p, :, 16 * two:16 * two + 16].rearrange("p b (j t) -> p b j t", j=4), src).then_inc(s_staged, 1)
            c(V.memset(pZ[:, :], 0.0))
            dve.wait_ge(s_scores, 1)
            for q, nb in enumerate((3, 3, 2)):
                c(V.tensor_reduce(mxs[:, 3 * q:3 * q + nb], ps[:, 3 + q, 0:nb * (P + NT)].rearrange("p (b k) -> p b k", b=nb), AX_X, ALU.max))
            c(V.scalar_tensor_tensor(ngs[:, :], mxs[:, :], -SCALE, bc(nsink_s[:, :], (P, NB)), ALU.mult, ALU.min))
            V.tensor_tensor(sks[:, :], ngs[:, :], bc(nsink_s[:, :], (P, NB)), ALU.subtract).then_inc(s_negmax, 1)
            dve.wait_ge(s_exp, 1)
            c(V.tensor_tensor(sms[:, :], sms[:, :], skes[:, :], ALU.add))
            c(V.reciprocal(rcs[:, :], sms[:, :]))
            c(V.tensor_tensor(pS[:, :, :], pS[:, :, :], bc(rcs[:, :].unsqueeze(2), (P, NB, P + NT)), ALU.mult))
            V.tensor_copy(pZ[:, :].rearrange("p (b x) -> p b x", b=NB)[:, :, 0:NT], pS[:, :, P:]).then_inc(s_norm, 1)
            dve.wait_ge(s_pv, 1)
            for p in range(2):
                ins = V.tensor_copy(oT[:, 4 * p:4 * p + 4, SEQ:TOK].rearrange("p j (b t) -> p b j t", b=NB),
                                    ps[:, 5, P * p:P * (p + 1)].rearrange("p (b j t) -> p b j t", b=NB, j=4))
            ins.then_inc(s_out, 1)

            u, l = Chain(dve, ch_unit), Chain(dve, ch_lru)
            dve.wait_ge(st_kws, 32)
            dve.wait_ge(s_out, 1)
            l(V.memset(xlp[:, 0:XPAD], 0.0))
            dve.sem_inc(xc_ready, 1)
            dve.sem_inc(lru_done, 1)
            dve.sem_inc(u_kept, 2)
            xcs = xc[:, SEQ:TOK].rearrange("p (b t) -> p b t", b=NB)
            def first(i, s):
                w = s % 2
                dve.wait_ge(u_scores, 8 * i + s + 1)
                u(V.tensor_reduce(mx[:, w, :], ps[:, 3 + w, :].rearrange("p (a k) -> p a k", a=2), AX_X, ALU.max))
                u(V.scalar_tensor_tensor(ngm[:, w, :], mx[:, w, :], -SCALE, nsink[:, 2 * s:2 * s + 2], ALU.mult, ALU.min))
                V.tensor_tensor(skd[:, w, :], ngm[:, w, :], nsink[:, 2 * s:2 * s + 2], ALU.subtract).then_inc(u_negmax, 1)

            def second(i, s):
                w = s % 2
                dve.wait_ge(u_exp, 8 * i + s + 3)
                u(V.tensor_tensor(sme[:, w, :], sme[:, w, :], ske[:, w, :], ALU.add))
                u(V.reciprocal(rcp[:, w, :], sme[:, w, :]))
                V.tensor_scalar(pp[:, w, 0, :], pp[:, w, 0, :], rcp[:, w, 0:1], None, ALU.mult)
                V.tensor_scalar(pp[:, w, 1, :], pp[:, w, 1, :], rcp[:, w, 1:2], None, ALU.mult).then_inc(u_norm, 1)

            def conv(i, s):
                j = s - 4
                if j == 0:
                    dve.wait_ge(proj_kept, number(i, 2) + 1)
                    l(V.tensor_copy(lcur[:, :], lvec[:, bass.ds(i, 1), :].rearrange("p a v -> p (a v)")))
                    l(V.tensor_scalar(xc[:, 0:SEQ], xlp[:, 0:SEQ], lcur[:, 4:5], lcur[:, 3:4], ALU.mult, ALU.add))
                    l(V.tensor_scalar(xcs, xls[:, :, 0:NT], lcur[:, 4:5], lcur[:, 3:4], ALU.mult, ALU.add))
                else:
                    w = lcur[:, 4 + j:5 + j]
                    l(V.scalar_tensor_tensor(xc[:, 0:SEQ], xlp[:, j:j + SEQ], w, xc[:, 0:SEQ], ALU.mult, ALU.add))
                    l(V.scalar_tensor_tensor(xcs, xls[:, :, j:j + NT], w, xcs, ALU.mult, ALU.add))
                if s == 7:
                    V.tensor_copy(tail[:, bass.ds(i, 1), 0:XPAD].rearrange("p a t -> p (a t)"), xlp[:, SEQ:SEQ + XPAD])
                    V.tensor_copy(tail[:, bass.ds(i, 1), 12:36].rearrange("p a (b t) -> p (a b) t", t=XPAD), xls[:, :, NT:]).then_inc(xc_ready, 1)

            def lru_step(i, s):
                if s == 0:
                    dve.wait_ge(proj_kept, number(i - 1, 11) + 1)
                    l(V.tensor_scalar(gA[:, :], gA[:, :], 1.0, None, ALU.add))
                    V.reciprocal(gA[:, :], gA[:, :]).then_inc(gates_sum, 1)
                if s == 1:
                    l(V.tensor_scalar(gB[:, :], gB[:, :], 1.0, None, ALU.add))
                    l(V.reciprocal(gB[:, :], gB[:, :]))
                    l(V.tensor_tensor(gB[:, :], gB[:, :], xc[:, :], ALU.mult))
                if s == 2:
                    dve.wait_ge(decay, i)
                    l(V.tensor_tensor(xc[:, :], gC[:, :], gC[:, :], ALU.mult))
                    V.scalar_tensor_tensor(xc[:, :], xc[:, :], 1.0, gA[:, :], ALU.add, ALU.mult).then_inc(gap, 1)
                if s == 3:
                    dve.wait_ge(gap_root, i)
                    V.tensor_tensor(xc[:, :], xc[:, :], gB[:, :], ALU.mult).then_inc(lru_in, 1)
                    at0 = gC[:, SEQ:TOK].rearrange("p (b t) -> p b t", b=NB)[:, :, 0]
                    l(V.tensor_tensor(t8[:, :], at0, h0[:, bass.ds(i - 1, 1), :].rearrange("p a b -> p (a b)"), ALU.mult))
                    dve.wait_ge(lru_in, i)
                    l(V.tensor_tensor(xcs[:, :, 0], xcs[:, :, 0], t8[:, :], ALU.add))
                    l(V.memset(at0, 0.0))
                    l(V.tensor_tensor_scan(gA[:, 0:SEQ], gC[:, 0:SEQ], xc[:, 0:SEQ], 0.0, ALU.mult, ALU.add))
                    l(V.tensor_tensor_scan(gA[:, SEQ:TOK], gC[:, SEQ:TOK], xc[:, SEQ:TOK], 0.0, ALU.mult, ALU.add))
                    l(V.tensor_copy(tail[:, bass.ds(i - 1, 1), 3:4].rearrange("p a t -> p (a t)"), gA[:, SEQ - 1:SEQ]))
                    l(V.tensor_copy(tail[:, bass.ds(i - 1, 1), 4:12].rearrange("p a t -> p (a t)"),
                                    gA[:, SEQ:TOK].rearrange("p (b t) -> p b t", b=NB)[:, :, NT - 1]))
                if s == 6:
                    dve.wait_ge(y_sq, i)
                    l(V.tensor_scalar(gB[:, :], gB[:, :], GELU_A, 1.0, ALU.mult, ALU.add))
                    V.tensor_tensor(gB[:, :], gB[:, :], yl[:, :], ALU.mult).then_inc(y_arg, 1)
                if s == 7:
                    dve.wait_ge(y_tanh, i)
                    l(V.scalar_tensor_tensor(gB[:, :], gB[:, :], 1.0, yl[:, :], ALU.add, ALU.mult))
                    V.scalar_tensor_tensor(olT[:, bass.ds(i - 1, 1), :].rearrange("p a t -> p (a t)"), gB[:, :], 0.5, gA[:, :],
                                           ALU.mult, ALU.mult).then_inc(lru_done, 1)

            def dve_round(i, begin=False):
                for s in range(KC + 2):
                    if s < KC:
                        first(i, s)
                    if s == 0:
                        l(V.tensor_copy(xls[:, :, 0:XPAD], stc[:, bass.ds(i, 1), :, :].rearrange("p a b t -> p (a b) t")))
                    if not begin:
                        lru_step(i, s)
                    if 4 <= s < KC:
                        conv(i, s)
                    if s < KC:
                        second(i, s)
                    if 1 <= s <= KC:
                        w = (s - 1) % 2
                        dve.wait_ge(u_turned, 8 * i + s - 1 + 3)
                        dve.wait_ge(u_pv, 8 * i + s - 1 + 1)
                        V.tensor_copy(pT[:, w, :, :], ps[:, 5 + w, :].rearrange("p (k q) -> p k q", k=4)).then_inc(u_kept, 1)

            dve_round(0, True)
            with dve.Fori(1, BLKS) as i:
                u.enter(i - 1, 4 * KC)
                l.enter(i - 1, 24)
                dve_round(i)
            u.leave(BLKS - 1)
            l.leave(BLKS - 1)
            dve.wait_ge(st_side, 64)
            dve.sem_inc(mg_out, 3)
            for s in range(KC):
                lru_step(KC, s)

            with dve.Fori(0, KC) as n:
                l.enter(n, GRP)
                for g in range(GRP):
                    dve.wait_ge(mg_done, 12 * n + 4 * g + 2)
                    dve.wait_ge(mg_sig, 6 * n + 2 * g + 4)
                    dve.wait_ge(mg_out, 6 * n + 2 * g + 3)
                    V.tensor_tensor(mtmp[:, :], sga[:, :], ps[:, (4 * g + 1) % 6, 0:GW], ALU.mult).then_inc(mg_out, 1)
                    dve.wait_ge(mg_done, 12 * n + 4 * g + 4)
                    dve.wait_ge(mg_sig, 6 * n + 2 * g + 5)
                    l(V.tensor_tensor(sgr[:, :], sgr[:, :], ps[:, (4 * g + 3) % 6, 0:GW], ALU.mult))
                    dve.wait_ge(mg_out, 6 * n + 2 * g + 4)
                    V.tensor_tensor(merged[:, bass.ds(n, 1), GC[g]].rearrange("p a t -> p (a t)"), mtmp[:, :], sgr[:, :],
                                    ALU.add).then_inc(mg_out, 1)
            l.leave(KC)

            dve.wait_ge(ld_spread, 96)
            kinds = ((G1p, G1s), (B2p, B2s), (A2p, A2s), (G2p, G2s))
            q = 0
            for r in range(4):
                for nn in range(2):
                    for t, n in zip(kinds[r], (P, NS)):
                        dst, src = t[0:n, nn * 512:(nn + 1) * 512], ps[0:n, 4 + q % 4, :]
                        q += 1
                        dve.wait_ge(spread_done, q)
                        if r == 1:
                            ins = V.tensor_copy(dst, src)
                        elif r == 2:
                            ins = V.scalar_tensor_tensor(dst, src, 1.0, dst, ALU.add, ALU.mult)
                        else:
                            ins = V.tensor_tensor(dst, src, dst, ALU.mult)
                        ins.then_inc(spread_kept, 1)
            dve.wait_ge(spread_kept, 16)
            k = Chain(dve, ch_tok)
            k(V.memset(lg[:, TILES - 1, :], 0.0))
            dve.wait_ge(ld_route, 80)

            def keep_logits(t, n=P):
                dve.wait_ge(lg_done, t + 1)
                V.tensor_tensor(lg[0:n, bass.ds(t, 1), :].rearrange("p a c -> p (a c)"), ps[0:n, 6, 0:NG + NE], brt[0:n, :],
                                ALU.add).then_inc(lg_kept, 1)

            def tile_sums(t, s, i, n=P):
                G1, A2, B2 = (G1p, A2p, B2p) if n == P else (G1s, A2s, B2s)
                xt = x1[0:n, bass.ds(t, 1), :].rearrange("p a c -> p (a c)")
                half = lambda x: x.rearrange("p (h c) -> p h c", h=2)
                dve.wait_ge(mix_sq, t + 1)
                k(V.reciprocal(sst[0:n, s, 1:2], sst[0:n, s, 1:2]))
                V.scalar_tensor_tensor(half(xt), ps[0:n, 2 * s:2 * s + 2, :], sst[0:n, s, 1:2], half(G1[0:n, :]),
                                       ALU.mult, ALU.mult).then_inc(x1_half, 1)
                dve.wait_ge(x1_half, t + 1)
                dve.wait_ge(ld_xin[s], 16 * i + 16)
                V.tensor_tensor(xt, xt, xin[0:n, s, :], ALU.add).then_inc(x1_ready, 1)
                dve.wait_ge(x1_sq, t + 1)
                k(V.reciprocal(sst[0:n, s, 3:4], sst[0:n, s, 3:4]))
                ge(dve, st_h2[s], 16 * i)
                ge(dve, h2_turned, t - 1)
                k(V.scalar_tensor_tensor(h2[0:n, s, :], xt, sst[0:n, s, 3:4], A2[0:n, :], ALU.mult, ALU.mult))
                V.tensor_tensor(h2[0:n, s, :], h2[0:n, s, :], B2[0:n, :], ALU.add).then_inc(h2_ready, 1)
                if not (isinstance(t, int) and t == 0):
                    keep_logits(t - 1)

            tile_sums(0, 0, 0)
            tile_sums(1, 1, 0)
            with dve.Fori(1, 4) as i:
                k.enter(i - 1, 6)
                for s in range(2):
                    tile_sums(2 * i + s, s, i)
            k.leave(3)
            tile_sums(8, 0, 4, NS)
            keep_logits(8, NS)

            dve.wait_ge(lg_kept, TILES)
            dve.wait_ge(h2_ready, TILES)
            k(V.memset(lg8[:, :, :], -3.0e38))
            k(V.tensor_copy(lg8[:, :, 0:NG], lg[:, :, 0:NG]))
            for t in range(TILES):
                k(V.max(gm8[:, t, :], lg8[:, t, :]))
            for t in range(TILES):
                k(V.max_index(gi8[:, t, :], gm8[:, t, :], lg8[:, t, :]))
            k(V.tensor_copy(gix[:, :], gi8[:, :, 0]))
            k(V.tensor_tensor(ohg[:, :, :], bc(iot[:, 0:NG].unsqueeze(1), (P, TILES, NG)), bc(gix[:, :].unsqueeze(2), (P, TILES, NG)), ALU.is_equal))
            for t in range(TILES):
                k(V.tensor_tensor(prd[:, t, :, :], lg[:, t, NG:].rearrange("p (g e) -> p e g", g=NG),
                                  bc(ohg[:, t, :].unsqueeze(1), (P, EPG, NG)), ALU.mult))
            k(V.tensor_reduce(ing[:, :, :], prd[:, :, :, :], AX_X, ALU.add))
            for t in range(TILES):
                k(V.max(em8[:, t, :], ing[:, t, :]))
            for t in range(TILES):
                k(V.max_index(ei8[:, t, :], em8[:, t, :], ing[:, t, :]))
            k(V.tensor_copy(eix[:, :, :], ei8[:, :, 0:2]))
            k(V.scalar_tensor_tensor(eix[:, :, :], bc(gix[:, :].unsqueeze(2), (P, TILES, 2)), float(EPG), eix[:, :, :], ALU.mult, ALU.add))
            k(V.tensor_tensor(oh[:, :, :, :].rearrange("p t k e -> p (t k) e"), bc(iot[:, 0:NE].unsqueeze(1), (P, TK, NE)),
                              bc(eix[:, :, :].rearrange("p t k -> p (t k)").unsqueeze(2), (P, TK, NE)), ALU.is_equal))
            V.tensor_tensor(ohs[:, :, :], oh[:, :, 0, :], oh[:, :, 1, :], ALU.add).then_inc(oh_ready, 1)
            k(V.tensor_tensor(gex[:, :, :], lg[:, :, 0:NG], bc(gm8[:, :, 0:1], (P, TILES, NG)), ALU.subtract))
            V.tensor_tensor(e1[:, :], em8[:, :, 1], em8[:, :, 0], ALU.subtract).then_inc(rt_sub, 1)
            dve.wait_ge(rank_done, 1)
            k(V.tensor_copy(cntf[:, :], ps[:, 7, TILES * NE:(TILES + 1) * NE]))
            k(V.scalar_tensor_tensor(cmp9[:, :, :], bc(iot[:, 0:TILES].unsqueeze(1), (P, NE, TILES)), float(P),
                                     bc(cntf[:, :].unsqueeze(2), (P, NE, TILES)), ALU.mult, ALU.is_lt))
            k(V.tensor_reduce(nbk[:, :], cmp9[:, :, :], AX_X, ALU.add))
            k(V.memset(bas[:, :], 1.0))
            k(V.tensor_tensor_scan(incl[:, :], bas[:, :], nbk[:, :], 0.0, ALU.mult, ALU.add))
            dve.wait_ge(st_h2[0], 16 * 5)
            dve.wait_ge(st_h2[1], 16 * 4)
            k(V.tensor_tensor(cmpb[:, :, :], bc(iot[:, 0:MAXB].unsqueeze(2), (P, MAXB, NE)), bc(incl[:, :].unsqueeze(1), (P, MAXB, NE)), ALU.is_ge))
            k(V.tensor_reduce(slf[:, :], cmpb[:, :, :], AX_X, ALU.add))
            k(V.tensor_scalar(blk_i[:, 0:MAXB], slf[:, :], float(NE - 1), None, ALU.min))
            k(V.tensor_scalar(cnt_i[:, 1:2], incl[:, NE - 1:NE], 1.0, None, ALU.add))
            V.tensor_scalar(cnt_i[:, 0:1], cnt_i[:, 1:2], 1, None, ALU.logical_shift_right).then_inc(pairs_ready, 1)
            k(V.tensor_tensor(bas[:, :], incl[:, :], nbk[:, :], ALU.subtract))
            k(V.tensor_scalar(bas[:, :], bas[:, :], float(P), None, ALU.mult))
            k(V.tensor_tensor(qrk[:, :, :], ps[:, 7, 0:TILES * NE].rearrange("p (t e) -> p t e", t=TILES), bc(bas[:, :].unsqueeze(1), (P, TILES, NE)), ALU.add))
            for a in range(2):
                k(V.tensor_tensor(mq[:, :, a, :], oh[:, :, a, :], qrk[:, :, :], ALU.mult))
            k(V.tensor_reduce(pos_f[:, :], mq[:, :, :, :].rearrange("p t k e -> p (t k) e"), AX_X, ALU.add))
            k(V.tensor_copy(pos_i[:, :], pos_f[:, :]))
            k(V.tensor_scalar(sl_i[:, 0, :], pos_i[:, :], P - 1, None, ALU.bitwise_and))
            k(V.tensor_scalar(sl_i[:, 1, :], pos_i[:, :], 7, None, ALU.logical_shift_right))
            k(V.tensor_copy(sl_f[:, :, :], sl_i[:, :, :]))
            k(V.tensor_tensor(ohslot[:, :, :], bc(iot[:, :].unsqueeze(1), (P, TK, P)), bc(sl_f[:, 0, :].unsqueeze(2), (P, TK, P)), ALU.is_equal))
            k(V.tensor_tensor(ohblk[:, :, :], bc(iot[:, 0:MAXB].unsqueeze(1), (P, TK, MAXB)), bc(sl_f[:, 1, :].unsqueeze(2), (P, TK, MAXB)), ALU.is_equal))
            for a in range(2):
                ins = V.tensor_tensor(rhs2[:, :, a, :], ohblk[:, :, :], bc(tpid[:, a, :].unsqueeze(2), (P, TK, MAXB)), ALU.mult)
            ins.then_inc(hot_ready, 1)
            k(V.memset(slot_tok[:, :], 0))
            dve.wait_ge(slot_done, 1)
            k(V.tensor_copy(slf[:, :], ps[:, 6, MAXB:2 * MAXB]))
            V.scalar_tensor_tensor(slot_tok[:, 0:MAXB], ps[:, 6, 0:MAXB], float(P), slf[:, :], ALU.mult, ALU.add).then_inc(slots_ready, 1)
            dve.wait_ge(rt_exp, 1)
            k(V.tensor_reduce(gsm[:, :], gex[:, :, :], AX_X, ALU.add))
            k(V.scalar_tensor_tensor(gsm[:, :], e1[:, :], 1.0, gsm[:, :], ALU.add, ALU.mult))
            k(V.reciprocal(wts[:, :, 0], gsm[:, :]))
            k(V.tensor_tensor(wts[:, :, 1], wts[:, :, 0], e1[:, :], ALU.mult))

            pairs = dve.value_load(cnt_i[0:1, 0:1], min_val=1, max_val=MAXB // 2)
            dve.sem_inc(yk_b, 1)

            def keep_x(n):
                dve.wait_ge(xg_used, n + 2)
                V.tensor_copy(xT[:, 4:8, :], ps[:, 1, :].rearrange("p (k c) -> p k c", c=P)).then_inc(xT_b, 1)

            keep_x(0)
            with dve.Fori(0, pairs) as i:
                for s in range(2):
                    n = 2 * i + s
                    dve.wait_ge(sg_ready, n + 1)
                    V.tensor_tensor(sgm[:, :, :], sgm[:, :, :], ps[:, 2, :].rearrange("p (m c) -> p m c", c=P), ALU.mult).then_inc(ch_moe, 1)
                    dve.wait_ge(ch_moe, n + 1)
                    dve.wait_ge(up_done, n + 3)
                    V.tensor_tensor(aT[:, :, :], sgm[:, :, :], ps[:, 3, :].rearrange("p (m c) -> p m c", c=P), ALU.mult).then_inc(a_ready, 1)
                    keep_x(n + 1)
                    dve.wait_ge(y_done, n + 3)
                    dve.wait_ge(st_y[s], 16 * i + 16)
                    V.tensor_copy(ysb[:, s, 512:1024], ps[:, 5, :]).then_inc(yk_b, 1)

            z = Chain(dve, ch_fin2)

            def fin(t, s, i, n=P):
                dve.wait_ge(ld_f[s], 32 * i + 32)
                w = wts[0:n, bass.ds(t, 1), :].rearrange("p a k -> p (a k)")
                G2 = G2p if n == P else G2s
                z(V.tensor_copy(wcur[0:n, :], w))
                z(V.tensor_scalar(f0[0:n, s, :], f0[0:n, s, :], wcur[0:n, 0:1], None, ALU.mult))
                V.scalar_tensor_tensor(f0[0:n, s, :], f1[0:n, s, :], wcur[0:n, 1:2], f0[0:n, s, :], ALU.mult, ALU.add).then_inc(f_sum, 1)
                dve.wait_ge(f_sq, t + 1)
                z(V.reciprocal(sst[0:n, s, 1:2], sst[0:n, s, 1:2]))
                ge(dve, st_out[s], 16 * i)
                V.scalar_tensor_tensor(yo[0:n, s, :], f0[0:n, s, :], sst[0:n, s, 1:2], G2[0:n, :], ALU.mult, ALU.mult).then_inc(f_used, 1)
                dve.wait_ge(f_used, t + 3)
                V.tensor_tensor(yo[0:n, s, :], yo[0:n, s, :], x1[0:n, bass.ds(t, 1), :].rearrange("p a c -> p (a c)"), ALU.add).then_inc(yo_ready, 1)

            fin(0, 0, 0)
            fin(1, 1, 0)
            with dve.Fori(1, 4) as i:
                z.enter(i - 1, 6)
                for s in range(2):
                    fin(2 * i + s, s, i)
            z.leave(3)
            fin(8, 0, 4, NS)

        @block.tensor
        def _(pe):
            def mm(out, lhsT, rhs, start, stop):
                return pe.matmul(out, lhsT, rhs, start=start, stop=stop, skip_group_check=True)

            def chunk_sum(out, w, src):
                for k in range(KC):
                    ins = mm(out, w(k), src(k), k == 0, k == KC - 1)
                return ins

            def ada(n):
                pe.wait_ge(ld_wada[n % 4], 16 * (n // 4 + 1))
                ge(pe, ada_kept, n - 3)
                chunk_sum(ps[0:1 + NB, 3 + n % 4, :], lambda k: cE[:, k, :], lambda k: wada[n % 4][:, k, :]).then_inc(ada_done, 1)

            pe.wait_ge(c_silu, 1)
            for n in range(4):
                ada(n)
            pe.wait_ge(ones_set, 1)
            for k in range(KC):
                pe.wait_ge(sq_ready, k + 1)
                for g in range(GRP):
                    ins = mm(ps[:, g, 0:GW], ones[:, :], sq[:, k % 2, GC[g]], k == 0, k == KC - 1)
                    if g == GRP - 1:
                        ins.then_inc(ssq_done if k == KC - 1 else sq_used, 1)
            pe.wait_ge(ld_small, 13 * 16)
            pe.wait_ge(ada_kept, 4)
            for k in range(2 * KC):
                ins = pe.transpose(ps[:, 7, k * (1 + NB):(k + 1) * (1 + NB)], modh[:, k * P:(k + 1) * P], ident[0:1 + NB, 0:1 + NB])
            ins.then_inc(modT_done, 1)
            for n in range(4, NADA):
                ada(n)

            pe.wait_ge(h_ready, KC)
            pe.wait_ge(hs_ready, 1)
            pe.wait_ge(rms_root, 1)

            def project(n, w):
                for g in range(GRP):
                    ge(pe, proj_kept, n + g - 2)
                    chunk_sum(ps[:, g, 0:GW], lambda k: w[:, k, :], lambda k: hT[:, k, GC[g]]).then_inc(proj_done, 1)

            def turn(n, src):
                pe.wait_ge(proj_kept, 3 * n + 3)
                ge(pe, rope_done, n)
                for g in range(GRP):
                    ins = mm(ps[:, 3 + g, 0:GW], rot[:, :], src(g), True, True)
                ins.then_inc(rot_done, 1)

            pe.wait_ge(ld_wA, 16)
            project(0, wA)
            pe.wait_ge(ld_wB, 16)
            project(3, wB)
            pe.wait_ge(ada_kept, NADA)
            turn(0, lambda g: kT[:, 0, P + g * GW:P + (g + 1) * GW])
            pe.wait_ge(ld_wV, 16)
            for t in range(TILES):
                n = P if t < BLKS else NS
                ge(pe, v_kept, t - 1)
                chunk_sum(ps[0:n, 6 + t % 2, 0:KV], lambda k: hT[:, k, t * P:t * P + n], lambda k: wV[:, k, :]).then_inc(v_done, 1)
            turn(1, lambda g: kT[:, 1, P + g * GW:P + (g + 1) * GW])
            with pe.Fori(0, 4) as i:
                pe.wait_ge(ld_wA, 16 * i + 32)
                project(6 * i + 6, wA)
                pe.wait_ge(ld_wB, 16 * i + 32)
                project(6 * i + 9, wB)
                for q in range(2):
                    turn(2 * i + 2 + q, lambda g: oT[:, bass.ds(2 * i + q, 1), GC[g]].rearrange("p a t -> p (a t)"))

            pe.wait_ge(s_staged, 6)
            pe.wait_ge(rope_done, 10)
            for b in range(NB):
                cols = slice((b % 3) * (P + NT), (b % 3 + 1) * (P + NT))
                mm(ps[:, 3 + b // 3, cols], identb[:, :], mask_s[:, :], True, False)
                for kv in range(4):
                    p, a = kv // 2, HD * (kv % 2)
                    ins = mm(ps[32 * kv:32 * kv + 32, 3 + b // 3, cols], qs[a:a + HD, p, b, :], kcx[a:a + HD, p, b, :], False, True)
            ins.then_inc(s_scores, 1)
            pe.wait_ge(s_norm, 1)
            for hf in range(2):
                for b in range(4):
                    ins = pe.transpose(ps[:, 6 + hf, b * P:(b + 1) * P], pS[:, 4 * hf + b, 0:P], ident[:, :])
                ins.then_inc(s_turned, 1)
                for b in range(4):
                    at = (4 * hf + b) * NS
                    ins = pe.transpose(ps[0:NS, 3 + hf, b * P:(b + 1) * P], pZ[:, at:at + NS], ident[:, :])
                ins.then_inc(s_turned, 1)
            pe.wait_ge(s_kept, 4)
            for kv in range(4):
                p, a = kv // 2, HD * (kv % 2)
                mm(ps[a:a + HD, 5, P * p:P * (p + 1)], vtok[0:NS, TILES, HD * kv:HD * kv + HD], pTn[:, :, 32 * kv:32 * kv + 16], p == 0, False)
            for kv in range(4):
                p, a = kv // 2, HD * (kv % 2)
                for b in range(NB):
                    ins = mm(ps[a:a + HD, 5, P * p + 16 * b:P * p + 16 * b + 16], vc[:, b, HD * kv:HD * kv + HD],
                             pTs[:, b, 32 * kv:32 * kv + 16], False, True)
            ins.then_inc(s_pv, 1)

            pe.sem_inc(u_turned, 2)
            pe.sem_inc(u_pv, 2)
            pe.wait_ge(s_out, 1)
            def outs(i, s):
                for o in outs_at(s):
                    if o == 0:
                        pe.wait_ge(ld_wA, 16 * i + 96)
                    if o == 3:
                        pe.wait_ge(ld_wB, 16 * i + 80)
                    if o == 6:
                        pe.wait_ge(ld_wlg, 16 * i + 16)
                        pe.wait_ge(xc_ready, i + 2)
                    pe.wait_ge(proj_kept, number(i, o) - 2)
                    out = ps[:, o % 3, 0:GW]
                    if o < 6:
                        w = wA if o < 3 else wB
                        chunk_sum(out, lambda k: w[:, k, :], lambda k: hT[:, k, GC[o % 3]]).then_inc(proj_done, 1)
                    else:
                        mm(out, wlg[:, o % 2, :], xc[:, GC[(o - 6) // 2]], True, True).then_inc(proj_done, 1)

            def pe_round(i, begin=False):
                for s in range(KC + 2):
                    if s < KC:
                        pe.wait_ge(u_staged, 16 * i + 2 * s + 2)
                        pe.wait_ge(u_exp, 8 * i + s + 1)
                        for a in range(2):
                            out = ps[:, 3 + s % 2, a * 2 * P:(a + 1) * 2 * P]
                            mm(out, identb[:, :], masks[:, bass.ds(i, 1), :].rearrange("p a k -> p (a k)"), True, False)
                            ins = mm(out, qst[:, s % 4, a, :], kT[:, s // 4, bass.ds(i * P, 2 * P)], False, True)
                        ins.then_inc(u_scores, 1)
                    if s < KC and not (begin and 3 <= s < 6):
                        outs(i, s)
                    if 1 <= s <= KC:
                        w = (s - 1) % 2
                        pe.wait_ge(u_norm, 8 * i + s)
                        pe.wait_ge(u_kept, 8 * i + s)
                        for a in range(2):
                            for hf in range(2):
                                q = 2 * a + hf
                                ins = pe.transpose(ps[:, 5 + w, q * P:(q + 1) * P], pp[:, w, a, hf * P:(hf + 1) * P], ident[:, :])
                        ins.then_inc(u_turned, 1)
                    if s >= 2:
                        w = (s - 2) % 2
                        pe.wait_ge(u_kept, 8 * i + s - 2 + 3)
                        pe.wait_ge(u_out, 8 * i + s - 2 + 4)
                        for a in range(2):
                            for hf in range(2):
                                ins = mm(ps[HD * a:HD * a + HD, 7, 0:P], vst[:, (s - 2) % 4, hf, HD * a:HD * a + HD],
                                         pT[:, w, 2 * a + hf, :], hf == 0, hf == 1)
                        ins.then_inc(u_pv, 1)
                    if s >= KC:
                        outs(i, s)

            pe_round(0, True)
            with pe.Fori(1, BLKS) as i:
                pe_round(i)
            pe.wait_ge(ld_wB, 16 * KC + 80)
            for g in range(GRP):
                pe.wait_ge(proj_kept, N_PROJ - 5 + g)
                chunk_sum(ps[:, g, 0:GW], lambda k: wB[:, k, :], lambda k: hT[:, k, GC[g]]).then_inc(proj_done, 1)

            pe.wait_ge(u_out, 4 + KC * BLKS)
            pe.wait_ge(proj_kept, N_PROJ)
            with pe.Fori(0, KC) as n:
                srcs = (hT, oT, hT, olT)
                for m in range(4 * GRP):
                    g, q = m // 4, m % 4
                    if g == 0:
                        pe.wait_ge(ld_wmg[q], 16 * n + 16)
                    if m == 3:
                        pe.wait_ge(lru_done, KC + 1)
                    pe.wait_ge(mg_out if q % 2 else mg_sig, 6 * n + m // 2 + 1)
                    chunk_sum(ps[:, m % 6, 0:GW], lambda k: wmg[q][:, k, :], lambda k: srcs[q][:, k, GC[g]]).then_inc(mg_done, 1)

            def wout(k):
                return wout_lo[:, k, :] if k < KLO else wout_hi[:, k - KLO, :]

            def mix(t, s, n=P):
                pe.wait_ge(mst_ready, t + 1)
                ge(pe, x1_half, t - 1)
                for nn in range(2):
                    ins = chunk_sum(ps[0:n, 2 * s + nn, :], lambda k: mst[:, s, k, 0:n], lambda k: wout(k)[:, nn * 512:(nn + 1) * 512])
                ins.then_inc(mix_done, 1)

            def route(t, s, n=P):
                pe.wait_ge(h2_ready, t + 1)
                ge(pe, h2T_ready, t)
                for k in range(KC):
                    ins = pe.transpose(ps[:, 4 + k // 4, (k % 4) * P:(k % 4) * P + n], h2[0:n, s, k * P:(k + 1) * P], ident[0:n, 0:n])
                ins.then_inc(h2_turned, 1)
                pe.wait_ge(h2T_ready, t + 1)
                ge(pe, lg_kept, t)
                chunk_sum(ps[0:n, 6, 0:NG + NE], lambda k: h2T[:, k, 0:n], lambda k: wr[:, k, :]).then_inc(lg_done, 1)

            pe.wait_ge(ld_wout, 32)
            mix(0, 0)
            q = 0
            for r in range(4):
                for nn in range(2):
                    for n, at in ((P, 0), (NS, P)):
                        ge(pe, spread_kept, q - 3)
                        mm(ps[0:n, 4 + q % 4, :], sel[:, at:at + n], mod[:, r * D + nn * 512:r * D + (nn + 1) * 512], True, True).then_inc(spread_done, 1)
                        q += 1
            pe.wait_ge(spread_kept, 16)
            mix(1, 1)
            pe.wait_ge(ld_route, 80)
            route(0, 0)
            mix(2, 0)
            route(1, 1)
            with pe.Fori(1, 3) as i:
                for s in range(2):
                    mix(2 * i + s + 1, 1 - s)
                    route(2 * i + s, s)
            mix(7, 1)
            route(6, 0)
            mix(8, 0, NS)
            route(7, 1)
            route(8, 0, NS)

            pe.wait_ge(oh_ready, 1)

            def rows(t):
                return P if t < BLKS else NS

            for t in range(TILES + 1):
                out = ps[:, 7, t * NE:(t + 1) * NE]
                for b in range(min(t + 1, TILES)):
                    w = ubf[0:rows(b), 0 if b == t else 1, :]
                    ins = mm(out, w, ohs[0:rows(b), b, :], b == 0, b == min(t, TILES - 1))
            ins.then_inc(rank_done, 1)
            pe.wait_ge(hot_ready, 1)
            for q in range(TK):
                n = rows(q // 2)
                ins = mm(ps[:, 6, 0:2 * MAXB], ohslot[0:n, q, :], rhs2[0:n, q, :, :].rearrange("p a b -> p (a b)"), q == 0, q == TK - 1)
            ins.then_inc(slot_done, 1)

            pe.wait_ge(pairs_ready, 1)
            pairs = pe.value_load(cnt_i[0:1, 0:1], min_val=1, max_val=MAXB // 2)
            for credit in (gate_done, up_done, y_done):
                pe.sem_inc(credit, 2)

            def turn_x(n, s, times):
                pe.wait_ge(xg_ready[s], 16 * times)
                ge(pe, xT_a, n)
                ge(pe, xT_b, n)
                for k in range(KC):
                    ins = pe.transpose(ps[:, k // 4, (k % 4) * P:(k % 4 + 1) * P],
                                       xg[:, s, :].rearrange("r (p k) -> r k p", k=KC)[:, k, :], ident[:, :])
                ins.then_inc(xg_used, 1)

            turn_x(0, 0, 1)
            with pe.Fori(0, pairs) as i:
                for s in range(2):
                    n = 2 * i + s
                    pe.wait_ge(xT_a, n + 1)
                    pe.wait_ge(xT_b, n + 1)
                    for bank, w, ready, done in ((2, wg[s], ld_g[s], gate_done), (3, wu[s], ld_u[s], up_done)):
                        pe.wait_ge(ready, 16 * i + 16)
                        for m in range(FC):
                            ins = chunk_sum(ps[:, bank, m * P:(m + 1) * P], lambda k: w[:, k, m * P:(m + 1) * P], lambda k: xT[:, k, :])
                        ins.then_inc(done, 1)
                    turn_x(n + 1, 1 - s, i + 1 + s)
                    pe.wait_ge(a_ready, n + 1)
                    pe.wait_ge(ld_d[s], 16 * i + 16)
                    for nn, (kept, done) in enumerate(((yk_a, y_half), (yk_b, y_done))):
                        pe.wait_ge(kept, n + 1)
                        for m in range(FC):
                            ins = mm(ps[:, 4 + nn, :], aT[:, m, :], wd[s][:, m, nn * 512:(nn + 1) * 512], m == 0, m == FC - 1)
                        ins.then_inc(done, 1)



HEADS = [8 * (c // 4) + 4 * a + c % 4 for c in range(KC) for a in range(2)]


def layouts(g):
    x = np.concatenate([g["x_prompt"][0], g["x_sample"].reshape(NS, D)])
    chunks = lambda w: np.ascontiguousarray(w.reshape(KC, P, w.shape[1] // P, P).transpose(2, 1, 0, 3))
    by_part = lambda v: v.reshape(KC, P, *v.shape[1:]).swapaxes(0, 1)
    w_in = g["w_in"][0]
    q, k, v, xl, yl, ga, gr = np.split(w_in, np.cumsum([D, KV, KV, D, D, D]), axis=1)
    q = q.reshape(D, 16, HD)[:, HEADS].reshape(D, D)
    w_at = g["w_attn_branch"][0].reshape(16, HD, D)[HEADS].reshape(D, D)
    lg = np.zeros((KC, P, 2, P), np.float32)
    for m, name in enumerate(("w_lru_a", "w_lru_x")):
        w = g[name][0].reshape(KC, 2, HD, HD)
        for a in range(2):
            lg[:, a * HD:(a + 1) * HD, m, a * HD:(a + 1) * HD] = w[:, a]
    vec = [g["b_lru_a"][0], g["b_lru_x"][0], g["lru_lambda"][0], g["b_conv"][0], *g["w_conv"][0]]
    sinks = g["sinks"][0]
    sink_s = np.repeat(np.broadcast_to(sinks.reshape(4, 1, 4), (4, 2, 4)).reshape(-1), NT)
    kc = g["cache_k_win"][0].reshape(NB, P, 2, P)
    return {name: np.ascontiguousarray(t) for name, t in {
        "x": x, "xT": x.T,
        "cT": by_part(np.concatenate([g["c_prompt"], g["c_sample"]]).T),
        "w_ada": g["w_ada"][0], "b_ada": g["b_ada"][0],
        "w_qk": np.concatenate([chunks(k), chunks(q)]), "w_v": v.reshape(KC, P, KV).swapaxes(0, 1),
        "w_xl": chunks(xl), "w_yl": chunks(yl), "w_ga": chunks(ga), "w_gr": chunks(gr),
        "w_at": chunks(w_at), "w_lr": chunks(g["w_lru_branch"][0]), "w_lg": lg, "w_out": g["w_out"][0],
        "lvec": by_part(np.stack(vec, axis=1)),
        "h0": by_part(g["state_h"][0].T), "stc": by_part(g["state_conv"][0].transpose(2, 0, 1)),
        "gpre": by_part(g["g_pre_mix"][0]), "sinks": sinks[HEADS], "sink_s": sink_s[:, None],
        "g_rows": np.concatenate([g["g_post_mix"], g["g_pre_ffn"], g["g_post_ffn"]]),
        "w_r": by_part(np.concatenate([g["w_router_group"][0], g["w_router_expert"][0]], axis=1)),
        "b_r": np.concatenate([g["b_router_group"][0], g["b_router_expert"][0]]),
        "kcT": kc.transpose(3, 2, 0, 1), "v_cache": g["cache_v_win"][0].reshape(NB, P, KV),
        "w_gate": g["w_exp_gate"][0], "w_up": g["w_exp_up"][0], "w_down": g["w_exp_down"][0],
    }.items()}


def constants():
    bf16 = mybir.dt.np(BF16)
    half = HD // 2
    inv = (10000.0 ** (-np.arange(half) / half)).astype(np.float32)
    pos = np.concatenate([np.arange(SEQ), np.tile(PAST + np.arange(NT), NB)]).astype(np.float32)
    ang = (pos[None, :] * inv[:, None]).astype(np.float32)
    m = np.arange(P)
    rot = np.zeros((P, P), np.float32)
    low = m % HD < half
    rot[m[low] + half, m[low]] = -1.0
    rot[m[~low] - half, m[~low]] = 1.0
    q, k = m[:, None], m[None, :]
    out = np.float32(-1e30)
    masks = np.zeros((P, BLKS, 2 * P), np.float32)
    masks[:, :, :P] = np.where(k >= q, 0, out)[:, None, :]
    masks[:, :, P:] = np.where(k <= q, 0, out)[:, None, :]
    masks[:, 0, :P] = out
    t, j = (m % NT)[:, None], np.arange(P + NT)[None, :]
    sel = np.zeros((1 + NB, P + NS), np.float32)
    sel[0, :P] = 1.0
    for b in range(NB):
        sel[1 + b, P + NT * b:P + NT * (b + 1)] = 1.0
    upper = np.ones((P, 2, P), np.float32)
    upper[:, 0] = q < k
    tpid = np.zeros((P, 2, TILES * 2), np.float32)
    tpid[:, 0] = np.arange(TILES * 2) // 2
    tpid[:, 1] = q
    return {
        "ident": np.eye(P, dtype=np.float32), "identb": np.eye(P).astype(bf16), "rot": rot,
        "masks": masks.astype(bf16), "mask_s": np.where((j >= t) & (j <= P + t), 0, out).astype(bf16),
        "sel": sel, "cos": np.tile(np.cos(ang), (4, 1)), "sin": np.tile(np.sin(ang), (4, 1)),
        "halves": np.repeat(np.eye(2, dtype=np.float32), HD, axis=0),
        "iota": np.tile(m.astype(np.float32), (P, 1)), "upper": upper.astype(bf16), "tpid": tpid.astype(bf16),
    }


def outputs(r):
    tail = r["tail"].swapaxes(0, 1).reshape(D, 36)
    kws = r["kws"].transpose(2, 3, 1, 0).reshape(1, NB, P, 4, HD)
    vws = np.concatenate([r["vold"], r["vnew"].reshape(NB, NT, KV)], axis=1).reshape(1, NB, P, 4, HD)
    return (r["y"][:SEQ].reshape(1, SEQ, D), r["y"][SEQ:].reshape(NB, NT, D),
            r["kwp"].transpose(2, 1, 0).reshape(1, 1, P, 4, HD), r["vwp"].reshape(1, 1, P, 4, HD),
            tail[:, 0:3].T.reshape(1, 1, 3, D), tail[:, 3].reshape(1, 1, D),
            kws, vws, tail[:, 12:36].reshape(D, NB, 3).transpose(1, 2, 0)[None], tail[:, 4:12].T[None])


def kernel(x_prompt, x_sample, cache_k_win, cache_v_win, state_conv, state_h, c_prompt, c_sample,
           w_ada, b_ada, g_pre_mix, g_post_mix, g_pre_ffn, g_post_ffn, w_in, sinks,
           w_conv, b_conv, w_lru_a, b_lru_a, w_lru_x, b_lru_x, lru_lambda,
           w_attn_branch, w_lru_branch, w_out, w_router_group, b_router_group,
           w_router_expert, b_router_expert, w_exp_gate, w_exp_up, w_exp_down):
    from concourse import bacc as _bacc
    from concourse.bass_utils import run_bass_kernel_spmd

    given = dict(locals())
    g = {name: np.asarray(v) for name, v in given.items() if hasattr(v, "shape")}
    arrays = layouts(g) | constants()
    shapes = {"y": (TOK, D), "kwp": (P, 2, P), "vwp": (P, KV), "vnew": (NS, KV), "vold": (NB, P - NT, KV),
              "tail": (P, KC, 36), "kws": (P, 2, NB, P)}
    nc = _bacc.Bacc("TRN2", target_bir_lowering=False, num_devices=1)
    I = {n: nc.dram_tensor(n, list(v.shape), mybir.dt.from_np(v.dtype), kind="ExternalInput").ap() for n, v in arrays.items()}
    O = {n: nc.dram_tensor(n, list(s), F32, kind="ExternalOutput").ap() for n, s in shapes.items()}
    build(nc, I, O)
    nc.finalize()
    r = run_bass_kernel_spmd(nc, [arrays], core_ids=[0]).results[0]
    return outputs({n: np.asarray(r[n]).reshape(s) for n, s in shapes.items()})
```

```python
from contextlib import ExitStack

import numpy as np

import concourse.bass as bass
from concourse import mybir
from concourse.alu_op_type import AluOpType as ALU

F32 = mybir.dt.float32
F32R = mybir.dt.float32r
BF16 = mybir.dt.bfloat16
I32 = mybir.dt.int32
U32 = mybir.dt.uint32
ACT = mybir.ActivationFunctionType
AX_X = mybir.AxisListType.X

P = 128
D = 1024
SEQ = 1024
NB, NT = 8, 4
NS = NB * NT
PAST = 4096
TOK = SEQ + NS
KC = D // P
HD = 64
KV = 256
GRP = 3
GW = TOK // GRP
BLKS = SEQ // P
TILES = BLKS + 1
SCALE = 0.125
EPS = 1e-6
NE, NG, EPG = 32, 4, 8
FE = 512
FC = FE // P
A_MAX = 2 * TOK
MAXB = NE + A_MAX // P
MAXB += MAXB % 2
ZB = -(-(MAXB + 2 - NE) // BLKS)
NADA = 6 * D // 512
N_QK = 30
N_PROJ = N_QK + 12 * KC
GELU_C = 0.7978845608028654
GELU_A = 0.044715
DVE_ADDS = 2
XPAD = 3


class Chain:

    def __init__(self, eng, sem):
        self.eng, self.sem, self.base, self.n = eng, sem, 0, 0

    def __call__(self, ins):
        self.n += 1
        ins.then_inc(self.sem, 1)
        self.eng.wait_ge(self.sem, self.base + self.n)

    def enter(self, i, per):
        self.kept, self.per, self.start = self.n, per, self.base
        self.base, self.n = self.base + self.kept + i * per, 0

    def leave(self, trips):
        assert self.n == self.per, (self.n, self.per)
        self.base, self.n = self.start, self.kept + trips * self.per


def build(nc, I, O):
    ctx = ExitStack()
    with ctx:
        base0 = (nc.sbuf_base + 63) // 64 * 64
        room = (nc.sbuf_usable_end - base0) // 4

        def at(name, shape, word, dt=F32):
            words = int(np.prod(shape[1:])) * (2 if dt == BF16 else 4) // 4
            assert word + words <= room, (name, word, words, room)
            return nc.alloc_sbuf_tensor_at(name, list(shape), dt, offset=base0 + 4 * word)

        big = KC * TOK
        hT = at("hT", [P, KC, TOK], 0)
        oT = at("oT", [P, KC, TOK], big)
        olT = at("olT", [P, KC, TOK], 2 * big)

        cur = 3 * big

        def small(name, shape, dt=F32):
            nonlocal cur
            t = at(name, shape, cur, dt)
            cur += (int(np.prod(shape[1:])) * (2 if dt == BF16 else 4) + 31) // 32 * 8
            return t

        ident = small("ident", [P, P])
        identb = small("identb", [P, P], BF16)
        mask_s = small("mask_s", [P, P + NT], BF16)
        sel = small("sel", [1 + NB, P + NS])
        halves = small("halves", [P, 2])
        nsink = small("nsink", [P, 2 * KC])
        nsink_s = small("nsink_s", [P, 1])
        lvec = small("lvec", [P, KC, 8])
        lcur = small("lcur", [P, 8])
        h0 = small("h0", [P, KC, NB])
        stc = small("stc", [P, KC, NB, XPAD])
        tail = small("tail", [P, KC, 36])
        eps = small("eps", [P, 1])
        mx = small("mx", [P, 2, 2])
        ngm = small("ngm", [P, 2, 2])
        skd = small("skd", [P, 2, 2])
        sme = small("sme", [P, 2, 2])
        ske = small("ske", [P, 2, 2])
        rcp = small("rcp", [P, 2, 2])
        spt = small("spt", [P, 5, KC])
        sst = small("sst", [P, 2, 4])
        mod = at("mod", [1 + NB, 4 * D], cur)
        cur += 4 * D
        zone_k = cur
        kT = at("kT", [P, 2, P + TOK], zone_k)
        vtok = at("vtok", [P, TILES + 1, KV], zone_k + 2 * (P + TOK))
        wA = at("wA", [P, KC, P], zone_k + 2 * (P + TOK) + (TILES + 1) * KV)
        w0 = zone_k + 2 * (P + TOK) + (TILES + 1) * KV + KC * P
        wB = at("wB", [P, KC, P], w0)
        wlg = at("wlg", [P, 2, P], w0 + KC * P)
        tmp0 = w0 + KC * P + 2 * P
        merged = at("merged", [P, KC, TOK], zone_k)
        after_merged = zone_k + big
        assert after_merged <= room

        wada = [at(f"wada{i}", [P, KC, 512], w) for i, w in
                enumerate((big, big + 4096, 2 * big, 2 * big + 4096))]
        cT = at("cT", [P, KC, 1 + NB], tmp0)
        cE = at("cE", [P, KC, 1 + NB], tmp0 + 80)
        gpre = at("gpre", [P, KC], tmp0 + 160)
        shT = at("shT", [P, KC, 1 + NB], tmp0 + 176)
        scT = at("scT", [P, KC, 1 + NB], tmp0 + 256)
        modh = at("modh", [1 + NB, 2 * D], tmp0 + 336)
        bada = at("bada", [1 + NB, 6 * D], tmp0 + 336 + 2 * D)
        sq = at("sq", [P, 2, TOK], zone_k)
        rms_bc = at("rms_bc", [P, TOK], zone_k + 2 * TOK)
        hs_tmp = at("hs_tmp", [P, KC, NS], zone_k + 3 * TOK)
        ones = at("ones", [P, P], zone_k + 3 * TOK + KC * NS)
        ssum = at("ssum", [P, TOK], zone_k + 3 * TOK + KC * NS + P)

        cosT = at("cosT", [P, TOK], tmp0)
        sinT = at("sinT", [P, TOK], tmp0 + TOK)
        rtmp = at("rtmp", [P, TOK], tmp0 + 2 * TOK)
        wV = at("wV", [P, KC, KV], tmp0 + 3 * TOK)
        sa = tmp0 + 3 * TOK + KC * KV
        kcx = at("kcx", [P, 2, NB, P + NT], sa)
        vc = at("vc", [P, NB, KV], sa + 2 * NB * (P + NT))
        turned = at("turned", [P, TOK], sa + 2 * NB * (P + NT) + NB * KV)
        qs = at("qs", [P, 2, NB, 32], tmp0)
        pS = at("pS", [P, NB, P + NT], tmp0 + 512)
        pZ = at("pZ", [P, NB * 36], tmp0 + 512 + 1056)
        pTs = at("pTs", [P, NB, P], tmp0 + 512 + 1056 + 288)
        pTn = at("pTn", [NS, NB, P], tmp0 + 512 + 1056 + 288 + 1024)
        ss0 = tmp0 + 512 + 1056 + 288 + 2048
        mxs, ngs, sks, sms, skes, rcs = [at(n, [P, NB], ss0 + 8 * i) for i, n in
                                         enumerate(("mxs", "ngs", "sks", "sms", "skes", "rcs"))]
        xlp = at("xlp", [P, XPAD + SEQ], tmp0)
        xls = at("xls", [P, NB, XPAD + NT], tmp0 + 1032)
        l1 = tmp0 + 1032 + 56
        yl, xc, gA, gB, gC = [at(n, [P, TOK], l1 + i * TOK) for i, n in
                              enumerate(("yl", "xc", "gA", "gB", "gC"))]
        t8 = at("t8", [P, NB], l1 + 5 * TOK)
        a0 = l1 + 5 * TOK + 8
        qst = at("qst", [P, 4, 2, P], a0)
        vst = at("vst", [P, 4, 2, P], a0 + 1024)
        pp = at("pp", [P, 2, 2, 2 * P], a0 + 2048)
        pT = at("pT", [P, 2, 4, P], a0 + 2048 + 1024)
        masks = at("masks", [P, BLKS, 2 * P], a0 + 2048 + 2048, BF16)
        zeros = at("zeros", [P, D], a0 + 2048 + 2048 + 1024)
        wmg = [at(f"wmg{i}", [P, KC, P], a0 + i * KC * P) for i in range(4)]
        KLO = 5
        wout_lo = at("wout_lo", [P, KLO, D], after_merged)
        assert after_merged + KLO * D <= a0
        wout_hi = at("wout_hi", [P, KC - KLO, D], a0 + 4 * KC * P)
        sg0 = a0 + 4 * KC * P + (KC - KLO) * D
        sga, sgr, mtmp = [at(n, [P, GW], sg0 + i * GW) for i, n in enumerate(("sga", "sgr", "mtmp"))]
        x1 = at("x1", [P, TILES, D], 0)
        bc0 = TILES * D
        G2p, G2s = at("G2p", [P, D], bc0), at("G2s", [NS, D], bc0 + D)
        G1p, G1s = at("G1p", [P, D], bc0 + 2 * D), at("G1s", [NS, D], bc0 + 3 * D)
        A2p, A2s = at("A2p", [P, D], bc0 + 4 * D), at("A2s", [NS, D], bc0 + 5 * D)
        B2p, B2s = at("B2p", [P, D], bc0 + 6 * D), at("B2s", [NS, D], bc0 + 7 * D)
        t4 = bc0 + 8 * D
        xin = at("xin", [P, 2, D], t4)
        h2 = at("h2", [P, 2, D], t4 + 2 * D)
        h2T = at("h2T", [P, KC, P], t4 + 4 * D)
        mst = at("mst", [P, 2, KC, P], t4 + 5 * D)
        junk = at("junk", [P, D], t4 + 7 * D, BF16)
        rcur = cur - 4 * D

        def keep(name, shape, dt=F32):
            nonlocal rcur
            t = at(name, shape, rcur, dt)
            rcur += (int(np.prod(shape[1:])) * (2 if dt == BF16 else 4) + 31) // 32 * 8
            return t

        EW = KC * FE * 2 + FC * D
        ew0 = room // 8 * 8 - 2 * EW
        wr = keep("wr", [P, KC, NG + NE])
        lg = keep("lg", [P, TILES, NG + NE])
        brt = keep("brt", [P, NG + NE])
        slot_tok = keep("slot_tok", [P, MAXB + 2], I32)
        pos_i = keep("pos_i", [P, TILES * 2], I32)
        wts = keep("wts", [P, TILES, 2])
        blk_i = keep("blk_i", [P, MAXB + 2], I32)
        cnt_i = keep("cnt_i", [P, 2], I32)
        idx = keep("idx", [P, 4], I32)
        fst = keep("fst", [P, TILES, 2])
        tpid = keep("tpid", [P, 2, TILES * 2], BF16)
        assert rcur <= ew0, (rcur, ew0)
        wg = [at(f"wg{s}", [P, KC, FE], ew0 + s * EW) for s in range(2)]
        wu = [at(f"wu{s}", [P, KC, FE], ew0 + s * EW + KC * FE) for s in range(2)]
        wd = [at(f"wd{s}", [P, FC, D], ew0 + s * EW + 2 * KC * FE) for s in range(2)]
        xg = at("xg", [P, 2, D], t4)
        xT = [at("xT0", [P, KC, P], t4 + 2 * D), at("xT1", [P, KC, P], bc0 + 6 * D)]
        wd_up = at("wd_up", [P, FC, D], bc0 + 2 * D, F32R)
        a_up = at("a_up", [P, FC, P], t4 + 7 * D, F32R)
        wd_low = [at(f"wd_low{s}", [P, FC, D], ew0 + s * EW + 2 * KC * FE, F32R) for s in range(2)]
        sgm = at("sgm", [P, FC, P], t4 + 3 * D)
        aT = at("aT", [P, FC, P], t4 + 3 * D + FC * P)
        a_low = at("a_low", [P, FC, P], t4 + 3 * D + FC * P, F32R)
        ysb = at("ysb", [P, 2, D], t4 + 4 * D)
        fy = at("fy", [P, TILES, 2, D], ew0)
        fjunk = at("fjunk", [P, D], t4 + 6 * D, BF16)
        rt = bc0 + 2 * D

        def rtm(name, shape, dt=F32):
            nonlocal rt
            t = at(name, shape, rt, dt)
            rt += (int(np.prod(shape[1:])) * (2 if dt == BF16 else 4) + 31) // 32 * 8
            assert rt <= t4
            return t

        TK = TILES * 2
        lg8 = rtm("lg8", [P, TILES, 8])
        gm8 = rtm("gm8", [P, TILES, 8])
        gi8 = rtm("gi8", [P, TILES, 8], U32)
        gix = rtm("gix", [P, TILES])
        ohg = rtm("ohg", [P, TILES, NG])
        prd = rtm("prd", [P, TILES, EPG, NG])
        ing = rtm("ing", [P, TILES, EPG])
        em8 = rtm("em8", [P, TILES, 8])
        ei8 = rtm("ei8", [P, TILES, 8], U32)
        eix = rtm("eix", [P, TILES, 2])
        oh = rtm("oh", [P, TILES, 2, NE], BF16)
        ohs = rtm("ohs", [P, TILES, NE], BF16)
        gex = rtm("gex", [P, TILES, NG])
        gsm = rtm("gsm", [P, TILES])
        e1 = rtm("e1", [P, TILES])
        cmp9 = rtm("cmp9", [P, NE, TILES])
        nbk = rtm("nbk", [P, NE])
        incl = rtm("incl", [P, NE])
        bas = rtm("bas", [P, NE])
        cntf = rtm("cntf", [P, NE])
        qrk = rtm("qrk", [P, TILES, NE])
        mq = rtm("mq", [P, TILES, 2, NE])
        pos_f = rtm("pos_f", [P, TK])
        sl_i = rtm("sl_i", [P, 2, TK], I32)
        sl_f = rtm("sl_f", [P, 2, TK])
        ohslot = rtm("ohslot", [P, TK, P], BF16)
        ohblk = rtm("ohblk", [P, TK, MAXB], BF16)
        rhs2 = rtm("rhs2", [P, TK, 2, MAXB], BF16)
        slf = rtm("slf", [P, MAXB])
        cmpb = rtm("cmpb", [P, MAXB - NE, NE])
        iot = at("iot", [P, P], t4 + 7 * D + 512)
        ubf = at("ubf", [P, 2, P], t4 + 7 * D + 512 + P, BF16)
        assert t4 + 7 * D + 512 + 2 * P <= 3 * big
        ps = ctx.enter_context(nc.psum_tensor("ps", [P, 8, 512], F32))
        h2_dram = nc.dram_tensor("h2_dram", [TOK, D], F32)
        y_dram = nc.dram_tensor("y_dram", [(MAXB + 2) * P, D], F32)

        def sem(name):
            return ctx.enter_context(nc.semaphore(name))

        ld_c, ld_bada, ld_small = sem("ld_c"), sem("ld_bada"), sem("ld_small")
        ld_wada = [sem(f"ld_wada{i}") for i in range(4)]
        ld_x = [sem(f"ld_x{i}") for i in range(4)]
        ld_rope, ld_kc, ld_wV = sem("ld_rope"), sem("ld_kc"), sem("ld_wV")
        ld_wA, ld_wB, ld_wlg = sem("ld_wA"), sem("ld_wB"), sem("ld_wlg")
        ld_wmg = [sem(f"ld_wmg{i}") for i in range(4)]
        ld_wout, ld_spread, ld_route = sem("ld_wout"), sem("ld_spread"), sem("ld_route")
        ld_xin = [sem(f"ld_xin{i}") for i in range(2)]
        ch_dve, ch_act = sem("ch_dve"), sem("ch_act")
        ch_unit, ch_lru, ch_tok, ch_fin = sem("ch_unit"), sem("ch_lru"), sem("ch_tok"), sem("ch_fin")
        ones_set, c_sig, c_silu = sem("ones_set"), sem("c_sig"), sem("c_silu")
        lam_abs, lam_exp = sem("lam_abs"), sem("lam_exp")
        ada_done, ada_kept = sem("ada_done"), sem("ada_kept")
        sq_ready, sq_used, ssq_done = sem("sq_ready"), sem("sq_used"), sem("ssq_done")
        rms_root, modT_done = sem("rms_root"), sem("modT_done")
        h_scaled, h_ready, hs_ready = sem("h_scaled"), sem("h_ready"), sem("hs_ready")
        pads_set = sem("pads_set")
        proj_done, proj_kept = sem("proj_done"), sem("proj_kept")
        v_done, v_kept = sem("v_done"), sem("v_kept")
        swapped, rope_done = sem("swapped"), sem("rope_done")
        s_staged, s_scores, s_negmax, s_exp = sem("s_staged"), sem("s_scores"), sem("s_negmax"), sem("s_exp")
        s_norm, s_turned, s_kept, s_pv, s_out = sem("s_norm"), sem("s_turned"), sem("s_kept"), sem("s_pv"), sem("s_out")
        u_staged, u_scores, u_negmax, u_exp = sem("u_staged"), sem("u_scores"), sem("u_negmax"), sem("u_exp")
        u_norm, u_turned, u_kept, u_pv, u_out = sem("u_norm"), sem("u_turned"), sem("u_kept"), sem("u_pv"), sem("u_out")
        xc_ready, decay, gap, gap_root = sem("xc_ready"), sem("decay"), sem("gap"), sem("gap_root")
        y_sq, y_arg, y_tanh, lru_done = sem("y_sq"), sem("y_arg"), sem("y_tanh"), sem("lru_done")
        lru_in = sem("lru_in")
        lru_scan = sem("lru_scan")
        mg_done, mg_sig, mg_out = sem("mg_done"), sem("mg_sig"), sem("mg_out")
        mst_ready, mix_done, mix_sq, x1_half, x1_ready = sem("mst_ready"), sem("mix_done"), sem("mix_sq"), sem("x1_half"), sem("x1_ready")
        x1_sq, h2_ready, st_h2, h2_turned, h2T_ready = sem("x1_sq"), sem("h2_ready"), [sem("st_h2a"), sem("st_h2b")], sem("h2_turned"), sem("h2T_ready")
        lg_done, lg_kept, spread_done, spread_kept = sem("lg_done"), sem("lg_kept"), sem("spread_done"), sem("spread_kept")
        oh_ready, rank_done, rt_sub, rt_exp, pairs_ready = sem("oh_ready"), sem("rank_done"), sem("rt_sub"), sem("rt_exp"), sem("pairs_ready")
        hot_ready, slot_done, slots_ready = sem("hot_ready"), sem("slot_done"), sem("slots_ready")
        blocks_ready = sem("blocks_ready")
        ld_g, ld_u, ld_d = [[sem(f"ld_{n}{s}") for s in range(2)] for n in "gud"]
        idx_ready, xg_ready, xg_used = sem("idx_ready"), [sem("xg_ready0"), sem("xg_ready1")], sem("xg_used")
        xT_a, xT_b = sem("xT_a"), sem("xT_b")
        gate_done, up_done, sg_ready, a_ready = sem("gate_done"), sem("up_done"), sem("sg_ready"), sem("a_ready")
        y_half, y_done, yk_a, yk_b = sem("y_half"), sem("y_done"), sem("yk_a"), sem("yk_b")
        st_y = [sem("st_y0"), sem("st_y1")]
        ch_moe, ch_fin2 = sem("ch_moe"), sem("ch_fin2")
        ch_split, wd_split = sem("ch_split"), sem("wd_split")
        idx_seen = sem("idx_seen")
        ld_f = [sem(f"ld_f{t}") for t in range(TILES)]
        f_first, f_sum, f_sq, f_norm, yo_ready = sem("f_first"), sem("f_sum"), sem("f_sq"), sem("f_norm"), sem("yo_ready")
        yo_last = sem("yo_last")
        st_out = sem("st_out")
        st_side, st_kws, st_tail = sem("st_side"), sem("st_kws"), sem("st_tail")
        zeros_set, st_zeros = sem("zeros_set"), sem("st_zeros")

        block = ctx.enter_context(nc.Block())

        def bc(ap, shape):
            return ap.broadcast_to(list(shape))

        def grp(t):
            return t.rearrange("p (g t) -> p g t", g=GRP)

        def ge(eng, s, v):
            if not (isinstance(v, int) and v <= 0):
                eng.wait_ge(s, v)

        def outs_at(s):
            return ((0,), (1,), (2,), (3,), (), (4,), (), (5,), (6, 7, 8), (9, 10, 11))[s]

        GC = [slice(g * GW, (g + 1) * GW) for g in range(GRP)]

        def number(i, o):
            return N_QK + 12 * i - 3 + o + (3 if isinstance(i, int) and i == 0 and o < 3 else 0)

        @block.sync
        def _(sp):
            sp.dma_start(cT[:, :, :], I["cT"]).then_inc(ld_c, 16)
            for n in range(NADA):
                if n >= 4:
                    sp.wait_ge(ada_done, n - 3)
                sp.dma_start(wada[n % 4][:, :, :],
                             I["w_ada"][:, n * 512:(n + 1) * 512].rearrange("(k p) n -> p k n", p=P)
                             ).then_inc(ld_wada[n % 4], 16)
                if 4 <= n < 8:
                    k = 2 * (n - 4)
                    sp.dma_start(hT[:, k:k + 2, :],
                                 I["xT"][k * P:(k + 2) * P, :].rearrange("(k p) t -> p k t", p=P)
                                 ).then_inc(ld_x[n - 4], 16)
            sp.dma_start(wA[:, :, :], I["w_qk"][0]).then_inc(ld_wA, 16)
            sp.dma_start(wB[:, :, :], I["w_qk"][1]).then_inc(ld_wB, 16)
            sp.wait_ge(ada_kept, NADA)
            sp.wait_ge(h_ready, KC)
            sp.wait_ge(hs_ready, 1)
            sp.dma_start(wV[:, :, :], I["w_v"]).then_inc(ld_wV, 16)
            sp.dma_start(cosT[:, :], I["cos"]).then_inc(ld_rope, 16)
            sp.dma_start(sinT[:, :], I["sin"]).then_inc(ld_rope, 16)
            for p in range(2):
                sp.dma_start(kcx[:, p, :, 0:P], I["kcT"][:, p]).then_inc(ld_kc, 16)
            sp.dma_start(vc[:, :, :], I["v_cache"].rearrange("b k n -> k b n")).then_inc(ld_kc, 16)
            with sp.Fori(0, 4) as i:
                sp.wait_ge(proj_done, 6 * i + 3)
                sp.dma_start(wA[:, :, :], I["w_qk"][bass.ds(2 * i + 2, 1)].rearrange("a p k m -> p (a k) m")).then_inc(ld_wA, 16)
                sp.wait_ge(proj_done, 6 * i + 6)
                sp.dma_start(wB[:, :, :], I["w_qk"][bass.ds(2 * i + 3, 1)].rearrange("a p k m -> p (a k) m")).then_inc(ld_wB, 16)
            sp.wait_ge(proj_done, N_QK - 3)
            sp.dma_start(wA[:, :, :], I["w_xl"][0]).then_inc(ld_wA, 16)
            sp.wait_ge(proj_done, N_QK)
            sp.dma_start(wB[:, :, :], I["w_yl"][0]).then_inc(ld_wB, 16)
            sp.dma_start(wlg[:, :, :], I["w_lg"][0]).then_inc(ld_wlg, 16)

            def store_zeros(i):
                to = MAXB + 2 - ZB * BLKS + ZB * i
                sp.dma_start(y_dram[bass.ds(to * P, ZB * P), :].rearrange("(b p) n -> p b n", p=P),
                             bc(zeros[:, :].unsqueeze(1), (P, ZB, D))).then_inc(st_zeros, 16)

            def round_weights(i):
                nxt = lambda name: I[name][bass.ds(i, 1)].rearrange("a p k m -> p (a k) m")
                sp.wait_ge(proj_done, number(i - 1, 2) + 1)
                sp.dma_start(wA[:, :, :], nxt("w_xl")).then_inc(ld_wA, 16)
                sp.wait_ge(proj_done, number(i - 1, 11) + 1)
                sp.dma_start(wlg[:, :, :], nxt("w_lg")).then_inc(ld_wlg, 16)
                sp.wait_ge(proj_done, number(i, 5) + 1)
                sp.dma_start(wB[:, :, :], nxt("w_yl")).then_inc(ld_wB, 16)
                store_zeros(i)

            sp.wait_ge(zeros_set, 1)
            store_zeros(0)
            round_weights(1)
            with sp.Fori(2, KC) as i:
                round_weights(i)
            sp.wait_ge(u_out, 4 + KC * BLKS)
            names = ("w_ga", "w_at", "w_gr", "w_lr")
            for q in range(4):
                sp.dma_start(wmg[q][:, :, :], I[names[q]][0]).then_inc(ld_wmg[q], 16)
            w_out = I["w_out"].rearrange("(k p) n -> p k n", p=P)
            sp.wait_ge(st_zeros, 16 * BLKS)
            sp.dma_start(wout_hi[:, :, :], w_out[:, KLO:, :]).then_inc(ld_wout, 16)
            sp.wait_ge(lru_done, KC + 1)
            sp.dma_start(wout_lo[:, :, :], w_out[:, 0:KLO, :]).then_inc(ld_wout, 16)
            with sp.Fori(1, KC) as i:
                for q in range(4):
                    sp.wait_ge(mg_done, 12 * i - 3 + q)
                    sp.dma_start(wmg[q][:, :, :], I[names[q]][bass.ds(i, 1)].rearrange("a p k m -> p (a k) m")).then_inc(ld_wmg[q], 16)
            sp.wait_ge(mg_done, 4 * GRP * KC)
            for row, (tp, ts) in enumerate(((G1p, G1s), (A2p, A2s), (G2p, G2s))):
                sp.dma_start(tp[:, :], I["g_rows"][row].partition_broadcast(P)).then_inc(ld_spread, 16)
                sp.dma_start(ts[:, :], I["g_rows"][row].partition_broadcast(NS)).then_inc(ld_spread, 16)
            for t in range(2):
                sp.dma_start(xin[:, t, :], I["x"][t * P:(t + 1) * P, :]).then_inc(ld_xin[t], 16)
            sp.dma_start(iot[:, :], I["iota"]).then_inc(ld_route, 16)
            sp.dma_start(ubf[:, :, :], I["upper"]).then_inc(ld_route, 16)
            sp.wait_ge(spread_done, 16)
            sp.dma_start(wr[:, :, :], I["w_r"]).then_inc(ld_route, 16)
            sp.dma_start(brt[:, :], I["b_r"].partition_broadcast(P)).then_inc(ld_route, 16)
            sp.dma_start(tpid[:, :, :], I["tpid"]).then_inc(ld_route, 16)

            def h2_store(t, s, n=P):
                sp.wait_ge(h2_ready, t + 1)
                sp.dma_start(h2_dram[bass.ds(t * P, n), :], h2[0:n, s, :]).then_inc(st_h2[s], 16)

            with sp.Fori(0, 3) as i:
                for s in range(2):
                    t = 2 * i + s
                    h2_store(t, s)
                    sp.wait_ge(x1_ready, t + 1)
                    sp.dma_start(xin[:, s, :], I["x"][bass.ds(t * P + 2 * P, P), :]).then_inc(ld_xin[s], 16)
            h2_store(6, 0)
            sp.wait_ge(x1_ready, 7)
            sp.dma_start(xin[0:NS, 0, :], I["x"][SEQ:TOK, :]).then_inc(ld_xin[0], 16)
            h2_store(7, 1)
            h2_store(8, 0, NS)

            def expert(s, e, ready, gathered=None):
                for w, name, ld, done, dims in ((wg, "w_gate", ld_g, gate_done, "a (p k) n -> p (a k) n"),
                                                (wu, "w_up", ld_u, up_done, "a (p k) n -> p (a k) n"),
                                                (wd, "w_down", ld_d, y_done, "a (k p) n -> p (a k) n")):
                    if ready is not None:
                        sp.wait_ge(done, ready)
                    sp.dma_start(w[s][:, :, :], I[name][bass.ds(e, 1)].rearrange(dims, k=w[s].shape[1])).then_inc(ld[s], 16)
                    if gathered is not None and w is wg:
                        sp.wait_ge(gathered, 16)

            sp.wait_ge(mix_done, TILES)
            expert(0, 0, None)
            expert(1, 1, None, xg_ready[0])
            sp.wait_ge(pairs_ready, 1)
            more = sp.value_load(cnt_i[0:1, 0:1], min_val=NE // 2 - 1, max_val=MAXB // 2 - 1)
            sp.wait_ge(blocks_ready, 1)
            with sp.Fori(1, more + 1) as i:
                for s in range(2):
                    e = sp.value_load(blk_i[0:1, bass.ds(2 * i + s, 1)], min_val=0, max_val=NE - 1)
                    expert(s, e, 2 * i + s + 1)

            for t in range(TILES):
                n = P if t < BLKS else NS
                if t < TILES - DVE_ADDS:
                    sp.wait_ge(yo_ready, t + 1)
                else:
                    sp.wait_ge(yo_last, t + 1 - (TILES - DVE_ADDS))
                sp.dma_start(O["y"][t * P:t * P + n, :], fy[0:n, t, 1, :]).then_inc(st_out, 16)
            sp.wait_ge(st_out, 16 * TILES)
            sp.wait_ge(st_side, 16 * 4)
            sp.wait_ge(st_tail, 16)
            sp.wait_ge(st_kws, 32)

        @block.gpsimd
        def _(pool):
            pool.memset(ones[:, :], 1.0).then_inc(ones_set, 1)
            pool.memset(eps[:, :], EPS).then_inc(ones_set, 1)
            pool.memset(zeros[:, :], 0.0).then_inc(zeros_set, 1)
            pool.wait_ge(h_ready, KC)
            pool.wait_ge(hs_ready, 1)
            pool.memset(kT[:, :, 0:P], 0.0).then_inc(pads_set, 1)
            pool.memset(vtok[:, 0, :], 0.0).then_inc(pads_set, 1)
            pool.wait_ge(rope_done, 10)
            pool.wait_ge(v_kept, TILES)
            pool.wait_ge(s_out, 1)
            pool.wait_ge(st_kws, 32)
            pool.wait_ge(ld_small, 12 * 16)
            pool.sem_inc(u_out, 4)
            with pool.Fori(0, BLKS) as i:
                for u in range(KC):
                    pool.wait_ge(u_out, 8 * i + u + 1)
                    pool.tensor_tensor(qst[:, u % 4, :, :], bc(oT[:, u, bass.ds(i * P, P)].unsqueeze(1), (P, 2, P)),
                                       bc(halves[:, :].unsqueeze(2), (P, 2, P)), ALU.mult).then_inc(u_staged, 1)
                    lo = (u // 4) * P
                    pool.tensor_copy(vst[:, u % 4, :, :], vtok[:, bass.ds(i, 2), lo:lo + P]).then_inc(u_staged, 1)

            pool.wait_ge(slots_ready, 1)
            pool.wait_ge(st_h2[0], 16 * 5)
            pool.wait_ge(st_h2[1], 16 * 4)
            more = pool.value_load(cnt_i[0:1, 0:1], min_val=NE // 2 - 1, max_val=MAXB // 2 - 1)
            pool.sem_inc(xg_used, 1)

            def gather(j, n, s):
                if not isinstance(n, int):
                    pool.wait_ge(xg_used, n - 1)
                pool.tensor_copy(idx[:, s:s + 1], slot_tok[:, bass.ds(j, 1)]).then_inc(idx_ready, 1)
                pool.wait_ge(idx_ready, n)
                pool.sem_inc(idx_seen, 1)
                pool.indirect_dma_start(xg[:, s, :], None, h2_dram[:, :],
                                        bass.IndirectOffsetOnAxis(idx[:, s:s + 1], 0)).then_inc(xg_ready[s], 16)

            gather(0, 1, 0)
            with pool.Fori(0, more + 1) as i:
                gather(2 * i + 1, 2 * i + 2, 1)
                gather(2 * i + 2, 2 * i + 3, 0)
            pool.wait_ge(st_y[0], more * 16 + 32)
            pool.wait_ge(st_y[1], more * 16 + 32)
            pool.wait_ge(xg_ready[0], more * 16 + 32)
            pool.wait_ge(y_done, more * 2 + 4)
            pool.sem_inc(idx_seen, 1)
            for t in range(TILES):
                n = P if t < BLKS else NS
                for k in range(2):
                    pool.indirect_dma_start(fy[0:n, t, k, :], None, y_dram[:, :],
                                            bass.IndirectOffsetOnAxis(pos_i[0:n, 2 * t + k:2 * t + k + 1], 0)).then_inc(ld_f[t], 16)
            for t in range(TILES - DVE_ADDS):
                n = P
                pool.wait_ge(f_norm, t + 1)
                pool.tensor_tensor(fy[0:n, t, 1, :], fy[0:n, t, 0, :], x1[0:n, t, :], ALU.add).then_inc(yo_ready, 1)

        @block.scalar
        def _(act):
            act.dma_start(bada[:, :], I["b_ada"].partition_broadcast(1 + NB)).then_inc(ld_bada, 16)
            for t, name in ((ident, "ident"), (identb, "identb"), (masks, "masks"), (halves, "halves"), (mask_s, "mask_s"), (sel, "sel"), (nsink_s, "sink_s"),
                            (lvec, "lvec"), (h0, "h0"), (stc, "stc"), (gpre, "gpre")):
                act.dma_start(t.ap(), I[name]).then_inc(ld_small, 16)
            act.dma_start(nsink[:, :], I["sinks"].partition_broadcast(P)).then_inc(ld_small, 16)
            act.wait_ge(ld_c, 16)
            act.activation(cE[:, :, :], cT[:, :, :], ACT.Sigmoid).then_inc(c_sig, 1)
            act.wait_ge(lam_abs, 1)
            act.activation(spt[:, 1, :], spt[:, 0, :], ACT.Exp, scale=-1.0).then_inc(lam_exp, 1)
            for k in range(KC):
                act.wait_ge(ld_x[k // 2], 16)
                ge(act, sq_used, k - 2)
                dst = ssum[:, :] if k == 0 else sq[:, k % 2, :]
                act.activation(dst, hT[:, k, :], ACT.Square).then_inc(sq_ready, 1)
            act.wait_ge(ssq_done, 1)
            act.wait_ge(ones_set, 2)
            act.activation(grp(rms_bc[:, :]), ps[:, 0:GRP, 0:GW], ACT.Sqrt, bias=eps[:, :], scale=1.0 / D).then_inc(rms_root, 1)
            for k in range(KC):
                act.wait_ge(h_scaled, k + 1)
                act.activation(hT[:, k, 0:SEQ], hT[:, k, 0:SEQ], ACT.Identity, bias=shT[:, k, 0:1]).then_inc(h_ready, 1)

            act.wait_ge(pads_set, 2)

            def keep(n, dst, bank):
                act.wait_ge(proj_done, n + 1)
                act.activation(dst, ps[:, bank, 0:GW], ACT.Copy).then_inc(proj_kept, 1)

            def swap(n, src):
                act.wait_ge(proj_kept, 3 * n + 3)
                if isinstance(n, int) and n == 0:
                    act.wait_ge(ada_kept, NADA)
                    act.wait_ge(hs_ready, 1)
                else:
                    act.wait_ge(rope_done, n)
                for q in range(4):
                    to, of = slice(32 * q, 32 * q + 32), slice(32 * (q ^ 1), 32 * (q ^ 1) + 32)
                    ins = act.activation(turned[to, :], src[of], ACT.Copy)
                ins.then_inc(swapped, 1)

            for p in range(2):
                for g in range(GRP):
                    keep(3 * p + g, kT[:, p, P + g * GW:P + (g + 1) * GW], g)
                swap(p, kT[:, p, P:])
            for t in range(TILES):
                n = P if t < BLKS else NS
                act.wait_ge(v_done, t + 1)
                act.activation(vtok[0:n, t + 1, :], ps[0:n, 6 + t % 2, 0:KV], ACT.Copy).then_inc(v_kept, 1)
            act.wait_ge(v_kept, TILES)
            act.dma_start(O["vwp"], vtok[:, BLKS, :]).then_inc(st_side, 16)
            act.dma_start(O["vnew"], vtok[0:NS, TILES, :]).then_inc(st_side, 16)
            act.dma_start(O["vold"], I["v_cache"][:, NT:P, :]).then_inc(st_side, 16)
            act.wait_ge(rope_done, 2)
            act.dma_start(O["kwp"], kT[:, :, SEQ:SEQ + P]).then_inc(st_side, 16)
            with act.Fori(0, 4) as i:
                for q in range(2):
                    for g in range(GRP):
                        keep(6 * i + 6 + 3 * q + g, oT[:, 2 * i + q, GC[g]], g)
                    swap(2 * i + 2 + q, oT[:, bass.ds(2 * i + q, 1), :].rearrange("p a t -> p (a t)"))

            act.wait_ge(s_negmax, 1)
            for b in range(NB):
                act.activation(pS[:, b, :], ps[:, 3 + b // 3, (b % 3) * (P + NT):(b % 3 + 1) * (P + NT)], ACT.Exp,
                               bias=ngs[:, b:b + 1], scale=SCALE, accum_out=sms[:, b:b + 1])
            act.activation(skes[:, :], sks[:, :], ACT.Exp).then_inc(s_exp, 1)
            for hf in range(2):
                act.wait_ge(s_turned, 2 * hf + 1)
                act.activation(pTs[:, 4 * hf:4 * hf + 4, :], ps[:, 6 + hf, :].rearrange("p (b r) -> p b r", b=4), ACT.Copy).then_inc(s_kept, 1)
                act.wait_ge(s_turned, 2 * hf + 2)
                act.activation(pTn[:, 4 * hf:4 * hf + 4, :], ps[0:NS, 3 + hf, :].rearrange("p (b r) -> p b r", b=4), ACT.Copy).then_inc(s_kept, 1)
            act.wait_ge(s_staged, 2)
            for p in range(2):
                act.dma_start(O["kws"][:, p], kcx[:, p, :, NT:P + NT]).then_inc(st_kws, 16)

            act.wait_ge(s_out, 1)
            act.wait_ge(st_kws, 32)
            act.sem_inc(u_exp, 2)

            def keep_outs(i, s):
                if s == 0:
                    act.wait_ge(xc_ready, i + 1)
                if s == 3:
                    act.wait_ge(lru_done, i)
                if s == KC and not (isinstance(i, int) and i == 0):
                    act.wait_ge(lru_in, i)
                for o in outs_at(s):
                    act.wait_ge(proj_done, number(i, o) + 1)
                    src = ps[:, o % 3, 0:GW]
                    g = o % 3
                    if o < 3 and g < 2:
                        act.activation(xlp[:, XPAD + g * GW:XPAD + (g + 1) * GW], src, ACT.Copy).then_inc(proj_kept, 1)
                    elif o < 3:
                        act.activation(xlp[:, XPAD + g * GW:], ps[:, o % 3, 0:GW - NS], ACT.Copy)
                        act.activation(xls[:, :, XPAD:], ps[:, o % 3, GW - NS:GW].rearrange("p (b t) -> p b t", b=NB), ACT.Copy).then_inc(proj_kept, 1)
                    elif o < 6:
                        act.activation(yl[:, GC[g]], src, ACT.Copy).then_inc(proj_kept, 1)
                    else:
                        dst, bias = ((gA, 0), (gB, 1))[o % 2]
                        act.activation(dst[:, GC[(o - 6) // 2]], src, ACT.Sigmoid, bias=lcur[:, bias:bias + 1]).then_inc(proj_kept, 1)

            def lru_step(i, s):
                if s == 1:
                    act.wait_ge(proj_kept, number(i - 1, 11) + 1)
                    act.wait_ge(lru_done, i)
                    act.activation(gC[:, :], gA[:, :], ACT.Exp, scale=lcur[:, 2:3])
                    act.activation(gA[:, :], gA[:, :], ACT.Tanh, scale=lcur[:, 2:3]).then_inc(decay, 1)
                if s == 2:
                    act.wait_ge(gap, i)
                    act.activation(xc[:, :], xc[:, :], ACT.Sqrt, scale=-1.0).then_inc(gap_root, 1)
                if s == 7:
                    act.wait_ge(lru_scan, i)
                    act.activation(gC[:, :], yl[:, :], ACT.Square).then_inc(y_sq, 1)
                if s == 8:
                    act.wait_ge(y_arg, i)
                    act.activation(gC[:, :], gC[:, :], ACT.Tanh, scale=GELU_C).then_inc(y_tanh, 1)

            def act_round(i, first=False):
                for s in range(KC + 2):
                    if s < KC:
                        act.wait_ge(u_negmax, 8 * i + s + 1)
                        act.wait_ge(u_turned, 8 * i + s + 1)
                        for a in range(2):
                            act.activation(pp[:, s % 2, a, :], ps[:, 3 + s % 2, a * 2 * P:(a + 1) * 2 * P], ACT.Exp,
                                           bias=ngm[:, s % 2, a:a + 1], scale=SCALE, accum_out=sme[:, s % 2, a:a + 1])
                        act.activation(ske[:, s % 2, :], skd[:, s % 2, :], ACT.Exp).then_inc(u_exp, 1)
                    if s < KC and not (first and s >= 3):
                        keep_outs(i, s)
                    if not first:
                        if s == 7:
                            act.wait_ge(proj_kept, number(i, 5) + 1)
                        if s < KC:
                            lru_step(i, s)
                    if s >= 2:
                        act.wait_ge(u_pv, 8 * i + s - 2 + 3)
                        act.activation(oT[:, s - 2, bass.ds(i * P, P)], ps[:, 7, 0:P], ACT.Copy).then_inc(u_out, 1)
                    if s >= KC:
                        keep_outs(i, s)
                        if not first:
                            lru_step(i, s)

            act_round(0, True)
            with act.Fori(1, BLKS) as i:
                act_round(i)
            act.sem_inc(mg_sig, 3)
            act.wait_ge(lru_done, KC)
            for g in range(GRP):
                act.wait_ge(proj_done, N_PROJ - 2 + g)
                act.activation(yl[:, GC[g]], ps[:, g, 0:GW], ACT.Copy).then_inc(proj_kept, 1)
            act.wait_ge(proj_kept, N_PROJ)
            for s in range(KC + 2):
                lru_step(KC, s)
            act.wait_ge(lru_done, KC + 1)
            act.dma_start(O["tail"], tail[:, :, :]).then_inc(st_tail, 16)

            with act.Fori(0, KC) as n:
                for g in range(GRP):
                    for q, dst in ((0, sga), (2, sgr)):
                        m = 4 * g + q
                        act.wait_ge(mg_done, 12 * n + m + 1)
                        act.wait_ge(mg_out, 6 * n + 2 * g + (2 if q == 0 else 3))
                        act.activation(dst[:, :], ps[:, m % 6, 0:GW], ACT.Sigmoid).then_inc(mg_sig, 1)

            def stage(t, s, n=P):
                act.activation(mst[:, s, :, 0:n], merged[:, :, bass.ds(t * P, n)], ACT.Copy).then_inc(mst_ready, 1)

            def tile_norms(t, s, n=P, ahead=True, ahead_n=P):
                act.wait_ge(mix_done, t + 1)
                act.activation(junk[0:n, :].rearrange("p (h c) -> p h c", h=2), ps[0:n, 2 * s:2 * s + 2, :], ACT.Square,
                               accum_out=sst[0:n, s, 0:1]).then_inc(ch_act, 1)
                act.wait_ge(ch_act, 2 * t + 1)
                act.activation(sst[0:n, s, 1:2], sst[0:n, s, 0:1], ACT.Sqrt, bias=eps[0:n, :], scale=1.0 / D).then_inc(mix_sq, 1)
                if ahead:
                    stage(t + 2, s, ahead_n)
                act.wait_ge(x1_ready, t + 1)
                act.activation(junk[0:n, :], x1[0:n, bass.ds(t, 1), :].rearrange("p a c -> p (a c)"), ACT.Square,
                               accum_out=sst[0:n, s, 2:3]).then_inc(ch_act, 1)
                act.wait_ge(ch_act, 2 * t + 2)
                act.activation(sst[0:n, s, 3:4], sst[0:n, s, 2:3], ACT.Sqrt, bias=eps[0:n, :], scale=1.0 / D).then_inc(x1_sq, 1)
                act.wait_ge(h2_turned, t + 1)
                ge(act, lg_done, t)
                act.activation(h2T[:, :, 0:n], ps[:, 4:6, :].rearrange("p h (k c) -> p (h k) c", c=P)[:, :, 0:n], ACT.Copy).then_inc(h2T_ready, 1)

            act.wait_ge(mg_out, 6 * KC + 3)
            stage(0, 0)
            stage(1, 1)
            tile_norms(0, 0)
            tile_norms(1, 1)
            with act.Fori(1, 3) as i:
                for s in range(2):
                    tile_norms(2 * i + s, s)
            tile_norms(6, 0, ahead_n=NS)
            tile_norms(7, 1, ahead=False)
            tile_norms(8, 0, n=NS, ahead=False)

            act.wait_ge(rt_sub, 1)
            act.activation(gex[:, :, :], gex[:, :, :], ACT.Exp)
            act.activation(e1[:, :], e1[:, :], ACT.Exp).then_inc(rt_exp, 1)

            act.wait_ge(pairs_ready, 1)
            more = act.value_load(cnt_i[0:1, 0:1], min_val=NE // 2 - 1, max_val=MAXB // 2 - 1)
            act.sem_inc(st_y[0], 16)
            act.sem_inc(st_y[1], 16)
            act.sem_inc(yk_a, 1)

            def keep_x(n, s):
                act.wait_ge(xg_used, n + 2)
                act.activation(xT[s][:, 0:4, :], ps[:, 0, :].rearrange("p (k c) -> p k c", c=P), ACT.Copy).then_inc(xT_a, 1)

            def gate_sigmoid(n):
                act.wait_ge(gate_done, n + 3)
                act.activation(sgm[:, :, :], ps[:, 2, :].rearrange("p (m c) -> p m c", c=P), ACT.Sigmoid).then_inc(sg_ready, 1)

            def act_block(i, s, last=False):
                n = 2 * i + s
                if not last:
                    keep_x(n + 1, 1 - s)
                    act.wait_ge(a_ready, n + 1)
                    gate_sigmoid(n + 1)
                act.wait_ge(y_half, n + 1)
                act.wait_ge(st_y[s], 16 * i + 16)
                act.activation(ysb[:, s, 0:512], ps[:, 4, :], ACT.Copy).then_inc(yk_a, 1)
                act.wait_ge(yk_a, n + 2)
                act.wait_ge(yk_b, n + 2)
                act.dma_start(y_dram[bass.ds(n * P, P), :], ysb[:, s, :]).then_inc(st_y[s], 16)

            keep_x(0, 0)
            gate_sigmoid(0)
            act.wait_ge(blocks_ready, 1)
            with act.Fori(0, more) as i:
                for s in range(2):
                    act_block(i, s)
            act_block(more, 0)
            act_block(more, 1, True)

            def weigh(t):
                n = P if t < BLKS else NS
                act.wait_ge(ld_f[t], 32)
                act.activation(fy[0:n, t, 0, :], fy[0:n, t, 0, :], ACT.Copy, scale=wts[0:n, t, 0:1]).then_inc(f_first, 1)

            weigh(0)
            for t in range(TILES):
                n = P if t < BLKS else NS
                if t + 1 < TILES:
                    weigh(t + 1)
                act.wait_ge(f_sum, t + 1)
                act.activation(fjunk[0:n, :], fy[0:n, t, 0, :], ACT.Square, accum_out=fst[0:n, t, 0:1]).then_inc(ch_fin, 1)
                act.wait_ge(ch_fin, t + 1)
                act.activation(fst[0:n, t, 1:2], fst[0:n, t, 0:1], ACT.Sqrt, bias=eps[0:n, :], scale=1.0 / D).then_inc(f_sq, 1)

        @block.vector
        def _(dve):
            c = Chain(dve, ch_dve)
            V = nc.vector
            dve.wait_ge(c_sig, 1)
            V.tensor_tensor(cE[:, :, :], cE[:, :, :], cT[:, :, :], ALU.mult).then_inc(c_silu, 1)
            dve.wait_ge(ld_small, 12 * 16)
            lam = lvec[:, :, 2]
            c(V.tensor_scalar(spt[:, 2, :], lam, -1.0, None, ALU.mult))
            V.tensor_tensor(spt[:, 0, :], lam, spt[:, 2, :], ALU.max).then_inc(lam_abs, 1)
            dve.wait_ge(lam_abs, 1)
            dve.wait_ge(lam_exp, 1)
            c(V.tensor_scalar(spt[:, 2, :], spt[:, 2, :], 0.0, None, ALU.max))
            c(V.tensor_scalar(spt[:, 3, :], spt[:, 1, :], 2.0, None, ALU.add))
            c(V.reciprocal(spt[:, 3, :], spt[:, 3, :]))
            c(V.tensor_tensor(spt[:, 3, :], spt[:, 1, :], spt[:, 3, :], ALU.mult))
            c(V.tensor_tensor(spt[:, 4, :], spt[:, 3, :], spt[:, 3, :], ALU.mult))
            c(V.tensor_scalar(spt[:, 0, :], spt[:, 4, :], 1.0 / 17, None, ALU.mult))
            for d in (15, 13, 11, 9, 7, 5, 3):
                c(V.scalar_tensor_tensor(spt[:, 0, :], spt[:, 0, :], 1.0 / d, spt[:, 4, :], ALU.add, ALU.mult))
            c(V.scalar_tensor_tensor(spt[:, 0, :], spt[:, 0, :], 1.0, spt[:, 3, :], ALU.add, ALU.mult))
            c(V.scalar_tensor_tensor(spt[:, 0, :], spt[:, 0, :], 2.0, spt[:, 2, :], ALU.mult, ALU.add))
            c(V.tensor_scalar(lvec[:, :, 2], spt[:, 0, :], -8.0, None, ALU.mult))
            c(V.tensor_scalar(nsink[:, :], nsink[:, :], -1.0, None, ALU.mult))
            c(V.tensor_scalar(nsink_s[:, :], nsink_s[:, :], -1.0, None, ALU.mult))
            dve.wait_ge(ld_bada, 16)

            def keep_mod(n):
                dve.wait_ge(ada_done, n + 1)
                dst = modh[:, n * 512:(n + 1) * 512] if n < 4 else mod[:, (n - 4) * 512:(n - 3) * 512]
                V.tensor_tensor(dst, ps[0:1 + NB, 3 + n % 4, :], bada[:, n * 512:(n + 1) * 512], ALU.add).then_inc(ada_kept, 1)

            for n in range(4):
                keep_mod(n)
            for q in range(KC - 1):
                dve.wait_ge(sq_ready, q + 2)
                ge(dve, sq_used, q)
                V.tensor_tensor(ssum[:, :], ssum[:, :], sq[:, (q + 1) % 2, :], ALU.add).then_inc(sq_used, 1)
                if q % 2 == 0:
                    keep_mod(4 + q // 2)
            dve.wait_ge(modT_done, 1)
            c(V.tensor_copy(shT[:, :, :], ps[:, 7, 0:KC * (1 + NB)].rearrange("p (k j) -> p k j", k=KC)))
            c(V.scalar_tensor_tensor(scT[:, :, :], ps[:, 7, KC * (1 + NB):2 * KC * (1 + NB)].rearrange("p (k j) -> p k j", k=KC),
                                     1.0, bc(gpre[:, :].unsqueeze(2), (P, KC, 1 + NB)), ALU.add, ALU.mult))
            dve.wait_ge(rms_root, 1)
            c(V.reciprocal(rms_bc[:, :], rms_bc[:, :]))
            for k in range(KC):
                V.scalar_tensor_tensor(hT[:, k, 0:SEQ], hT[:, k, 0:SEQ], scT[:, k, 0:1], rms_bc[:, 0:SEQ],
                                       ALU.mult, ALU.mult).then_inc(h_scaled, 1)
            hs4 = hs_tmp[:, :, :].rearrange("p k (b t) -> p k b t", b=NB)
            c(V.tensor_tensor(hs_tmp[:, :, :], hT[:, :, SEQ:TOK], bc(rms_bc[:, SEQ:TOK].unsqueeze(1), (P, KC, NS)), ALU.mult))
            c(V.tensor_tensor(hs4, hs4, bc(scT[:, :, 1:1 + NB].unsqueeze(3), (P, KC, NB, NT)), ALU.mult))
            V.tensor_tensor(hT[:, :, SEQ:TOK].rearrange("p k (b t) -> p k b t", b=NB), hs4,
                            bc(shT[:, :, 1:1 + NB].unsqueeze(3), (P, KC, NB, NT)), ALU.add).then_inc(hs_ready, 1)

            for n in range(8, NADA):
                keep_mod(n)

            dve.wait_ge(ld_rope, 32)

            def rope(n, dst):
                dve.wait_ge(proj_kept, 3 * n + 3)
                ge(dve, rope_done, n)
                c(V.tensor_tensor(rtmp[:, :], dst, cosT[:, :], ALU.mult))
                dve.wait_ge(swapped, n + 1)
                c(V.tensor_tensor(turned[:, :], turned[:, :], sinT[:, :], ALU.mult))
                V.tensor_tensor(dst, turned[:, :], rtmp[:, :], ALU.add).then_inc(rope_done, 1)

            for p in range(2):
                rope(p, kT[:, p, P:])
            with dve.Fori(0, 4) as i:
                c.enter(i, 4)
                for q in range(2):
                    rope(2 * i + 2 + q, oT[:, bass.ds(2 * i + q, 1), :].rearrange("p a t -> p (a t)"))
            c.leave(4)

            dve.wait_ge(rope_done, 10)
            dve.wait_ge(ld_kc, 48)
            for p in range(2):
                V.tensor_copy(kcx[:, p, :, P:], kT[:, p, P + SEQ:].rearrange("p (b t) -> p b t", b=NB)).then_inc(s_staged, 1)
            for p in range(2):
                src = oT[:, 4 * p:4 * p + 4, SEQ:TOK].rearrange("p j (b t) -> p b j t", b=NB)
                for two in range(2):
                    V.tensor_copy(qs[:, p, :, 16 * two:16 * two + 16].rearrange("p b (j t) -> p b j t", j=4), src).then_inc(s_staged, 1)
            c(V.memset(pZ[:, :], 0.0))
            dve.wait_ge(s_scores, 1)
            for q, nb in enumerate((3, 3, 2)):
                c(V.tensor_reduce(mxs[:, 3 * q:3 * q + nb], ps[:, 3 + q, 0:nb * (P + NT)].rearrange("p (b k) -> p b k", b=nb), AX_X, ALU.max))
            c(V.scalar_tensor_tensor(ngs[:, :], mxs[:, :], -SCALE, bc(nsink_s[:, :], (P, NB)), ALU.mult, ALU.min))
            V.tensor_tensor(sks[:, :], ngs[:, :], bc(nsink_s[:, :], (P, NB)), ALU.subtract).then_inc(s_negmax, 1)
            dve.wait_ge(s_exp, 1)
            c(V.tensor_tensor(sms[:, :], sms[:, :], skes[:, :], ALU.add))
            c(V.reciprocal(rcs[:, :], sms[:, :]))
            c(V.tensor_tensor(pS[:, :, :], pS[:, :, :], bc(rcs[:, :].unsqueeze(2), (P, NB, P + NT)), ALU.mult))
            V.tensor_copy(pZ[:, :].rearrange("p (b x) -> p b x", b=NB)[:, :, 0:NT], pS[:, :, P:]).then_inc(s_norm, 1)
            dve.wait_ge(s_pv, 1)
            for p in range(2):
                ins = V.tensor_copy(oT[:, 4 * p:4 * p + 4, SEQ:TOK].rearrange("p j (b t) -> p b j t", b=NB),
                                    ps[:, 5, P * p:P * (p + 1)].rearrange("p (b j t) -> p b j t", b=NB, j=4))
            ins.then_inc(s_out, 1)

            u, l = Chain(dve, ch_unit), Chain(dve, ch_lru)
            dve.wait_ge(st_kws, 32)
            dve.wait_ge(s_out, 1)
            l(V.memset(xlp[:, 0:XPAD], 0.0))
            dve.sem_inc(xc_ready, 1)
            dve.sem_inc(lru_done, 1)
            dve.sem_inc(u_kept, 2)
            xcs = xc[:, SEQ:TOK].rearrange("p (b t) -> p b t", b=NB)
            def first(i, s):
                w = s % 2
                dve.wait_ge(u_scores, 8 * i + s + 1)
                u(V.tensor_reduce(mx[:, w, :], ps[:, 3 + w, :].rearrange("p (a k) -> p a k", a=2), AX_X, ALU.max))
                u(V.scalar_tensor_tensor(ngm[:, w, :], mx[:, w, :], -SCALE, nsink[:, 2 * s:2 * s + 2], ALU.mult, ALU.min))
                V.tensor_tensor(skd[:, w, :], ngm[:, w, :], nsink[:, 2 * s:2 * s + 2], ALU.subtract).then_inc(u_negmax, 1)

            def second(i, s):
                w = s % 2
                dve.wait_ge(u_exp, 8 * i + s + 3)
                u(V.tensor_tensor(sme[:, w, :], sme[:, w, :], ske[:, w, :], ALU.add))
                u(V.reciprocal(rcp[:, w, :], sme[:, w, :]))
                V.tensor_scalar(pp[:, w, 0, :], pp[:, w, 0, :], rcp[:, w, 0:1], None, ALU.mult)
                V.tensor_scalar(pp[:, w, 1, :], pp[:, w, 1, :], rcp[:, w, 1:2], None, ALU.mult).then_inc(u_norm, 1)

            def conv(i, s):
                j = s - 4
                if j == 0:
                    dve.wait_ge(proj_kept, number(i, 2) + 1)
                    l(V.tensor_copy(lcur[:, :], lvec[:, bass.ds(i, 1), :].rearrange("p a v -> p (a v)")))
                    l(V.tensor_scalar(xc[:, 0:SEQ], xlp[:, 0:SEQ], lcur[:, 4:5], lcur[:, 3:4], ALU.mult, ALU.add))
                    l(V.tensor_scalar(xcs, xls[:, :, 0:NT], lcur[:, 4:5], lcur[:, 3:4], ALU.mult, ALU.add))
                else:
                    w = lcur[:, 4 + j:5 + j]
                    l(V.scalar_tensor_tensor(xc[:, 0:SEQ], xlp[:, j:j + SEQ], w, xc[:, 0:SEQ], ALU.mult, ALU.add))
                    l(V.scalar_tensor_tensor(xcs, xls[:, :, j:j + NT], w, xcs, ALU.mult, ALU.add))
                if s == 7:
                    V.tensor_copy(tail[:, bass.ds(i, 1), 0:XPAD].rearrange("p a t -> p (a t)"), xlp[:, SEQ:SEQ + XPAD])
                    V.tensor_copy(tail[:, bass.ds(i, 1), 12:36].rearrange("p a (b t) -> p (a b) t", t=XPAD), xls[:, :, NT:]).then_inc(xc_ready, 1)

            def lru_step(i, s):
                if s == 1:
                    dve.wait_ge(proj_kept, number(i - 1, 11) + 1)
                    l(V.tensor_tensor(gB[:, :], gB[:, :], xc[:, :], ALU.mult))
                if s == 2:
                    dve.wait_ge(decay, i)
                    l(V.tensor_tensor(xc[:, :], gC[:, :], gC[:, :], ALU.mult))
                    V.scalar_tensor_tensor(xc[:, :], xc[:, :], 1.0, gA[:, :], ALU.add, ALU.mult).then_inc(gap, 1)
                if s == 3:
                    dve.wait_ge(gap_root, i)
                    V.tensor_tensor(xc[:, :], xc[:, :], gB[:, :], ALU.mult).then_inc(lru_in, 1)
                    at0 = gC[:, SEQ:TOK].rearrange("p (b t) -> p b t", b=NB)[:, :, 0]
                    l(V.tensor_tensor(t8[:, :], at0, h0[:, bass.ds(i - 1, 1), :].rearrange("p a b -> p (a b)"), ALU.mult))
                    dve.wait_ge(lru_in, i)
                    l(V.tensor_tensor(xcs[:, :, 0], xcs[:, :, 0], t8[:, :], ALU.add))
                    l(V.memset(at0, 0.0))
                    h = olT[:, bass.ds(i - 1, 1), :].rearrange("p a t -> p (a t)")
                    l(V.tensor_tensor_scan(h[:, 0:SEQ], gC[:, 0:SEQ], xc[:, 0:SEQ], 0.0, ALU.mult, ALU.add))
                    V.tensor_tensor_scan(h[:, SEQ:TOK], gC[:, SEQ:TOK], xc[:, SEQ:TOK], 0.0, ALU.mult, ALU.add).then_inc(lru_scan, 1)
                    dve.wait_ge(lru_scan, i)
                    l(V.tensor_copy(tail[:, bass.ds(i - 1, 1), 3:4].rearrange("p a t -> p (a t)"), h[:, SEQ - 1:SEQ]))
                    l(V.tensor_copy(tail[:, bass.ds(i - 1, 1), 4:12].rearrange("p a t -> p (a t)"),
                                    h[:, SEQ:TOK].rearrange("p (b t) -> p b t", b=NB)[:, :, NT - 1]))
                if s == 8:
                    dve.wait_ge(y_sq, i)
                    l(V.tensor_scalar(gC[:, :], gC[:, :], GELU_A, 1.0, ALU.mult, ALU.add))
                    V.tensor_tensor(gC[:, :], gC[:, :], yl[:, :], ALU.mult).then_inc(y_arg, 1)
                if s == 9:
                    dve.wait_ge(y_tanh, i)
                    h = olT[:, bass.ds(i - 1, 1), :].rearrange("p a t -> p (a t)")
                    l(V.scalar_tensor_tensor(gC[:, :], gC[:, :], 1.0, yl[:, :], ALU.add, ALU.mult))
                    V.scalar_tensor_tensor(h, gC[:, :], 0.5, h, ALU.mult, ALU.mult).then_inc(lru_done, 1)

            def dve_round(i, begin=False):
                for s in range(KC + 2):
                    if s < KC:
                        first(i, s)
                    if s == 0:
                        l(V.tensor_copy(xls[:, :, 0:XPAD], stc[:, bass.ds(i, 1), :, :].rearrange("p a b t -> p (a b) t")))
                    if not begin and s < KC:
                        lru_step(i, s)
                    if 4 <= s < KC:
                        conv(i, s)
                    if s < KC:
                        second(i, s)
                    if 1 <= s <= KC:
                        w = (s - 1) % 2
                        dve.wait_ge(u_turned, 8 * i + s - 1 + 3)
                        dve.wait_ge(u_pv, 8 * i + s - 1 + 1)
                        V.tensor_copy(pT[:, w, :, :], ps[:, 5 + w, :].rearrange("p (k q) -> p k q", k=4)).then_inc(u_kept, 1)
                    if not begin and s >= KC:
                        lru_step(i, s)

            dve_round(0, True)
            with dve.Fori(1, BLKS) as i:
                u.enter(i - 1, 4 * KC)
                l.enter(i - 1, 20)
                dve_round(i)
            u.leave(BLKS - 1)
            l.leave(BLKS - 1)
            dve.wait_ge(st_side, 64)
            dve.sem_inc(mg_out, 3)
            for s in range(KC + 2):
                lru_step(KC, s)

            with dve.Fori(0, KC) as n:
                l.enter(n, GRP)
                for g in range(GRP):
                    dve.wait_ge(mg_done, 12 * n + 4 * g + 2)
                    dve.wait_ge(mg_sig, 6 * n + 2 * g + 4)
                    dve.wait_ge(mg_out, 6 * n + 2 * g + 3)
                    V.tensor_tensor(mtmp[:, :], sga[:, :], ps[:, (4 * g + 1) % 6, 0:GW], ALU.mult).then_inc(mg_out, 1)
                    dve.wait_ge(mg_done, 12 * n + 4 * g + 4)
                    dve.wait_ge(mg_sig, 6 * n + 2 * g + 5)
                    l(V.tensor_tensor(sgr[:, :], sgr[:, :], ps[:, (4 * g + 3) % 6, 0:GW], ALU.mult))
                    dve.wait_ge(mg_out, 6 * n + 2 * g + 4)
                    V.tensor_tensor(merged[:, bass.ds(n, 1), GC[g]].rearrange("p a t -> p (a t)"), mtmp[:, :], sgr[:, :],
                                    ALU.add).then_inc(mg_out, 1)
            l.leave(KC)

            dve.wait_ge(ld_spread, 96)
            kinds = ((G1p, G1s), (B2p, B2s), (A2p, A2s), (G2p, G2s))
            q = 0
            for r in range(4):
                for nn in range(2):
                    for t, n in zip(kinds[r], (P, NS)):
                        dst, src = t[0:n, nn * 512:(nn + 1) * 512], ps[0:n, 4 + q % 4, :]
                        q += 1
                        dve.wait_ge(spread_done, q)
                        if r == 1:
                            ins = V.tensor_copy(dst, src)
                        elif r == 2:
                            ins = V.scalar_tensor_tensor(dst, src, 1.0, dst, ALU.add, ALU.mult)
                        else:
                            ins = V.tensor_tensor(dst, src, dst, ALU.mult)
                        ins.then_inc(spread_kept, 1)
            dve.wait_ge(spread_kept, 16)
            k = Chain(dve, ch_tok)
            k(V.memset(lg[:, TILES - 1, :], 0.0))
            dve.wait_ge(ld_route, 80)

            def keep_logits(t, n=P):
                dve.wait_ge(lg_done, t + 1)
                V.tensor_tensor(lg[0:n, bass.ds(t, 1), :].rearrange("p a c -> p (a c)"), ps[0:n, 6, 0:NG + NE], brt[0:n, :],
                                ALU.add).then_inc(lg_kept, 1)

            def tile_sums(t, s, i, n=P):
                G1, A2, B2 = (G1p, A2p, B2p) if n == P else (G1s, A2s, B2s)
                xt = x1[0:n, bass.ds(t, 1), :].rearrange("p a c -> p (a c)")
                half = lambda x: x.rearrange("p (h c) -> p h c", h=2)
                dve.wait_ge(mix_sq, t + 1)
                k(V.reciprocal(sst[0:n, s, 1:2], sst[0:n, s, 1:2]))
                V.scalar_tensor_tensor(half(xt), ps[0:n, 2 * s:2 * s + 2, :], sst[0:n, s, 1:2], half(G1[0:n, :]),
                                       ALU.mult, ALU.mult).then_inc(x1_half, 1)
                dve.wait_ge(x1_half, t + 1)
                dve.wait_ge(ld_xin[s], 16 * i + 16)
                V.tensor_tensor(xt, xt, xin[0:n, s, :], ALU.add).then_inc(x1_ready, 1)
                dve.wait_ge(x1_sq, t + 1)
                k(V.reciprocal(sst[0:n, s, 3:4], sst[0:n, s, 3:4]))
                ge(dve, st_h2[s], 16 * i)
                ge(dve, h2_turned, t - 1)
                k(V.scalar_tensor_tensor(h2[0:n, s, :], xt, sst[0:n, s, 3:4], A2[0:n, :], ALU.mult, ALU.mult))
                V.tensor_tensor(h2[0:n, s, :], h2[0:n, s, :], B2[0:n, :], ALU.add).then_inc(h2_ready, 1)
                if not (isinstance(t, int) and t == 0):
                    keep_logits(t - 1)

            def best(t0, t1):
                ts, n = slice(t0, t1), t1 - t0
                k(V.tensor_copy(lg8[:, ts, 0:NG], lg[:, ts, 0:NG]))
                for t in range(t0, t1):
                    k(V.max(gm8[:, t, :], lg8[:, t, :]))
                for t in range(t0, t1):
                    k(V.max_index(gi8[:, t, :], gm8[:, t, :], lg8[:, t, :]))
                k(V.tensor_copy(gix[:, ts], gi8[:, ts, 0]))
                k(V.tensor_tensor(ohg[:, ts, :], bc(iot[:, 0:NG].unsqueeze(1), (P, n, NG)), bc(gix[:, ts].unsqueeze(2), (P, n, NG)), ALU.is_equal))
                for t in range(t0, t1):
                    k(V.tensor_tensor(prd[:, t, :, :], lg[:, t, NG:].rearrange("p (g e) -> p e g", g=NG),
                                      bc(ohg[:, t, :].unsqueeze(1), (P, EPG, NG)), ALU.mult))
                k(V.tensor_reduce(ing[:, ts, :], prd[:, ts, :, :], AX_X, ALU.add))
                for t in range(t0, t1):
                    k(V.max(em8[:, t, :], ing[:, t, :]))
                for t in range(t0, t1):
                    k(V.max_index(ei8[:, t, :], em8[:, t, :], ing[:, t, :]))

            tile_sums(0, 0, 0)
            tile_sums(1, 1, 0)
            with dve.Fori(1, 4) as i:
                k.enter(i - 1, 6)
                for s in range(2):
                    tile_sums(2 * i + s, s, i)
            k.leave(3)
            k(V.memset(lg8[:, :, :], -3.0e38))
            dve.wait_ge(lg_kept, TILES - 2)
            best(0, TILES - 2)
            tile_sums(8, 0, 4, NS)
            keep_logits(8, NS)

            dve.wait_ge(lg_kept, TILES)
            dve.wait_ge(h2_ready, TILES)
            best(TILES - 2, TILES)
            k(V.tensor_copy(eix[:, :, :], ei8[:, :, 0:2]))
            k(V.scalar_tensor_tensor(eix[:, :, :], bc(gix[:, :].unsqueeze(2), (P, TILES, 2)), float(EPG), eix[:, :, :], ALU.mult, ALU.add))
            k(V.tensor_tensor(oh[:, :, :, :].rearrange("p t k e -> p (t k) e"), bc(iot[:, 0:NE].unsqueeze(1), (P, TK, NE)),
                              bc(eix[:, :, :].rearrange("p t k -> p (t k)").unsqueeze(2), (P, TK, NE)), ALU.is_equal))
            V.tensor_tensor(ohs[:, :, :], oh[:, :, 0, :], oh[:, :, 1, :], ALU.add).then_inc(oh_ready, 1)
            k(V.tensor_tensor(gex[:, :, :], lg[:, :, 0:NG], bc(gm8[:, :, 0:1], (P, TILES, NG)), ALU.subtract))
            V.tensor_tensor(e1[:, :], em8[:, :, 1], em8[:, :, 0], ALU.subtract).then_inc(rt_sub, 1)
            dve.wait_ge(rank_done, 1)
            k(V.tensor_copy(cntf[:, :], ps[:, 7, TILES * NE:(TILES + 1) * NE]))
            k(V.scalar_tensor_tensor(cmp9[:, :, :], bc(iot[:, 1:TILES + 1].unsqueeze(1), (P, NE, TILES)), float(P),
                                     bc(cntf[:, :].unsqueeze(2), (P, NE, TILES)), ALU.mult, ALU.is_lt))
            k(V.tensor_reduce(nbk[:, :], cmp9[:, :, :], AX_X, ALU.add))
            k(V.memset(bas[:, :], 1.0))
            k(V.tensor_tensor_scan(incl[:, :], bas[:, :], nbk[:, :], 0.0, ALU.mult, ALU.add))
            k(V.tensor_scalar(cnt_i[:, 1:2], incl[:, NE - 1:NE], float(NE - 1), None, ALU.add))
            V.tensor_scalar(cnt_i[:, 0:1], cnt_i[:, 1:2], 1, None, ALU.logical_shift_right).then_inc(pairs_ready, 1)
            k(V.tensor_tensor(bas[:, :], incl[:, :], nbk[:, :], ALU.subtract))
            k(V.scalar_tensor_tensor(bas[:, :], bas[:, :], float(NE - 1), iot[:, 0:NE], ALU.add, ALU.subtract))
            k(V.tensor_scalar(bas[:, :], bas[:, :], float(P), None, ALU.mult))
            rank = ps[:, 7, 0:TILES * NE].rearrange("p (t e) -> p t e", t=TILES)
            k(V.scalar_tensor_tensor(qrk[:, :, :], rank, float(P), bc(bas[:, :].unsqueeze(1), (P, TILES, NE)), ALU.is_ge, ALU.mult))
            k(V.tensor_tensor(qrk[:, :, :], qrk[:, :, :], rank, ALU.add))
            k(V.scalar_tensor_tensor(qrk[:, :, :], bc(iot[:, 0:NE].unsqueeze(1), (P, TILES, NE)), float(P), qrk[:, :, :], ALU.mult, ALU.add))
            for a in range(2):
                k(V.tensor_tensor(mq[:, :, a, :], oh[:, :, a, :], qrk[:, :, :], ALU.mult))
            k(V.tensor_reduce(pos_f[:, :], mq[:, :, :, :].rearrange("p t k e -> p (t k) e"), AX_X, ALU.add))
            k(V.tensor_copy(pos_i[:, :], pos_f[:, :]))
            k(V.tensor_scalar(sl_i[:, 0, :], pos_i[:, :], P - 1, None, ALU.bitwise_and))
            k(V.tensor_scalar(sl_i[:, 1, :], pos_i[:, :], 7, None, ALU.logical_shift_right))
            k(V.tensor_copy(sl_f[:, :, :], sl_i[:, :, :]))
            k(V.tensor_tensor(ohslot[:, :, :], bc(iot[:, :].unsqueeze(1), (P, TK, P)), bc(sl_f[:, 0, :].unsqueeze(2), (P, TK, P)), ALU.is_equal))
            k(V.tensor_tensor(ohblk[:, :, :], bc(iot[:, 0:MAXB].unsqueeze(1), (P, TK, MAXB)), bc(sl_f[:, 1, :].unsqueeze(2), (P, TK, MAXB)), ALU.is_equal))
            for a in range(2):
                ins = V.tensor_tensor(rhs2[:, :, a, :], ohblk[:, :, :], bc(tpid[:, a, :].unsqueeze(2), (P, TK, MAXB)), ALU.mult)
            ins.then_inc(hot_ready, 1)
            k(V.memset(slot_tok[:, :], 0))
            dve.wait_ge(slot_done, 1)
            k(V.tensor_copy(slf[:, :], ps[:, 6, MAXB:2 * MAXB]))
            V.scalar_tensor_tensor(slot_tok[:, 0:MAXB], ps[:, 6, 0:MAXB], float(P), slf[:, :], ALU.mult, ALU.add).then_inc(slots_ready, 1)
            dve.wait_ge(rt_exp, 1)
            k(V.tensor_reduce(gsm[:, :], gex[:, :, :], AX_X, ALU.add))
            k(V.scalar_tensor_tensor(gsm[:, :], e1[:, :], 1.0, gsm[:, :], ALU.add, ALU.mult))
            k(V.reciprocal(wts[:, :, 0], gsm[:, :]))
            k(V.tensor_tensor(wts[:, :, 1], wts[:, :, 0], e1[:, :], ALU.mult))

            k(V.tensor_tensor(cmpb[:, :, :], bc(iot[:, 0:MAXB - NE].unsqueeze(2), (P, MAXB - NE, NE)),
                              bc(incl[:, :].unsqueeze(1), (P, MAXB - NE, NE)), ALU.is_ge))
            k(V.tensor_reduce(slf[:, 0:MAXB - NE], cmpb[:, :, :], AX_X, ALU.add))
            k(V.tensor_scalar(blk_i[:, NE:MAXB], slf[:, 0:MAXB - NE], float(NE - 1), None, ALU.min))
            V.tensor_copy(blk_i[:, 0:NE], iot[:, 0:NE]).then_inc(blocks_ready, 1)

            more = dve.value_load(cnt_i[0:1, 0:1], min_val=NE // 2 - 1, max_val=MAXB // 2 - 1)
            dve.sem_inc(yk_b, 1)

            def keep_x(n, s):
                dve.wait_ge(xg_used, n + 2)
                V.tensor_copy(xT[s][:, 4:8, :], ps[:, 1, :].rearrange("p (k c) -> p k c", c=P)).then_inc(xT_b, 1)

            def gate_product(n):
                dve.wait_ge(sg_ready, n + 1)
                V.tensor_tensor(sgm[:, :, :], sgm[:, :, :], ps[:, 2, :].rearrange("p (m c) -> p m c", c=P), ALU.mult).then_inc(ch_moe, 1)

            sp = Chain(dve, ch_split)

            def split(whole, up, low, done):
                sp(V.tensor_copy(up, whole))
                V.tensor_tensor(low, whole, up.bitcast(F32), ALU.subtract).then_inc(done, 1)

            def dve_block(i, s, last=False):
                n = 2 * i + s
                if not last:
                    keep_x(n + 1, 1 - s)
                dve.wait_ge(ld_d[s], 16 * i + 16)
                dve.wait_ge(y_done, n + 2)
                split(wd[s][:, :, :], wd_up[:, :, :], wd_low[s][:, :, :], wd_split)
                dve.wait_ge(ch_moe, n + 1)
                dve.wait_ge(up_done, n + 3)
                sp(V.tensor_tensor(aT[:, :, :], sgm[:, :, :], ps[:, 3, :].rearrange("p (m c) -> p m c", c=P), ALU.mult))
                split(aT[:, :, :], a_up[:, :, :], a_low[:, :, :], a_ready)
                if not last:
                    gate_product(n + 1)
                dve.wait_ge(y_done, n + 3)
                dve.wait_ge(st_y[s], 16 * i + 16)
                V.tensor_copy(ysb[:, s, 512:1024], ps[:, 5, :]).then_inc(yk_b, 1)

            keep_x(0, 0)
            gate_product(0)
            with dve.Fori(0, more) as i:
                sp.enter(i, 6)
                for s in range(2):
                    dve_block(i, s)
            sp.leave(more)
            dve_block(more, 0)
            dve_block(more, 1, True)

            def add_second(t):
                n = P if t < BLKS else NS
                dve.wait_ge(f_first, t + 1)
                dve.wait_ge(ld_f[t], 32)
                V.scalar_tensor_tensor(fy[0:n, t, 0, :], fy[0:n, t, 1, :], wts[0:n, t, 1:2], fy[0:n, t, 0, :],
                                       ALU.mult, ALU.add).then_inc(f_sum, 1)

            add_second(0)
            for t in range(TILES):
                n, G2 = (P, G2p) if t < BLKS else (NS, G2s)
                if t + 1 < TILES:
                    add_second(t + 1)
                dve.wait_ge(f_sq, t + 1)
                V.reciprocal(fst[0:n, t, 1:2], fst[0:n, t, 1:2]).then_inc(ch_fin2, 1)
                dve.wait_ge(ch_fin2, t + 1)
                V.scalar_tensor_tensor(fy[0:n, t, 0, :], fy[0:n, t, 0, :], fst[0:n, t, 1:2], G2[0:n, :],
                                       ALU.mult, ALU.mult).then_inc(f_norm, 1)
                if t >= TILES - DVE_ADDS:
                    dve.wait_ge(f_norm, t + 1)
                    V.tensor_tensor(fy[0:n, t, 1, :], fy[0:n, t, 0, :], x1[0:n, t, :], ALU.add).then_inc(yo_last, 1)

        @block.tensor
        def _(pe):
            def mm(out, lhsT, rhs, start, stop):
                return pe.matmul(out, lhsT, rhs, start=start, stop=stop, skip_group_check=True)

            def chunk_sum(out, w, src):
                for k in range(KC):
                    ins = mm(out, w(k), src(k), k == 0, k == KC - 1)
                return ins

            def ada(n):
                pe.wait_ge(ld_wada[n % 4], 16 * (n // 4 + 1))
                ge(pe, ada_kept, n - 3)
                chunk_sum(ps[0:1 + NB, 3 + n % 4, :], lambda k: cE[:, k, :], lambda k: wada[n % 4][:, k, :]).then_inc(ada_done, 1)

            pe.wait_ge(c_silu, 1)
            for n in range(8):
                ada(n)
            pe.wait_ge(ones_set, 1)
            pe.wait_ge(sq_used, KC - 1)
            for g in range(GRP):
                ins = mm(ps[:, g, 0:GW], ones[:, :], ssum[:, GC[g]], True, True)
            ins.then_inc(ssq_done, 1)
            pe.wait_ge(ld_small, 12 * 16)
            pe.wait_ge(ada_kept, 4)
            for k in range(2 * KC):
                ins = pe.transpose(ps[:, 7, k * (1 + NB):(k + 1) * (1 + NB)], modh[:, k * P:(k + 1) * P], ident[0:1 + NB, 0:1 + NB])
            ins.then_inc(modT_done, 1)
            for n in range(8, NADA):
                ada(n)

            pe.wait_ge(h_ready, KC)
            pe.wait_ge(hs_ready, 1)
            pe.wait_ge(rms_root, 1)

            def project(n, w):
                for g in range(GRP):
                    ge(pe, proj_kept, n + g - 2)
                    chunk_sum(ps[:, g, 0:GW], lambda k: w[:, k, :], lambda k: hT[:, k, GC[g]]).then_inc(proj_done, 1)

            pe.wait_ge(ld_wA, 16)
            project(0, wA)
            pe.wait_ge(ld_wB, 16)
            project(3, wB)
            pe.wait_ge(ld_wV, 16)
            for t in range(TILES):
                n = P if t < BLKS else NS
                ge(pe, v_kept, t - 1)
                chunk_sum(ps[0:n, 6 + t % 2, 0:KV], lambda k: hT[:, k, t * P:t * P + n], lambda k: wV[:, k, :]).then_inc(v_done, 1)
            with pe.Fori(0, 4) as i:
                pe.wait_ge(ld_wA, 16 * i + 32)
                project(6 * i + 6, wA)
                pe.wait_ge(ld_wB, 16 * i + 32)
                project(6 * i + 9, wB)

            def outs(i, s):
                for o in outs_at(s):
                    if o == 0:
                        pe.wait_ge(ld_wA, 16 * i + 96)
                    if o == 3:
                        pe.wait_ge(ld_wB, 16 * i + 80)
                    if o == 6:
                        pe.wait_ge(ld_wlg, 16 * i + 16)
                        pe.wait_ge(xc_ready, i + 2)
                    pe.wait_ge(proj_kept, number(i, o) - 2)
                    out = ps[:, o % 3, 0:GW]
                    if o < 6:
                        w = wA if o < 3 else wB
                        chunk_sum(out, lambda k: w[:, k, :], lambda k: hT[:, k, GC[o % 3]]).then_inc(proj_done, 1)
                    else:
                        mm(out, wlg[:, o % 2, :], xc[:, GC[(o - 6) // 2]], True, True).then_inc(proj_done, 1)

            outs(0, 0)
            pe.wait_ge(s_staged, 6)
            pe.wait_ge(rope_done, 10)
            for b in range(NB):
                cols = slice((b % 3) * (P + NT), (b % 3 + 1) * (P + NT))
                mm(ps[:, 3 + b // 3, cols], identb[:, :], mask_s[:, :], True, False)
                for kv in range(4):
                    p, a = kv // 2, HD * (kv % 2)
                    ins = mm(ps[32 * kv:32 * kv + 32, 3 + b // 3, cols], qs[a:a + HD, p, b, :], kcx[a:a + HD, p, b, :], False, True)
            ins.then_inc(s_scores, 1)
            outs(0, 1)
            pe.wait_ge(s_norm, 1)
            for hf in range(2):
                for b in range(4):
                    ins = pe.transpose(ps[:, 6 + hf, b * P:(b + 1) * P], pS[:, 4 * hf + b, 0:P], ident[:, :])
                ins.then_inc(s_turned, 1)
                for b in range(4):
                    at = (4 * hf + b) * NS
                    ins = pe.transpose(ps[0:NS, 3 + hf, b * P:(b + 1) * P], pZ[:, at:at + NS], ident[:, :])
                ins.then_inc(s_turned, 1)
            pe.wait_ge(s_kept, 4)
            for kv in range(4):
                p, a = kv // 2, HD * (kv % 2)
                mm(ps[a:a + HD, 5, P * p:P * (p + 1)], vtok[0:NS, TILES, HD * kv:HD * kv + HD], pTn[:, :, 32 * kv:32 * kv + 16], p == 0, False)
            for kv in range(4):
                p, a = kv // 2, HD * (kv % 2)
                for b in range(NB):
                    ins = mm(ps[a:a + HD, 5, P * p + 16 * b:P * p + 16 * b + 16], vc[:, b, HD * kv:HD * kv + HD],
                             pTs[:, b, 32 * kv:32 * kv + 16], False, True)
            ins.then_inc(s_pv, 1)
            outs(0, 2)

            pe.sem_inc(u_turned, 2)
            pe.sem_inc(u_pv, 2)
            pe.wait_ge(s_out, 1)
            def pe_round(i, begin=False):
                for s in range(KC + 2):
                    if s < KC:
                        pe.wait_ge(u_staged, 16 * i + 2 * s + 2)
                        pe.wait_ge(u_exp, 8 * i + s + 1)
                        for a in range(2):
                            out = ps[:, 3 + s % 2, a * 2 * P:(a + 1) * 2 * P]
                            mm(out, identb[:, :], masks[:, bass.ds(i, 1), :].rearrange("p a k -> p (a k)"), True, False)
                            ins = mm(out, qst[:, s % 4, a, :], kT[:, s // 4, bass.ds(i * P, 2 * P)], False, True)
                        ins.then_inc(u_scores, 1)
                    if s < KC and not begin:
                        outs(i, s)
                    if 1 <= s <= KC:
                        w = (s - 1) % 2
                        pe.wait_ge(u_norm, 8 * i + s)
                        pe.wait_ge(u_kept, 8 * i + s)
                        for a in range(2):
                            for hf in range(2):
                                q = 2 * a + hf
                                ins = pe.transpose(ps[:, 5 + w, q * P:(q + 1) * P], pp[:, w, a, hf * P:(hf + 1) * P], ident[:, :])
                        ins.then_inc(u_turned, 1)
                    if s >= 2:
                        w = (s - 2) % 2
                        pe.wait_ge(u_kept, 8 * i + s - 2 + 3)
                        pe.wait_ge(u_out, 8 * i + s - 2 + 4)
                        for a in range(2):
                            for hf in range(2):
                                ins = mm(ps[HD * a:HD * a + HD, 7, 0:P], vst[:, (s - 2) % 4, hf, HD * a:HD * a + HD],
                                         pT[:, w, 2 * a + hf, :], hf == 0, hf == 1)
                        ins.then_inc(u_pv, 1)
                    if s >= KC:
                        outs(i, s)

            pe_round(0, True)
            with pe.Fori(1, BLKS) as i:
                pe_round(i)
            pe.wait_ge(ld_wB, 16 * KC + 80)
            for g in range(GRP):
                pe.wait_ge(proj_kept, N_PROJ - 5 + g)
                chunk_sum(ps[:, g, 0:GW], lambda k: wB[:, k, :], lambda k: hT[:, k, GC[g]]).then_inc(proj_done, 1)

            pe.wait_ge(u_out, 4 + KC * BLKS)
            pe.wait_ge(proj_kept, N_PROJ)
            with pe.Fori(0, KC) as n:
                srcs = (hT, oT, hT, olT)
                for m in range(4 * GRP):
                    g, q = m // 4, m % 4
                    if g == 0:
                        pe.wait_ge(ld_wmg[q], 16 * n + 16)
                    if m == 3:
                        pe.wait_ge(lru_done, KC + 1)
                    pe.wait_ge(mg_out if q % 2 else mg_sig, 6 * n + m // 2 + 1)
                    chunk_sum(ps[:, m % 6, 0:GW], lambda k: wmg[q][:, k, :], lambda k: srcs[q][:, k, GC[g]]).then_inc(mg_done, 1)

            def wout(k):
                return wout_lo[:, k, :] if k < KLO else wout_hi[:, k - KLO, :]

            def mix(t, s, n=P):
                pe.wait_ge(mst_ready, t + 1)
                ge(pe, x1_half, t - 1)
                for nn in range(2):
                    ins = chunk_sum(ps[0:n, 2 * s + nn, :], lambda k: mst[:, s, k, 0:n], lambda k: wout(k)[:, nn * 512:(nn + 1) * 512])
                ins.then_inc(mix_done, 1)

            def route(t, s, n=P):
                pe.wait_ge(h2_ready, t + 1)
                ge(pe, h2T_ready, t)
                for k in range(KC):
                    ins = pe.transpose(ps[:, 4 + k // 4, (k % 4) * P:(k % 4) * P + n], h2[0:n, s, k * P:(k + 1) * P], ident[0:n, 0:n])
                ins.then_inc(h2_turned, 1)
                pe.wait_ge(h2T_ready, t + 1)
                ge(pe, lg_kept, t)
                chunk_sum(ps[0:n, 6, 0:NG + NE], lambda k: h2T[:, k, 0:n], lambda k: wr[:, k, :]).then_inc(lg_done, 1)

            pe.wait_ge(ld_wout, 32)
            mix(0, 0)
            q = 0
            for r in range(4):
                for nn in range(2):
                    for n, at in ((P, 0), (NS, P)):
                        ge(pe, spread_kept, q - 3)
                        mm(ps[0:n, 4 + q % 4, :], sel[:, at:at + n], mod[:, r * D + nn * 512:r * D + (nn + 1) * 512], True, True).then_inc(spread_done, 1)
                        q += 1
            pe.wait_ge(spread_kept, 16)
            mix(1, 1)
            pe.wait_ge(ld_route, 80)
            route(0, 0)
            mix(2, 0)
            route(1, 1)
            with pe.Fori(1, 3) as i:
                for s in range(2):
                    mix(2 * i + s + 1, 1 - s)
                    route(2 * i + s, s)
            mix(7, 1)
            route(6, 0)
            mix(8, 0, NS)
            route(7, 1)
            route(8, 0, NS)

            pe.wait_ge(oh_ready, 1)

            def rows(t):
                return P if t < BLKS else NS

            for t in range(TILES + 1):
                out = ps[:, 7, t * NE:(t + 1) * NE]
                for b in range(min(t + 1, TILES)):
                    w = ubf[0:rows(b), 0 if b == t else 1, :]
                    ins = mm(out, w, ohs[0:rows(b), b, :], b == 0, b == min(t, TILES - 1))
            ins.then_inc(rank_done, 1)
            pe.wait_ge(hot_ready, 1)
            for q in range(TK):
                n = rows(q // 2)
                ins = mm(ps[:, 6, 0:2 * MAXB], ohslot[0:n, q, :], rhs2[0:n, q, :, :].rearrange("p a b -> p (a b)"), q == 0, q == TK - 1)
            ins.then_inc(slot_done, 1)

            pe.wait_ge(pairs_ready, 1)
            more = pe.value_load(cnt_i[0:1, 0:1], min_val=NE // 2 - 1, max_val=MAXB // 2 - 1)
            for credit in (gate_done, up_done, y_done):
                pe.sem_inc(credit, 2)

            def turn_x(n, s, times):
                pe.wait_ge(xg_ready[s], 16 * times)
                ge(pe, xT_a, n)
                ge(pe, xT_b, n)
                for k in range(KC):
                    ins = pe.transpose(ps[:, k // 4, (k % 4) * P:(k % 4 + 1) * P],
                                       xg[:, s, :].rearrange("r (p k) -> r k p", k=KC)[:, k, :], ident[:, :])
                ins.then_inc(xg_used, 1)

            def products(bank, w, n, s, ready, done, i):
                pe.wait_ge(ready[s], 16 * i + 16)
                for m in range(FC):
                    ins = chunk_sum(ps[:, bank, m * P:(m + 1) * P], lambda k: w[s][:, k, m * P:(m + 1) * P], lambda k: xT[s][:, k, :])
                ins.then_inc(done, 1)

            def pe_block(i, s, last=False):
                n = 2 * i + s
                if not last:
                    turn_x(n + 1, 1 - s, i + 1 + s)
                products(3, wu, n, s, ld_u, up_done, i)
                if not last:
                    pe.wait_ge(xT_a, n + 2)
                    pe.wait_ge(xT_b, n + 2)
                    pe.wait_ge(ch_moe, n + 1)
                    products(2, wg, n + 1, 1 - s, ld_g, gate_done, i + s)
                pe.wait_ge(a_ready, n + 1)
                pe.wait_ge(wd_split, n + 1)
                for nn, (kept, done) in enumerate(((yk_a, y_half), (yk_b, y_done))):
                    pe.wait_ge(kept, n + 1)
                    cols = slice(nn * 512, (nn + 1) * 512)
                    terms = [(a, w, m) for m in range(FC) for a, w in ((a_up, wd_up), (a_up, wd_low[s]), (a_low, wd_up))]
                    for q, (a, w, m) in enumerate(terms):
                        ins = mm(ps[:, 4 + nn, :], a[:, m, :], w[:, m, cols], q == 0, q == len(terms) - 1)
                    ins.then_inc(done, 1)

            turn_x(0, 0, 1)
            pe.wait_ge(xT_a, 1)
            pe.wait_ge(xT_b, 1)
            products(2, wg, 0, 0, ld_g, gate_done, 0)
            with pe.Fori(0, more) as i:
                for s in range(2):
                    pe_block(i, s)
            pe_block(more, 0)
            pe_block(more, 1, True)


HEADS = [8 * (c // 4) + 4 * a + c % 4 for c in range(KC) for a in range(2)]


def layouts(g):
    x = np.concatenate([g["x_prompt"][0], g["x_sample"].reshape(NS, D)])
    chunks = lambda w: np.ascontiguousarray(w.reshape(KC, P, w.shape[1] // P, P).transpose(2, 1, 0, 3))
    by_part = lambda v: v.reshape(KC, P, *v.shape[1:]).swapaxes(0, 1)
    w_in = g["w_in"][0]
    q, k, v, xl, yl, ga, gr = np.split(w_in, np.cumsum([D, KV, KV, D, D, D]), axis=1)
    q = q.reshape(D, 16, HD)[:, HEADS].reshape(D, D)
    w_at = g["w_attn_branch"][0].reshape(16, HD, D)[HEADS].reshape(D, D)
    lg = np.zeros((KC, P, 2, P), np.float32)
    for m, name in enumerate(("w_lru_a", "w_lru_x")):
        w = g[name][0].reshape(KC, 2, HD, HD)
        for a in range(2):
            lg[:, a * HD:(a + 1) * HD, m, a * HD:(a + 1) * HD] = w[:, a]
    vec = [g["b_lru_a"][0], g["b_lru_x"][0], g["lru_lambda"][0], g["b_conv"][0], *g["w_conv"][0]]
    sinks = g["sinks"][0]
    sink_s = np.repeat(np.broadcast_to(sinks.reshape(4, 1, 4), (4, 2, 4)).reshape(-1), NT)
    kc = g["cache_k_win"][0].reshape(NB, P, 2, P)
    return {name: np.ascontiguousarray(t) for name, t in {
        "x": x, "xT": x.T,
        "cT": by_part(np.concatenate([g["c_prompt"], g["c_sample"]]).T),
        "w_ada": g["w_ada"][0], "b_ada": g["b_ada"][0],
        "w_qk": np.concatenate([chunks(k), chunks(q)]), "w_v": v.reshape(KC, P, KV).swapaxes(0, 1),
        "w_xl": chunks(xl), "w_yl": chunks(yl), "w_ga": chunks(ga), "w_gr": chunks(gr),
        "w_at": chunks(w_at), "w_lr": chunks(g["w_lru_branch"][0]), "w_lg": lg, "w_out": g["w_out"][0],
        "lvec": by_part(np.stack(vec, axis=1)),
        "h0": by_part(g["state_h"][0].T), "stc": by_part(g["state_conv"][0].transpose(2, 0, 1)),
        "gpre": by_part(g["g_pre_mix"][0]), "sinks": sinks[HEADS], "sink_s": sink_s[:, None],
        "g_rows": np.concatenate([g["g_post_mix"], g["g_pre_ffn"], g["g_post_ffn"]]),
        "w_r": by_part(np.concatenate([g["w_router_group"][0], g["w_router_expert"][0]], axis=1)),
        "b_r": np.concatenate([g["b_router_group"][0], g["b_router_expert"][0]]),
        "kcT": kc.transpose(3, 2, 0, 1), "v_cache": g["cache_v_win"][0].reshape(NB, P, KV),
        "w_gate": g["w_exp_gate"][0], "w_up": g["w_exp_up"][0], "w_down": g["w_exp_down"][0],
    }.items()}


def constants():
    bf16 = mybir.dt.np(BF16)
    half = HD // 2
    inv = (10000.0 ** (-np.arange(half) / half)).astype(np.float32)
    pos = np.concatenate([np.arange(SEQ), np.tile(PAST + np.arange(NT), NB)]).astype(np.float32)
    ang = (pos[None, :] * inv[:, None]).astype(np.float32)
    m = np.arange(P)
    sign = np.where(m % HD < half, -1.0, 1.0).astype(np.float32)[:, None]
    q, k = m[:, None], m[None, :]
    out = np.float32(-1e30)
    masks = np.zeros((P, BLKS, 2 * P), np.float32)
    masks[:, :, :P] = np.where(k >= q, 0, out)[:, None, :]
    masks[:, :, P:] = np.where(k <= q, 0, out)[:, None, :]
    masks[:, 0, :P] = out
    t, j = (m % NT)[:, None], np.arange(P + NT)[None, :]
    sel = np.zeros((1 + NB, P + NS), np.float32)
    sel[0, :P] = 1.0
    for b in range(NB):
        sel[1 + b, P + NT * b:P + NT * (b + 1)] = 1.0
    upper = np.ones((P, 2, P), np.float32)
    upper[:, 0] = q < k
    tpid = np.zeros((P, 2, TILES * 2), np.float32)
    tpid[:, 0] = np.arange(TILES * 2) // 2
    tpid[:, 1] = q
    return {
        "ident": np.eye(P, dtype=np.float32), "identb": np.eye(P).astype(bf16), 
        "masks": masks.astype(bf16), "mask_s": np.where((j >= t) & (j <= P + t), 0, out).astype(bf16),
        "sel": sel, "cos": np.tile(np.cos(ang), (4, 1)), "sin": np.tile(np.sin(ang), (4, 1)) * sign,
        "halves": np.repeat(np.eye(2, dtype=np.float32), HD, axis=0),
        "iota": np.tile(m.astype(np.float32), (P, 1)), "upper": upper.astype(bf16), "tpid": tpid.astype(bf16),
    }


def outputs(r):
    tail = r["tail"].swapaxes(0, 1).reshape(D, 36)
    kws = r["kws"].transpose(2, 3, 1, 0).reshape(1, NB, P, 4, HD)
    vws = np.concatenate([r["vold"], r["vnew"].reshape(NB, NT, KV)], axis=1).reshape(1, NB, P, 4, HD)
    return (r["y"][:SEQ].reshape(1, SEQ, D), r["y"][SEQ:].reshape(NB, NT, D),
            r["kwp"].transpose(2, 1, 0).reshape(1, 1, P, 4, HD), r["vwp"].reshape(1, 1, P, 4, HD),
            tail[:, 0:3].T.reshape(1, 1, 3, D), tail[:, 3].reshape(1, 1, D),
            kws, vws, tail[:, 12:36].reshape(D, NB, 3).transpose(1, 2, 0)[None], tail[:, 4:12].T[None])


def kernel(x_prompt, x_sample, cache_k_win, cache_v_win, state_conv, state_h, c_prompt, c_sample,
           w_ada, b_ada, g_pre_mix, g_post_mix, g_pre_ffn, g_post_ffn, w_in, sinks,
           w_conv, b_conv, w_lru_a, b_lru_a, w_lru_x, b_lru_x, lru_lambda,
           w_attn_branch, w_lru_branch, w_out, w_router_group, b_router_group,
           w_router_expert, b_router_expert, w_exp_gate, w_exp_up, w_exp_down):
    from concourse import bacc as _bacc
    from concourse.bass_utils import run_bass_kernel_spmd

    given = dict(locals())
    g = {name: np.asarray(v) for name, v in given.items() if hasattr(v, "shape")}
    arrays = layouts(g) | constants()
    shapes = {"y": (TOK, D), "kwp": (P, 2, P), "vwp": (P, KV), "vnew": (NS, KV), "vold": (NB, P - NT, KV),
              "tail": (P, KC, 36), "kws": (P, 2, NB, P)}
    nc = _bacc.Bacc("TRN2", target_bir_lowering=False, num_devices=1)
    I = {n: nc.dram_tensor(n, list(v.shape), mybir.dt.from_np(v.dtype), kind="ExternalInput").ap() for n, v in arrays.items()}
    O = {n: nc.dram_tensor(n, list(s), F32, kind="ExternalOutput").ap() for n, s in shapes.items()}
    build(nc, I, O)
    nc.finalize()
    r = run_bass_kernel_spmd(nc, [arrays], core_ids=[0]).results[0]
    return outputs({n: np.asarray(r[n]).reshape(s) for n, s in shapes.items()})
```
